# Optimizing a Trainium2 kernel written in Bass

```python
import jax, jax.numpy as jnp
from jax import lax
import numpy as np
import math

D_MODEL = 1024
BATCH = 1
SEQ = 256
DEPTH = 1

RET_HEADS = 8
RET_DK = 64
RET_DV = 128
DN_HEADS = 8
DN_DK = 128
DN_DV = 128
CHUNK = 128
SHORT_CONV = 4
FFN_CONV = 3
D_FF = 2816
ROPE_BASE = 10000.0
EPS = 1e-6
GN_EPS = 1e-5

RET_QK = RET_HEADS * RET_DK
RET_V = RET_HEADS * RET_DV
DN_QK = DN_HEADS * DN_DK
DN_V = DN_HEADS * DN_DV
SPLITS = (RET_QK, RET_QK, RET_V, RET_V, DN_QK, DN_QK, DN_V, DN_V, DN_HEADS, DN_HEADS, D_MODEL, D_MODEL)
D_IN = sum(SPLITS)
DN_CONV_CH = 2 * DN_QK + DN_V


def rmsnorm(x, g):
    xf = x.astype(jnp.float32)
    r = lax.rsqrt(jnp.mean(xf * xf, axis=-1, keepdims=True) + EPS)
    return (xf * r) * g

def l2norm(x):
    xf = x.astype(jnp.float32)
    return xf * lax.rsqrt(jnp.sum(xf * xf, axis=-1, keepdims=True) + EPS)

def rotary(x):
    T, d = x.shape[1], x.shape[-1]
    inv = ROPE_BASE ** (-jnp.arange(0, d, 2, dtype=jnp.float32) / d)
    ang = jnp.arange(T, dtype=jnp.float32)[:, None] * inv[None, :]
    cos = jnp.cos(ang)[None, :, None, :]
    sin = jnp.sin(ang)[None, :, None, :]
    x1, x2 = x[..., : d // 2], x[..., d // 2:]
    return jnp.concatenate([x1 * cos - x2 * sin, x1 * sin + x2 * cos], axis=-1)

def causal_dwconv(x, w):
    K, T = w.shape[0], x.shape[1]
    xp = jnp.pad(x, ((0, 0), (K - 1, 0), (0, 0)))
    y = xp[:, K - 1:K - 1 + T] * w[K - 1]
    for k in range(K - 1):
        y = y + xp[:, k:k + T] * w[k]
    return y

def retention_chunkwise(q, k, v):
    B, T, H, dk = q.shape
    dv = v.shape[-1]
    N = T // CHUNK
    f32 = jnp.float32
    gamma = 1.0 - 2.0 ** (-5.0 - jnp.arange(H, dtype=f32))
    log_g = jnp.log(gamma)
    idx = jnp.arange(CHUNK, dtype=f32)
    qc = q.astype(f32).reshape(B, N, CHUNK, H, dk)
    kc = k.astype(f32).reshape(B, N, CHUNK, H, dk)
    vc = v.astype(f32).reshape(B, N, CHUNK, H, dv)
    diff = idx[:, None] - idx[None, :]
    causal = diff >= 0
    dmat = jnp.where(causal[None], jnp.exp(log_g[:, None, None] * jnp.where(causal, diff, 0.0)[None]), 0.0)
    scores = jnp.einsum('bnihd,bnjhd->bnhij', qc, kc) * dmat
    inner = jnp.einsum('bnhij,bnjhv->bnihv', scores, vc)
    zeta = jnp.exp(log_g[:, None] * (CHUNK - 1.0 - idx)[None, :])
    kv = jnp.einsum('bnjhd,hj,bnjhv->bnhdv', kc, zeta, vc)
    chunk_decay = jnp.exp(log_g * CHUNK)[:, None, None]

    def step(S, kv_n):
        return S * chunk_decay + kv_n, S

    _, s_prev = lax.scan(step, jnp.zeros((B, H, dk, dv), f32), jnp.moveaxis(kv, 1, 0))
    xi = jnp.exp(log_g[:, None] * (idx + 1.0)[None, :])
    cross = jnp.einsum('bnihd,nbhdv,hi->bnihv', qc, s_prev, xi)
    return (inner + cross).reshape(B, T, H, dv)

def gated_delta_chunkwise(q, k, v, g, beta):
    B, T, H, dk = q.shape
    dv = v.shape[-1]
    N = T // CHUNK
    f32 = jnp.float32

    def to_chunks(t):
        return jnp.moveaxis(t.astype(f32).reshape((B, N, CHUNK, H) + t.shape[3:]), 3, 1)

    qc = to_chunks(q) * (dk ** -0.5)
    kc = to_chunks(k)
    vc = to_chunks(v)
    gc = to_chunks(g)
    bc = to_chunks(beta)
    G = jnp.cumsum(gc, axis=-1)
    idx = jnp.arange(CHUNK)
    causal = idx[:, None] >= idx[None, :]
    strict = idx[:, None] > idx[None, :]
    diff = G[..., :, None] - G[..., None, :]
    L = jnp.where(causal, jnp.exp(jnp.where(causal, diff, 0.0)), 0.0)
    k_beta = kc * bc[..., None]
    A = jnp.where(strict, jnp.einsum('bhnid,bhnjd->bhnij', k_beta, kc) * L, 0.0)
    eye = jnp.eye(CHUNK, dtype=f32)
    rhs = jnp.concatenate([vc * bc[..., None], k_beta * jnp.exp(G)[..., None]], axis=-1)
    sol = lax.linalg.triangular_solve(eye + A, rhs, left_side=True, lower=True, unit_diagonal=True)
    u, w = sol[..., :dv], sol[..., dv:]
    attn = jnp.where(causal, jnp.einsum('bhnid,bhnjd->bhnij', qc, kc) * L, 0.0)
    q_dec = qc * jnp.exp(G)[..., None]
    k_dec = kc * jnp.exp(G[..., -1:] - G)[..., None]
    chunk_dec = jnp.exp(G[..., -1])

    def step(S, inp):
        u_n, w_n, q_n, k_n, a_n, d_n = inp
        v_new = u_n - jnp.einsum('bhcd,bhdv->bhcv', w_n, S)
        o = jnp.einsum('bhcd,bhdv->bhcv', q_n, S) + jnp.einsum('bhij,bhjv->bhiv', a_n, v_new)
        S = S * d_n[..., None, None] + jnp.einsum('bhcd,bhcv->bhdv', k_n, v_new)
        return S, o

    xs = tuple(jnp.moveaxis(t, 2, 0) for t in (u, w, q_dec, k_dec, attn, chunk_dec))
    _, o = lax.scan(step, jnp.zeros((B, H, dk, dv), f32), xs)
    return o.transpose(1, 0, 3, 2, 4).reshape(B, T, H, dv)

def first_inputs(seed: int = 0) -> dict:
    key = jax.random.key(seed)
    ks = jax.random.split(key, 20)
    f32 = jnp.float32
    nrm = lambda k, shape, s: jax.random.normal(k, shape, f32) * s
    dt = jnp.exp(jax.random.uniform(ks[6], (DEPTH, DN_HEADS), f32, np.log(1e-3), np.log(1e-1)))
    return {
        "x": jax.random.normal(ks[0], (BATCH, SEQ, D_MODEL), f32),
        "g_mix": 1.0 + nrm(ks[1], (DEPTH, D_MODEL), 0.05),
        "w_in": nrm(ks[2], (DEPTH, D_MODEL, D_IN), D_MODEL ** -0.5),
        "ret_norm_g": 1.0 + nrm(ks[3], (DEPTH, RET_V), 0.05),
        "dn_conv_w": nrm(ks[4], (DEPTH, SHORT_CONV, DN_CONV_CH), SHORT_CONV ** -0.5),
        "dn_a_log": jnp.log(jax.random.uniform(ks[5], (DEPTH, DN_HEADS), f32, 1.0, 16.0)),
        "dn_dt_bias": dt + jnp.log(-jnp.expm1(-dt)),
        "dn_norm_g": 1.0 + nrm(ks[7], (DEPTH, DN_DV), 0.05),
        "w_ret_br": nrm(ks[8], (DEPTH, RET_V, D_MODEL), RET_V ** -0.5),
        "w_dn_br": nrm(ks[9], (DEPTH, DN_V, D_MODEL), DN_V ** -0.5),
        "w_o": nrm(ks[10], (DEPTH, D_MODEL, D_MODEL), D_MODEL ** -0.5),
        "g_ffn": 1.0 + nrm(ks[11], (DEPTH, D_MODEL), 0.05),
        "w_up": nrm(ks[12], (DEPTH, D_MODEL, 2 * D_FF), D_MODEL ** -0.5),
        "ffn_conv_w": nrm(ks[13], (DEPTH, FFN_CONV, 2 * D_FF), FFN_CONV ** -0.5),
        "ffn_conv_b": nrm(ks[14], (DEPTH, 2 * D_FF), 0.01),
        "w_down": nrm(ks[15], (DEPTH, D_FF, D_MODEL), D_FF ** -0.5),
        "g_final": 1.0 + nrm(ks[16], (D_MODEL,), 0.05),
    }

def first_block(x, g_mix, w_in, ret_norm_g, dn_conv_w, dn_a_log, dn_dt_bias, dn_norm_g,
              w_ret_br, w_dn_br, w_o, g_ffn, w_up, ffn_conv_w, ffn_conv_b, w_down, g_final):
    B, T, _ = x.shape
    h = x.astype(jnp.float32)
    split_at = np.cumsum(SPLITS)[:-1].tolist()
    for l in range(DEPTH):
        u = rmsnorm(h, g_mix[l])
        proj = u @ w_in[l]
        (rq, rk, rv, rgate, dq, dk_, dv_, dz, db, da, gate_r, gate_d) = jnp.split(proj, split_at, axis=-1)

        rq = rotary(rq.reshape(B, T, RET_HEADS, RET_DK))
        rk = rotary(rk.reshape(B, T, RET_HEADS, RET_DK)) * (RET_DK ** -0.5)
        ro = retention_chunkwise(rq, rk, rv.reshape(B, T, RET_HEADS, RET_DV))
        mu = jnp.mean(ro, axis=-1, keepdims=True)
        var = jnp.mean(jnp.square(ro - mu), axis=-1, keepdims=True)
        ro = ((ro - mu) * lax.rsqrt(var + GN_EPS)).reshape(B, T, RET_V) * ret_norm_g[l]
        y_ret = (jax.nn.silu(rgate) * ro) @ w_ret_br[l]

        qkv = jax.nn.silu(causal_dwconv(jnp.concatenate([dq, dk_, dv_], axis=-1), dn_conv_w[l]))
        cq, ck, cv = jnp.split(qkv, [DN_QK, 2 * DN_QK], axis=-1)
        cq = l2norm(cq.reshape(B, T, DN_HEADS, DN_DK))
        ck = l2norm(ck.reshape(B, T, DN_HEADS, DN_DK))
        cv = cv.reshape(B, T, DN_HEADS, DN_DV)
        g = -jnp.exp(dn_a_log[l]) * jax.nn.softplus(da.astype(jnp.float32) + dn_dt_bias[l])
        beta = jax.nn.sigmoid(db.astype(jnp.float32))
        do = gated_delta_chunkwise(cq, ck, cv, g, beta)
        do = do * lax.rsqrt(jnp.mean(do * do, axis=-1, keepdims=True) + EPS) * dn_norm_g[l]
        do = do.reshape(B, T, DN_V) * jax.nn.silu(dz)
        y_dn = do @ w_dn_br[l]

        merged = jax.nn.sigmoid(gate_r) * y_ret + jax.nn.sigmoid(gate_d) * y_dn
        h = h + merged @ w_o[l]

        u2 = rmsnorm(h, g_ffn[l])
        up = causal_dwconv(u2 @ w_up[l], ffn_conv_w[l]) + ffn_conv_b[l]
        a, b = jnp.split(up, 2, axis=-1)
        h = h + (jax.nn.silu(a) * b) @ w_down[l]
    return rmsnorm(h, g_final).astype(x.dtype)


DEPTH_2 = 2

N_META = 16
N_MIXERS = 2
EXPAND = 2
D_INNER = EXPAND * D_MODEL
RMS_EPS = 1e-6
N_RWKV_LAYERS = (DEPTH_2 + 1) // 2
N_MLA_LAYERS = DEPTH_2 // 2

RWKV_HEAD = 64
RWKV_HEADS = D_INNER // RWKV_HEAD
DECAY_LORA = 64
AAA_LORA = 64
RWKV_WIDTHS = (D_INNER, D_INNER, D_INNER, D_INNER, DECAY_LORA, AAA_LORA)
N_LERP = len(RWKV_WIDTHS)
RWKV_IN = sum(RWKV_WIDTHS)
GN_EPS_2 = 64e-5

MLA_HEADS = 16
QK_NOPE = 128
QK_ROPE = 64
V_HEAD = 128
Q_LORA = 512
KV_LORA = 256
MLA_IN = Q_LORA + KV_LORA + QK_ROPE + D_INNER
ROPE_THETA = 10000.0
Q_BLOCK = 128


def _rms_norm(x, g):
    xf = x.astype(jnp.float32)
    y = xf * lax.rsqrt(jnp.mean(xf * xf, axis=-1, keepdims=True) + RMS_EPS)
    return (y * g.astype(jnp.float32)).astype(x.dtype)

def _rope(x, pos):
    half = x.shape[-1] // 2
    inv_freq = jnp.exp(-math.log(ROPE_THETA) * jnp.arange(half, dtype=jnp.float32) / half)
    ang = pos[:, None] * inv_freq[None, :]
    ang = ang.reshape((1, ang.shape[0]) + (1,) * (x.ndim - 3) + (half,))
    cos, sin = jnp.cos(ang), jnp.sin(ang)
    xf = x.astype(jnp.float32)
    x1, x2 = xf[..., :half], xf[..., half:]
    return jnp.concatenate([x1 * cos - x2 * sin, x2 * cos + x1 * sin], axis=-1).astype(x.dtype)

def _wkv7_scan(r, decay, k, v, a_vec, b_vec):
    B, L, H, N = r.shape
    xs = tuple(jnp.moveaxis(t.astype(jnp.float32), 1, 0) for t in (r, decay, k, v, a_vec, b_vec))

    def step(S, inp):
        r_t, w_t, k_t, v_t, a_t, b_t = inp
        sa = jnp.einsum('bhij,bhj->bhi', S, a_t)
        S = S * w_t[:, :, None, :] + sa[..., None] * b_t[:, :, None, :] + v_t[..., None] * k_t[:, :, None, :]
        return S, jnp.einsum('bhij,bhj->bhi', S, r_t)

    S0 = jnp.zeros((B, H, N, N), jnp.float32)
    _, ys = lax.scan(step, S0, xs)
    return jnp.moveaxis(ys, 0, 1)

def _rwkv7_mixer(x, mu, w_in, w0, w2, a0, a2, k_k, k_a, r_k, ln_w, ln_b, w_out):
    B, L, _ = x.shape
    H, N = RWKV_HEADS, RWKV_HEAD
    x_prev = jnp.pad(x, ((0, 0), (1, 0), (0, 0)))[:, :-1]
    dx = x_prev - x
    widths = np.array(RWKV_WIDTHS)
    mu_cols = jnp.repeat(mu.T, widths, axis=1, total_repeat_length=RWKV_IN)
    w_comb = jnp.concatenate([w_in, mu_cols * w_in], axis=0)
    h = jnp.concatenate([x, dx], axis=-1) @ w_comb
    r, k, v, g, w_lo, a_lo = jnp.split(h, list(np.cumsum(widths)[:-1]), axis=-1)
    w = -jax.nn.softplus(-(w0 + jnp.tanh(w_lo) @ w2)) - 0.5
    a = jax.nn.sigmoid(a0 + a_lo @ a2)
    heads = lambda t: t.reshape(B, L, H, N)
    r, k, v, w, a = heads(r), heads(k), heads(v), heads(w), heads(a)
    k_k, k_a, r_k = k_k.reshape(H, N), k_a.reshape(H, N), r_k.reshape(H, N)
    kk = (k * k_k).astype(jnp.float32)
    kk = kk / jnp.maximum(jnp.linalg.norm(kk, axis=-1, keepdims=True), 1e-12)
    k = k * (1 + (a - 1) * k_a)
    decay = jnp.exp(-jnp.exp(w.astype(jnp.float32)))
    y = _wkv7_scan(r, decay, k, v, -kk, kk * a.astype(jnp.float32))
    mean = jnp.mean(y, axis=-1, keepdims=True)
    var = jnp.mean(jnp.square(y - mean), axis=-1, keepdims=True)
    y = ((y - mean) * lax.rsqrt(var + GN_EPS_2)).reshape(B, L, D_INNER)
    y = y * ln_w.astype(jnp.float32) + ln_b.astype(jnp.float32)
    bonus = (jnp.sum(r * k * r_k, axis=-1, keepdims=True) * v).reshape(B, L, D_INNER)
    y = (y + bonus.astype(jnp.float32)).astype(x.dtype) * jax.nn.silu(g)
    return y @ w_out

def _causal_block_attention(q_nope, q_rope, k_nope, k_rope, v):
    L = q_nope.shape[1]
    scale = (QK_NOPE + QK_ROPE) ** -0.5
    neg = jnp.finfo(jnp.float32).min
    bounds = [(0, N_META)] + [(s, min(s + Q_BLOCK, L)) for s in range(N_META, L, Q_BLOCK)]
    outs = []
    for s, e in bounds:
        sc = (jnp.einsum('bqhd,bkhd->bhqk', q_nope[:, s:e], k_nope[:, :e])
              + jnp.einsum('bqhr,bkr->bhqk', q_rope[:, s:e], k_rope[:, :e])).astype(jnp.float32) * scale
        mask = jnp.arange(s, e)[:, None] >= jnp.arange(e)[None, :]
        p = jax.nn.softmax(jnp.where(mask, sc, neg), axis=-1).astype(v.dtype)
        outs.append(jnp.einsum('bhqk,bkhd->bqhd', p, v[:, :e]))
    return jnp.concatenate(outs, axis=1)

def _mla_mixer(x, pos, w_in, q_norm, w_q_up, kv_norm, w_kv_up, w_out):
    B, L, _ = x.shape
    H = MLA_HEADS
    h = x @ w_in
    c_q, c_kv, k_rope, g = jnp.split(h, [Q_LORA, Q_LORA + KV_LORA, Q_LORA + KV_LORA + QK_ROPE], axis=-1)
    q = (_rms_norm(c_q, q_norm) @ w_q_up).reshape(B, L, H, QK_NOPE + QK_ROPE)
    q_nope, q_rope = q[..., :QK_NOPE], _rope(q[..., QK_NOPE:], pos)
    kv = (_rms_norm(c_kv, kv_norm) @ w_kv_up).reshape(B, L, H, QK_NOPE + V_HEAD)
    k_nope, v = kv[..., :QK_NOPE], kv[..., QK_NOPE:]
    k_rope = _rope(k_rope, pos)
    o = _causal_block_attention(q_nope, q_rope, k_nope, k_rope, v).reshape(B, L, D_INNER)
    return (o * jax.nn.silu(g)) @ w_out

def second_inputs(seed: int = 0) -> dict:
    key = jax.random.key(seed)
    ks = jax.random.split(key, 24)
    f32 = jnp.float32
    nrm = lambda k, shape, s: jax.random.normal(k, shape, f32) * s
    NR, NM = N_RWKV_LAYERS, N_MLA_LAYERS
    return {
        "x": nrm(ks[0], (BATCH, SEQ, D_MODEL), 1.0),
        "meta_tokens": nrm(ks[1], (N_META, D_MODEL), 1.0),
        "norm_pre": 1.0 + nrm(ks[2], (DEPTH_2, D_MODEL), 0.02),
        "norm_post": 1.0 + nrm(ks[3], (DEPTH_2, D_MODEL), 0.02),
        "rwkv_mu": jax.random.uniform(ks[4], (NR, N_LERP, D_MODEL), f32),
        "rwkv_w_in": nrm(ks[5], (NR, D_MODEL, RWKV_IN), D_MODEL ** -0.5),
        "rwkv_w0": -2.0 + nrm(ks[6], (NR, D_INNER), 0.5),
        "rwkv_w2": nrm(ks[7], (NR, DECAY_LORA, D_INNER), 0.5 * DECAY_LORA ** -0.5),
        "rwkv_a0": nrm(ks[8], (NR, D_INNER), 0.1),
        "rwkv_a2": nrm(ks[9], (NR, AAA_LORA, D_INNER), 0.5 * AAA_LORA ** -0.5),
        "rwkv_k_k": 0.85 + nrm(ks[10], (NR, D_INNER), 0.05),
        "rwkv_k_a": 1.0 + nrm(ks[11], (NR, D_INNER), 0.05),
        "rwkv_r_k": nrm(ks[12], (NR, D_INNER), 0.1),
        "rwkv_ln_w": 1.0 + nrm(ks[13], (NR, D_INNER), 0.02),
        "rwkv_ln_b": nrm(ks[14], (NR, D_INNER), 0.02),
        "rwkv_w_out": nrm(ks[15], (NR, D_INNER, D_MODEL), D_INNER ** -0.5),
        "mla_w_in": nrm(ks[16], (NM, D_MODEL, MLA_IN), D_MODEL ** -0.5),
        "mla_q_norm": 1.0 + nrm(ks[17], (NM, Q_LORA), 0.02),
        "mla_w_q_up": nrm(ks[18], (NM, Q_LORA, MLA_HEADS * (QK_NOPE + QK_ROPE)), Q_LORA ** -0.5),
        "mla_kv_norm": 1.0 + nrm(ks[19], (NM, KV_LORA), 0.02),
        "mla_w_kv_up": nrm(ks[20], (NM, KV_LORA, MLA_HEADS * (QK_NOPE + V_HEAD)), KV_LORA ** -0.5),
        "mla_w_out": nrm(ks[21], (NM, D_INNER, D_MODEL), D_INNER ** -0.5),
    }

def second_block(x, meta_tokens, norm_pre, norm_post,
              rwkv_mu, rwkv_w_in, rwkv_w0, rwkv_w2, rwkv_a0, rwkv_a2,
              rwkv_k_k, rwkv_k_a, rwkv_r_k, rwkv_ln_w, rwkv_ln_b, rwkv_w_out,
              mla_w_in, mla_q_norm, mla_w_q_up, mla_kv_norm, mla_w_kv_up, mla_w_out):
    B = x.shape[0]
    meta = jnp.broadcast_to(meta_tokens.astype(x.dtype)[None], (B, N_META, D_MODEL))
    h = jnp.concatenate([meta, x], axis=1)
    pos = jnp.arange(h.shape[1], dtype=jnp.float32)
    for i in range(DEPTH_2):
        j = i // N_MIXERS
        u = _rms_norm(h, norm_pre[i])
        if i % N_MIXERS == 0:
            m = _rwkv7_mixer(u, rwkv_mu[j], rwkv_w_in[j], rwkv_w0[j], rwkv_w2[j], rwkv_a0[j], rwkv_a2[j],
                             rwkv_k_k[j], rwkv_k_a[j], rwkv_r_k[j], rwkv_ln_w[j], rwkv_ln_b[j], rwkv_w_out[j])
        else:
            m = _mla_mixer(u, pos, mla_w_in[j], mla_q_norm[j], mla_w_q_up[j], mla_kv_norm[j],
                           mla_w_kv_up[j], mla_w_out[j])
        h = h + _rms_norm(m, norm_post[i])
    return h[:, N_META:]


def setup_inputs(seed=0):
    out = dict(first_inputs(seed))
    for name, value in second_inputs(seed + 1).items():
        if name != "x":
            out[name + "_2"] = value
    return out


def reference(
    x, g_mix, w_in, ret_norm_g, dn_conv_w, dn_a_log, dn_dt_bias, dn_norm_g, w_ret_br, w_dn_br,
    w_o, g_ffn, w_up, ffn_conv_w, ffn_conv_b, w_down, g_final, meta_tokens_2, norm_pre_2,
    norm_post_2, rwkv_mu_2, rwkv_w_in_2, rwkv_w0_2, rwkv_w2_2, rwkv_a0_2, rwkv_a2_2, rwkv_k_k_2,
    rwkv_k_a_2, rwkv_r_k_2, rwkv_ln_w_2, rwkv_ln_b_2, rwkv_w_out_2, mla_w_in_2, mla_q_norm_2,
    mla_w_q_up_2, mla_kv_norm_2, mla_w_kv_up_2, mla_w_out_2,
):
    x = first_block(
        x, g_mix, w_in, ret_norm_g, dn_conv_w, dn_a_log, dn_dt_bias, dn_norm_g, w_ret_br,
        w_dn_br, w_o, g_ffn, w_up, ffn_conv_w, ffn_conv_b, w_down, g_final,
    )
    return second_block(
        x, meta_tokens_2, norm_pre_2, norm_post_2, rwkv_mu_2, rwkv_w_in_2, rwkv_w0_2, rwkv_w2_2,
        rwkv_a0_2, rwkv_a2_2, rwkv_k_k_2, rwkv_k_a_2, rwkv_r_k_2, rwkv_ln_w_2, rwkv_ln_b_2,
        rwkv_w_out_2, mla_w_in_2, mla_q_norm_2, mla_w_q_up_2, mla_kv_norm_2, mla_w_kv_up_2,
        mla_w_out_2,
    )


_drawn_inputs = setup_inputs


def setup_inputs(seed=0):
    import zlib

    import numpy as np

    out = dict(_drawn_inputs(seed))
    spreads = {}
    factors = {'ffn_conv_b': 3.617,
     'rwkv_k_k_2': 3.21,
     'rwkv_ln_w_2': 2.977,
     'mla_q_norm_2': 5.043,
     'mla_kv_norm_2': 3.786,
     'rwkv_ln_b_2': 3.705}
    for name, (base, spread) in spreads.items():
        noise = np.random.default_rng([zlib.crc32(name.encode()), seed]).standard_normal(out[name].shape)
        drawn = base * np.exp(spread * noise) if base else spread * noise
        out[name] = __import__('jax').numpy.asarray(drawn.astype(out[name].dtype))
    for name, factor in factors.items():
        out[name] = (out[name] * factor).astype(out[name].dtype)
    return out
```

```python
from contextlib import ExitStack

import numpy as np

import concourse.bass as bass
from concourse import mybir

F32 = mybir.dt.float32
ALU = mybir.AluOpType
ACT = mybir.ActivationFunctionType
AX_X = mybir.AxisListType.X

P = 128
D = 1024
DT = D // P
T1 = 256
META = 16
T2 = T1 + META
H1 = 8
CH = 128
DFF = 2816
FT = DFF // P
RH = 32
RN = 64
PAIRS = RH // 2
RC = 68
NRC = T2 // RC
INNER = 2048
IT = INNER // P
AH = 16
LEVELS = 7
EPS = 1e-6
GN_EPS = 1e-5
GN_EPS_2 = 64e-5
DECAY_C = float(np.exp(-0.5))
SCALE_A = float(192 ** -0.5)

CB = 16
SLOTS = 8

SPLITS = (512, 512, 1024, 1024, 1024, 1024, 1024, 1024, 8, 8, 1024, 1024)
OFF = [int(v) for v in np.cumsum((0,) + SPLITS)]
O_RQ, O_RK, O_RV, O_RG, O_DQ, O_DK, O_DV, O_DZ, O_DB, O_DA, O_GR, O_GD = OFF[:12]
RW_G, RW_WLO = 3 * INNER, 4 * INNER
MLA_CKV, MLA_ROPE, MLA_G = 512, 768, 832


def weight_order():
    def tile(w, k, m, off=0):
        return (w, k * P, [(off + m * P, P)])

    def outs(w, off, ms, kt):
        return [tile(w, k, m, off) for m in ms for k in range(kt)]

    def wide(w, k, off):
        return [(w, k * P, [(off + j * P, P)]) for j in range(4)]

    order = []
    for off, n in ((O_RQ, 4), (O_RK, 4)):
        order += outs("w_in", off, range(n), DT)
    for g in range(2):
        for k in range(DT):
            order += wide("w_in", k, O_RV + 512 * g)
    for off in (O_DK, O_DQ, O_DV, O_RG, O_DZ, O_GR, O_GD):
        order += outs("w_in", off, range(8), DT)
    order += outs("w_ret_br", 0, range(8), DT)
    order += outs("w_dn_br", 0, range(8), DT)
    order += outs("w_o", 0, range(8), DT)
    for m in range(FT):
        order += outs("w_up", 0, [m], DT) + outs("w_up", DFF, [m], DT)
    order += outs("w_down", 0, range(8), FT)
    order += [("rwkv_w_in_2", k * P, [(RW_WLO, P)]) for k in range(DT)]
    for p in range(PAIRS):
        for off in (INNER, 0, 2 * INNER, RW_G):
            order += outs("rwkv_w_in_2", off, [p], DT)
    order += outs("rwkv_w_out_2", 0, range(8), IT)
    order += outs("mla_w_in_2", 0, range(4), DT) + outs("mla_w_in_2", MLA_CKV, range(2), DT)
    order += [("mla_w_in_2", k * P, [(MLA_ROPE, 64), (MLA_ROPE, 64)]) for k in range(DT)]
    for g in range(4):
        for k in range(2):
            order += [("mla_w_kv_up_2", k * P, [((4 * g + j) * 256 + 128, P)]) for j in range(4)]
    for h in range(AH):
        if h % 2 == 0:
            order += [("mla_w_q_up_2", k * P, [(h * 192 + 128, 64), (h * 192 + 320, 64)]) for k in range(4)]
        order += [("mla_w_q_up_2", k * P, [(h * 192, P)]) for k in range(4)]
        order += [("mla_w_kv_up_2", k * P, [(h * 256, P)]) for k in range(2)]
        order += outs("mla_w_in_2", MLA_G, [h], DT)
    order += outs("mla_w_out_2", 0, range(8), IT)
    return order


NBLOCKS = len(weight_order())
NCHUNKS = -(-NBLOCKS // CB)

VECTORS = [("g_mix", 8), ("ret_norm_g", 8), ("dn_conv_w", 96), ("dn_norm_g", 1), ("g_ffn", 8),
           ("ffn_conv_w", 132), ("ffn_conv_b", 44), ("g_final", 8), ("norm_pre_2", 16), ("norm_post_2", 16),
           ("rwkv_mu_2", 48), ("rwkv_w0_2", 16), ("rwkv_a0_2", 16), ("rwkv_k_k_2", 16), ("rwkv_k_a_2", 16),
           ("rwkv_r_k_2", 16), ("rwkv_ln_w_2", 16), ("rwkv_ln_b_2", 16), ("mla_q_norm_2", 4),
           ("mla_kv_norm_2", 2), ("a_log", 1), ("dt_bias", 1)]
VOFF, _at = {}, 0
for _name, _n in VECTORS:
    VOFF[_name] = _at
    _at += _n
NVEC = _at


def constants():
    f = np.float32
    i, j = np.arange(P)[None, :], np.arange(P)[:, None]
    out = {"ident": np.eye(P), "ones": np.ones((P, P)), "mean128": np.full((P, P), 1 / 128)}
    out["center128"] = np.eye(P) - 1 / 128
    half = (i // 64) == (j // 64)
    out["ones64"] = half * 1.0
    out["mean64"] = half / 64
    out["center64"] = np.eye(P) - half / 64
    out["perm"] = ((i ^ 32) == j) * 1.0
    out["strict"] = (i > j) * 1.0
    out["causal"] = (i >= j) * 1.0
    lv = np.zeros((LEVELS, P, P))
    for l in range(LEVELS):
        s = 1 << l
        lv[l] = ((i // s) % 2 == 1) & ((j // s) == (i // s) - 1)
    out["levels"] = lv.transpose(1, 0, 2).reshape(P, -1)
    sel = np.zeros((P, H1, P))
    for h in range(H1):
        sel[h, h] = 1
    out["sel"] = sel.reshape(P, -1)
    st, ca = (i > j)[:RC, :RC], (i >= j)[:RC, :RC]
    m1, m2 = np.zeros((P, 2, RC)), np.zeros((P, 2, RC))
    m1[:RC, 0], m1[:RC, 1], m2[:RC, 0], m2[:RC, 1] = st, -1.0 * ca, st, ca
    out["mask_bk"] = np.concatenate([m1.reshape(P, -1), m2.reshape(P, -1)], axis=1)
    out["reset"] = np.broadcast_to((np.arange(T2) % RC != 0) * 1.0, (P, T2))
    out["eps"] = np.broadcast_to(np.array([EPS, GN_EPS, GN_EPS_2]), (P, 3))
    inv = (f(10000.0) ** (-np.arange(0, 64, 2, dtype=f) / f(64))).astype(f)
    lane = np.arange(P) % 64
    ang = (np.arange(T2, dtype=f)[None, :] * inv[lane % 32][:, None]).astype(f).astype(np.float64)
    sign = np.where(lane < 32, -1.0, 1.0)[:, None]
    out["cos"], out["sin"] = np.cos(ang), np.sin(ang) * sign
    neg = -3.0e38
    m = np.zeros((P, 384))
    m[:, 0:128] = np.where(j >= i, 0, neg)
    m[:, 256:384] = m[:, 0:128]
    out["amask"] = m
    m = np.zeros((P, T2))
    m[:META, 256:] = np.where(j >= i, 0, neg)[:META, :META]
    out["amask2"] = m
    return out


def decay_table():
    g = 1.0 - 2.0 ** (-5.0 - np.arange(H1, dtype=np.float32))
    lg = np.log(g.astype(np.float64))
    d = np.arange(T1)[None, :] - np.arange(P)[:, None]
    t = np.where(d >= 0, np.exp(lg[:, None, None] * np.maximum(d, 0)), 0) * 0.125
    return t.transpose(1, 0, 2).reshape(P, -1).astype(np.float32)


CONST = constants()
COFF, _at = {}, 0
for _name, _v in CONST.items():
    COFF[_name] = _at
    _at += _v.shape[1]
NCONST = _at


def build(nc, xT, metaT, wstream, vecs, consts, decays, wdbda, wlora, outT):
    ctx = ExitStack()
    with ctx:
        def sb(name, shape):
            return ctx.enter_context(nc.sbuf_tensor(name, shape, F32))

        sems = {}

        def S(name):
            if name not in sems:
                sems[name] = ctx.enter_context(nc.semaphore(name))
            return sems[name]

        loaded = [S(f"weights_loaded{i}") for i in range(SLOTS)]

        ring = sb("ring", [P, SLOTS * CB * P])
        h = sb("h", [P, DT, T2])
        u = sb("u", [P, DT, T2])
        vec = sb("vec", [P, NVEC])
        con = sb("con", [P, NCONST])
        sq = sb("sq", [P, DT, T2])
        sd = sb("sd", [P, T2])
        rs = sb("rs", [P, T2])
        arena = sb("arena", [P, 27500])
        taken = [0]

        def area(at, *dims):
            n = int(np.prod(dims))
            assert at + n <= 27500, (at, n)
            v = arena[:, at:at + n]
            if len(dims) == 2:
                v = v.rearrange("p (a b) -> p a b", a=dims[0])
            elif len(dims) == 3:
                v = v.rearrange("p (a b c) -> p a b c", a=dims[0], b=dims[1])
            elif len(dims) == 4:
                v = v.rearrange("p (a b c d) -> p a b c d", a=dims[0], b=dims[1], c=dims[2])
            taken[0] = at + n
            return v

        raw = area(0, 24, T1 + 3)
        dz, gr, gd = area(0, 8, T1), area(2048, 8, T1), area(4096, 8, T1)
        conv = area(6216, 24, T1)
        qkraw = area(taken[0], 8, T1)
        ro = qkraw
        qk = area(taken[0], 8, T1)
        vtok = area(taken[0], 2, D)
        rgate = area(taken[0], 8, T1)
        sT = area(taken[0], 2, 384)
        rn2 = area(taken[0], 512)
        sq2 = area(taken[0], 512)
        decay = area(taken[0], 8, T1)
        wdb = area(taken[0], 8, 16)
        rows = area(taken[0], 6, T1)
        cols = area(taken[0], 48)
        base = 6216 + 6144 + 2048
        Em = area(base, 4, P)
        Ea = area(taken[0], 4, P)
        ATd = area(taken[0], 4, P)
        attn = area(taken[0], 4, P)
        Td = area(taken[0], 4, P)
        Ud = area(taken[0], 4, P)
        Yd = area(taken[0], 4, P)
        vb = area(taken[0], 4, P)
        at_decay = 6216 + 6144 + 2048 * 4 + 768 + 1024
        AMd = area(at_decay, 2, 4, P)
        kbg = area(taken[0], 2, P)
        kdec = area(taken[0], 2, P)
        eg = area(taken[0], 2, P)
        qd = area(taken[0], 2, P)
        w1T = area(6216 + 6144 + 2048 * 4, 2, P)
        vn0 = area(taken[0], 2, P)
        S1 = area(taken[0], 2, P)
        vn1 = Em[:, 0:2, :]
        up = area(0, 4, T1 + 2)
        upc = area(1040, 4, T1)
        prod = area(2064, FT, T1)
        down = area(taken[0], 8, T1)
        xs = area(0, 4, DT, T2)
        dx = area(8704, DT, T2)
        xs_wa = area(8704 + 2176, 2, DT, T2)
        yo = area(8704, PAIRS, T2)
        lo = area(8704 + 6528, T2)
        wl = area(taken[0], INNER)
        gin = area(taken[0], 2, 6, T2)
        f_off = taken[0]
        cs, dd, Wc, Wi, Wp, kk2, sdk, kkn, kp, tk = [area(f_off + i * T2, T2) for i in range(10)]
        ar = area(taken[0], 2, T2)
        bk = area(taken[0], 2, T2)
        GG = area(taken[0], NRC, 2, 4 * RC)
        AMr = area(f_off, 8, RC)
        AMr2 = area(f_off + 5 * T2, 8, RC)
        sqf = sq[:, :, :].rearrange("p a b -> p (a b)")
        uf = u[:, :, :].rearrange("p a b -> p (a b)")
        Tr, Ur, Yr = [sqf[:, i * 8 * RC:(i + 1) * 8 * RC].rearrange("p (a b) -> p a b", a=8) for i in range(3)]
        Zs, nSA, S0 = [sqf[:, 24 * RC + i * P:24 * RC + (i + 1) * P] for i in range(3)]
        tok = uf[:, 0:NRC * 3 * P].rearrange("p (a b c) -> p a b c", a=NRC, b=3)
        bon, ys = [uf[:, NRC * 3 * P + i * T2:NRC * 3 * P + (i + 1) * T2] for i in range(2)]
        cq = area(0, 4, T2)
        ckv = area(taken[0], 2, T2)
        cqn = area(taken[0], 4, T2)
        ckvn = area(taken[0], 2, T2)
        kr = area(taken[0], 2, T2)
        vt = area(taken[0], 3, INNER)
        om = area(taken[0], AH, T2)
        qr = area(taken[0], 2, 3, T2)
        hin = area(taken[0], 2, 3, T2)
        pr = area(taken[0], 2, 384)
        pr2 = area(taken[0], 2, T2)
        pT = area(taken[0], 2, 432)
        nm = area(taken[0], 2, 12)
        mo = area(20000, DT, T2)

        bank = [ctx.enter_context(nc.psum_tensor(f"bank{i}", [P, 512], F32)) for i in range(8)]

        def C(name, n=P, rows_=P):
            return con[0:rows_, COFF[name]:COFF[name] + n]

        def V(name, t, rows_=P):
            return vec[0:rows_, VOFF[name] + t:VOFF[name] + t + 1]

        def eps_col(i):
            return con[:, COFF["eps"] + i:COFF["eps"] + i + 1]

        levels = con[:, COFF["levels"]:COFF["levels"] + LEVELS * P].rearrange("p (l n) -> p l n", l=LEVELS)
        sel = con[:, COFF["sel"]:COFF["sel"] + H1 * P].rearrange("p (l n) -> p l n", l=H1)

        def over(ap, n):
            r, c = ap.shape
            return ap.unsqueeze(1).to_broadcast([r, n, c])

        block = ctx.enter_context(nc.Block())

        outputs = gemm_sizes()
        starts = np.cumsum([0] + outputs)
        assert starts[-1] == NBLOCKS, (starts[-1], NBLOCKS)
        last_reader = [int(np.searchsorted(starts, min((c + 1) * CB, NBLOCKS), side="left")) for c in range(NCHUNKS)]
        BLOCK_STARTS = starts
        order_ids = gemm_signal_ids()

        @block.sync
        def _(sp):
            sp.dma_start(h[:, :, META:], xT).then_inc(S("x_loaded"), 16)
            sp.dma_start(vec[:, :], vecs).then_inc(S("vec_loaded"), 16)
            sp.dma_start(con[:, :], consts).then_inc(S("con_loaded"), 16)
            for c in range(NCHUNKS):
                if c >= SLOTS:
                    sp.wait_ge(S("proj_done"), order_ids[last_reader[c - SLOTS] - 1])
                sp.dma_start(ring[:, (c % SLOTS) * CB * P:(c % SLOTS + 1) * CB * P], wstream[c])\
                  .then_inc(loaded[c % SLOTS], 16)
                if c == 1:
                    sp.dma_start(decay, decays.rearrange("p (a b) -> p a b", a=8)).then_inc(S("decay_loaded"), 16)
                    sp.dma_start(wdb, wdbda.rearrange("p (a b) -> p a b", a=8)).then_inc(S("wdb_loaded"), 16)
            sp.wait_ge(S("out_ready"), 1)
            sp.dma_start(outT, h[:, :, META:]).then_inc(S("out_stored"), 16)
            sp.wait_ge(S("out_stored"), 16)

        @block.tensor
        def _(pe):
            blk = [0]
            pn = [0]
            seen = [-1]

            def weights(width=1):
                b = blk[0]
                c = b // CB
                if c > seen[0]:
                    seen[0] = c
                    pe.wait_ge(loaded[c % SLOTS], 16 * (c // SLOTS + 1))
                at = (b % (CB * SLOTS)) * P
                blk[0] += width
                return ring[:, at:at + width * P]

            def free_bank():
                if pn[0] >= 2:
                    pe.wait_ge(S("proj_taken"), pn[0] - 1)
                b = bank[pn[0] % 2]
                pn[0] += 1
                return b

            def project(rhs, kt, T):
                b = free_bank()
                for k in range(kt):
                    ins = nc.tensor.matmul(b[:, 0:T], weights(), rhs(k), start=k == 0, stop=k == kt - 1)
                ins.then_inc(S("proj_done"), 1)

            def project_tokens(lhs, kt, spans):
                b0 = blk[0]
                for t, (a, n) in enumerate(spans):
                    blk[0] = b0
                    b = free_bank()
                    for k in range(kt):
                        ins = nc.tensor.matmul(b[0:n, :], lhs(k)[:, a:a + n], weights(4), start=k == 0, stop=k == kt - 1)
                    ins.then_inc(S("proj_done"), 1)

            norm_n = [0]

            def norm(nt, T):
                norm_n[0] += 1
                pe.wait_ge(S("norm_sq"), norm_n[0])
                for t in range(nt):
                    ins = nc.tensor.matmul(bank[2][:, 0:T], C("ones"), sq[:, t, 0:T], start=t == 0, stop=t == nt - 1)
                ins.then_inc(S("norm_sum"), 1)

            pe.wait_ge(S("con_loaded"), 16)
            norm(DT, T1)
            pe.wait_ge(S("u_ready"), 1)
            uT = lambda k: u[:, k, 0:T1]
            for _m in range(8):
                project(uT, DT, T1)
            for _g in range(2):
                project_tokens(uT, DT, [(0, P), (P, P)])
            for _m in range(24):
                project(uT, DT, T1)
            pe.wait_ge(S("wdb_loaded"), 16)
            for j in range(2):
                for k in range(DT):
                    ins = nc.tensor.matmul(bank[2][0:8, j * T1:(j + 1) * T1], wdb[:, k, 8 * j:8 * j + 8], uT(k),
                                           start=k == 0, stop=k == DT - 1)
            ins.then_inc(S("dbda_done"), 1)
            for _m in range(8):
                project(uT, DT, T1)
            pe.wait_ge(S("proj_taken"), 8)
            for b in range(8):
                ins = nc.tensor.matmul(bank[3 + b // 2][:, (b % 2) * T1:(b % 2 + 1) * T1], C("perm"), qkraw[:, b, :],
                                       start=True, stop=True)
            ins.then_inc(S("swapped"), 1)
            pe.wait_ge(S("qk_ready"), 1)

            def ret_scores(hd):
                r = slice(64 * (hd % 2), 64 * (hd % 2) + 64)
                q, k = qk[r, hd // 2, :], qk[r, 4 + hd // 2, :]
                if hd >= 2:
                    pe.wait_ge(S("ret_decayed"), hd - 1)
                nc.tensor.matmul(bank[3 + hd % 2][:, 0:256], k[:, 0:128], q, start=True, stop=True)
                nc.tensor.matmul(bank[3 + hd % 2][:, 256:384], k[:, 128:256], q[:, 128:256], start=True, stop=True)\
                    .then_inc(S("ret_scores"), 1)

            ret_scores(0)
            for hd in range(H1):
                if hd + 1 < H1:
                    ret_scores(hd + 1)
                pe.wait_ge(S("ret_decayed"), hd + 1)
                if hd >= 2:
                    pe.wait_ge(S("ret_out_taken"), hd - 1)
                o = bank[5 + hd % 2]
                nc.tensor.matmul(o[:, 0:256], vtok[:, 0, hd * P:(hd + 1) * P], sT[:, hd % 2, 0:256], start=True, stop=False)
                nc.tensor.matmul(o[:, 128:256], vtok[:, 1, hd * P:(hd + 1) * P], sT[:, hd % 2, 256:384], start=False, stop=True)\
                    .then_inc(S("ret_out"), 1)
            for g in range(4):
                pe.wait_ge(S("ret_out_taken"), 2 * g + 2)
                if g >= 1:
                    pe.wait_ge(S("ret_normed"), g)
                nc.tensor.matmul(bank[7][:, :], C("center128"), ro[:, 2 * g:2 * g + 2, :], start=True, stop=True)\
                    .then_inc(S("ret_centered"), 1)
                pe.wait_ge(S("ret_sq"), g + 1)
                nc.tensor.matmul(bank[2][:, :], C("mean128"), sq2, start=True, stop=True).then_inc(S("ret_var"), 1)

            for _m in range(24):
                project(uT, DT, T1)

            for n in range(8):
                pe.wait_ge(S("l2_sq"), n + 1)
                nc.tensor.matmul(bank[3][:, :], C("ones"), sq2, start=True, stop=True).then_inc(S("l2_sum"), 1)
            pe.wait_ge(S("rows_ready"), 1)
            for j, (r, c) in enumerate(((0, 0), (0, 1), (2, 0), (2, 1), (3, 0), (4, 1))):
                ins = nc.tensor.matmul(bank[3][:, 8 * j:8 * j + 8], rows[0:8, r, c * CH:(c + 1) * CH], C("ident", 8, 8),
                                       start=True, stop=True)
            ins.then_inc(S("cols_done"), 1)
            pe.wait_ge(S("l2_done"), 8)
            for g in range(4):
                hs = (2 * g, 2 * g + 1)
                if g >= 1:
                    pe.wait_ge(S("dn_out"), g)
                else:
                    pe.wait_ge(S("cols_taken"), 1)
                for i, hd in enumerate(hs):
                    nc.tensor.matmul(bank[2][:, i * T1:(i + 1) * T1], sel[0:8, hd, :], rows[0:8, 2, :], start=True, stop=True)
                for i, hd in enumerate(hs):
                    ins = nc.tensor.matmul(bank[3][:, i * T1:(i + 1) * T1], sel[0:8, hd, :], rows[0:8, 0, :], start=True, stop=True)
                ins.then_inc(S("dn_bcast"), 1)
                for i, hd in enumerate(hs):
                    for c in range(2):
                        m, t = 2 * i + c, slice(c * CH, (c + 1) * CH)
                        nc.tensor.matmul(bank[4][:, m * P:(m + 1) * P], conv[:, hd, t], conv[:, hd, t], start=True, stop=True)
                        nc.tensor.matmul(bank[5][:, m * P:(m + 1) * P], conv[:, hd, t], conv[:, 8 + hd, t], start=True, stop=True)
                        nc.tensor.matmul(bank[6][:, m * P:(m + 1) * P], conv[:, 16 + hd, t], C("ident"), start=True, stop=True)
                        ins = nc.tensor.matmul(bank[7][:, m * P:(m + 1) * P], conv[:, hd, t], C("ident"), start=True, stop=True)
                ins.then_inc(S("dn_grams"), 1)
                pe.wait_ge(S("dn_mask"), 7 * g + 1)
                pe.wait_ge(S("dn_e_ready"), g + 1)
                for m in range(4):
                    ins = nc.tensor.matmul(bank[3][:, m * P:(m + 1) * P], AMd[:, 0, m, :], C("ident"), start=True, stop=True)
                ins.then_inc(S("dn_first"), 1)
                for l in range(1, LEVELS):
                    pe.wait_ge(S("dn_mask"), 7 * g + l + 1)
                    pe.wait_ge(S("dn_step"), 7 * g + l)
                    for m in range(4):
                        ins = nc.tensor.matmul(bank[2][:, m * P:(m + 1) * P], AMd[:, l % 2, m, :], Td[:, m, :], start=True, stop=True)
                    ins.then_inc(S("dn_y"), 1)
                    pe.wait_ge(S("dn_y_taken"), 6 * g + l)
                    if l < LEVELS - 1:
                        for m in range(4):
                            nc.tensor.matmul(bank[3][:, m * P:(m + 1) * P], Ud[:, m, :], Yd[:, m, :], start=True, stop=True)
                    for m in range(4):
                        ins = nc.tensor.matmul(bank[4][:, m * P:(m + 1) * P], Yd[:, m, :], Ud[:, m, :], start=True, stop=True)
                    ins.then_inc(S("dn_delta"), 1)
                pe.wait_ge(S("dn_step"), 7 * g + 7)
                pe.wait_ge(S("dn_toks"), g + 1)
                for i in range(2):
                    nc.tensor.matmul(bank[2][:, i * P:(i + 1) * P], kbg[:, i, :], Ud[:, 2 * i + 1, :], start=True, stop=True)
                for i in range(2):
                    ins = nc.tensor.matmul(bank[2][:, (2 + i) * P:(3 + i) * P], Ud[:, 2 * i, :], vb[:, 2 * i, :], start=True, stop=True)
                ins.then_inc(S("dn_wv"), 1)
                pe.wait_ge(S("dn_wv_taken"), g + 1)
                for i in range(2):
                    ins = nc.tensor.matmul(bank[3][:, i * P:(i + 1) * P], kdec[:, i, :], vn0[:, i, :], start=True, stop=True)
                ins.then_inc(S("dn_s"), 1)
                pe.wait_ge(S("dn_s_taken"), g + 1)
                for i in range(2):
                    nc.tensor.matmul(bank[4][:, i * P:(i + 1) * P], Ud[:, 2 * i + 1, :], vb[:, 2 * i + 1, :], start=True, stop=False)
                    ins = nc.tensor.matmul(bank[4][:, i * P:(i + 1) * P], w1T[:, i, :], S1[:, i, :], start=False, stop=True)
                ins.then_inc(S("dn_v1"), 1)
                pe.wait_ge(S("dn_v1_taken"), g + 1)
                for i in range(2):
                    nc.tensor.matmul(bank[5][:, i * T1:i * T1 + P], vn0[:, i, :], attn[:, 2 * i, :], start=True, stop=True)
                    nc.tensor.matmul(bank[5][:, i * T1 + P:(i + 1) * T1], S1[:, i, :], qd[:, i, :], start=True, stop=False)
                    ins = nc.tensor.matmul(bank[5][:, i * T1 + P:(i + 1) * T1], vn1[:, i, :], attn[:, 2 * i + 1, :],
                                           start=False, stop=True)
                ins.then_inc(S("dn_o"), 1)
                pe.wait_ge(S("dn_o_sq"), g + 1)
                nc.tensor.matmul(bank[6][:, :], C("mean128"), sq2, start=True, stop=True).then_inc(S("dn_var"), 1)

            pe.wait_ge(S("ret_gated"), 1)
            for _m in range(8):
                project(lambda k: ro[:, k, :], DT, T1)
            pe.wait_ge(S("dn_gated"), 1)
            for _m in range(8):
                project(lambda k: conv[:, 16 + k, :], DT, T1)
            pe.wait_ge(S("merged"), 1)
            for _m in range(8):
                project(lambda k: gr[:, k, :], DT, T1)
            norm(DT, T1)
            pe.wait_ge(S("u_ready"), 2)
            for _m in range(2 * FT):
                project(uT, DT, T1)
            pe.wait_ge(S("ffn_prod"), FT)
            for _m in range(8):
                project(lambda k: prod[:, k, :], FT, T1)
            norm(DT, T1)

            norm(DT, T2)
            pe.wait_ge(S("lerped"), 1)
            b = free_bank()
            wb = []
            for k in range(DT):
                wb.append(weights())
                for j in range(2):
                    ins = nc.tensor.matmul(b[64 * j:64 * j + 64, 0:T2], wb[k][:, 64 * j:64 * j + 64], xs_wa[:, j, k, :],
                                           start=k == 0, stop=k == DT - 1)
            ins.then_inc(S("proj_done"), 1)

            def lora(j, p):
                b = free_bank()
                r = slice(64 * j, 64 * j + 64)
                nc.tensor.matmul(b[:, 0:T2], wl[r, p * P:(p + 1) * P], lo[r, :], start=True, stop=True)\
                    .then_inc(S("proj_done"), 1)

            def rwkv_project(p, j):
                if j == 0 and p >= 1:
                    pass
                if j < 2:
                    lora(j, p)
                else:
                    project(lambda k: xs[:, j - 2, k, :], DT, T2)

            pe.wait_ge(S("proj_taken"), pn[0])
            pe.wait_ge(S("wl_loaded"), 16)
            for j in range(6):
                rwkv_project(0, j)
            for p in range(PAIRS):
                pe.wait_ge(S("rw_kk2"), p + 1)
                nc.tensor.matmul(bank[2][:, 0:T2], C("ones64"), kk2, start=True, stop=True).then_inc(S("rw_kksum"), 1)
                pe.wait_ge(S("rw_feats"), p + 1)
                nc.tensor.matmul(bank[2][:, 0:T2], C("ones64"), tk, start=True, stop=True).then_inc(S("rw_bonus"), 1)
                vcur = gin[:, p % 2, 4, :]
                for c in range(NRC):
                    t = slice(c * RC, (c + 1) * RC)
                    if c >= 1:
                        pe.wait_ge(S("rw_grams_taken"), 4 * p + c)
                    for i in range(2):
                        for j in range(2):
                            r = slice(64 * j, 64 * j + 64)
                            ins = nc.tensor.matmul(bank[3 + j][0:RC, i * 2 * RC:(i + 1) * 2 * RC], bk[r, i, t], ar[r, :, t],
                                                   start=True, stop=True)
                    ins.then_inc(S("rw_grams"), 1)
                    if c >= 1:
                        pe.wait_ge(S("rw_toks_taken"), 4 * p + c)
                    for j, src in enumerate((vcur, bk[:, 1, :], bk[:, 0, :])):
                        ins = nc.tensor.matmul(bank[7][0:RC, j * P:(j + 1) * P], src[:, t], C("ident"), start=True, stop=True)
                    ins.then_inc(S("rw_toks"), 1)
                pe.wait_ge(S("rw_mask"), 7 * p + 1)
                pe.wait_ge(S("rw_grams_taken"), 4 * p + 4)
                for m in range(8):
                    ins = nc.tensor.matmul(bank[5 + m // 4][0:RC, (m % 4) * RC:(m % 4 + 1) * RC], AMr[0:RC, m, :],
                                           C("ident", RC, RC), start=True, stop=True)
                ins.then_inc(S("rw_first"), 1)
                for l in range(1, LEVELS):
                    pe.wait_ge(S("rw_mask"), 7 * p + l + 1)
                    pe.wait_ge(S("rw_step"), 7 * p + l)
                    am = (AMr, AMr2)[l % 2]
                    for m in range(8):
                        ins = nc.tensor.matmul(bank[3 + m // 4][0:RC, (m % 4) * RC:(m % 4 + 1) * RC], am[0:RC, m, :],
                                               Tr[0:RC, m, :], start=True, stop=True)
                    ins.then_inc(S("rw_y"), 1)
                    if p + 1 < PAIRS:
                        rwkv_project(p + 1, l - 1)
                    pe.wait_ge(S("rw_y_taken"), 6 * p + l)
                    if l < LEVELS - 1:
                        for m in range(8):
                            nc.tensor.matmul(bank[5 + m // 4][0:RC, (m % 4) * RC:(m % 4 + 1) * RC], Ur[0:RC, m, :],
                                             Yr[0:RC, m, :], start=True, stop=True)
                    for m in range(8):
                        ins = nc.tensor.matmul(bank[3 + m // 4][0:RC, (m % 4) * RC:(m % 4 + 1) * RC], Yr[0:RC, m, :],
                                               Ur[0:RC, m, :], start=True, stop=True)
                    ins.then_inc(S("rw_delta"), 1)
                pe.wait_ge(S("rw_step"), 7 * p + 7)
                pe.wait_ge(S("rw_toks_taken"), 4 * p + 4)
                for c in range(NRC):
                    t = slice(c * RC, (c + 1) * RC)
                    if c >= 1:
                        pe.wait_ge(S("rw_state_taken"), 3 * p + c)
                        nc.tensor.matmul(bank[7][:, t], S0, ar[:, 1, t], start=True, stop=False)
                        nc.tensor.matmul(bank[5][0:RC, 0:P], ar[:, 0, t], S0, start=True, stop=False)
                    for j in range(2):
                        f = slice(64 * j, 64 * j + 64)
                        ins = nc.tensor.matmul(bank[5][0:RC, f], GG[0:RC, c, j, 2 * RC:3 * RC], tok[0:RC, c, 0, f],
                                               start=c == 0, stop=c == 0 or j == 1)
                    ins.then_inc(S("rw_z"), 1)
                    pe.wait_ge(S("rw_z_taken"), 4 * p + c + 1)
                    for j in range(2):
                        f = slice(64 * j, 64 * j + 64)
                        ins = nc.tensor.matmul(bank[6][0:RC, f], Ur[0:RC, 2 * c + j, :], Zs[0:RC, f], start=True, stop=True)
                    ins.then_inc(S("rw_sa"), 1)
                    pe.wait_ge(S("rw_sa_taken"), 4 * p + c + 1)
                    if c < NRC - 1:
                        nc.tensor.matmul(bank[3][:, 0:P], tok[0:RC, c, 1, :], tok[0:RC, c, 0, :], start=True, stop=False)
                        nc.tensor.matmul(bank[3][:, 0:P], tok[0:RC, c, 2, :], nSA[0:RC, :], start=False, stop=True)\
                            .then_inc(S("rw_state"), 1)
                    for j in range(2):
                        f = slice(64 * j, 64 * j + 64)
                        nc.tensor.matmul(bank[7][f, t], nSA[0:RC, f], GG[0:RC, c, j, RC:2 * RC], start=c == 0, stop=False)
                        ins = nc.tensor.matmul(bank[7][f, t], tok[0:RC, c, 0, f], GG[0:RC, c, j, 3 * RC:4 * RC], start=False,
                                               stop=True)
                    ins.then_inc(S("rw_yc"), 1)
                pe.wait_ge(S("rw_ys"), p + 1)
                nc.tensor.matmul(bank[3][:, 0:T2], C("center64"), ys, start=True, stop=True).then_inc(S("rw_centered"), 1)
                pe.wait_ge(S("rw_sq"), p + 1)
                nc.tensor.matmul(bank[4][:, 0:T2], C("mean64"), kk2, start=True, stop=True).then_inc(S("rw_var"), 1)
                pe.wait_ge(S("rw_pair_done"), p + 1)
            for _m in range(8):
                project(lambda k: yo[:, k, :], IT, T2)
            norm(DT, T2)

            norm(DT, T2)
            pe.wait_ge(S("u_ready"), 3)
            u2 = lambda k: u[:, k, :]
            for _m in range(4 + 2 + 1):
                project(u2, DT, T2)
            norm(4, T2)
            norm(2, T2)
            pe.wait_ge(S("proj_taken"), pn[0])
            nc.tensor.matmul(bank[3][:, 0:T2], C("perm"), kr[:, 0, :], start=True, stop=True).then_inc(S("kr_swapped"), 1)
            pe.wait_ge(S("lat_ready"), 1)
            for g in range(4):
                project_tokens(lambda k: ckvn[:, k, :], 2, [(0, P), (P, P), (2 * P, META)])

            in_ready, raw_ready = {}, {}

            def head_project(hd):
                if hd % 2 == 0:
                    project(lambda k: cqn[:, k, :], 4, T2)
                    raw_ready[hd] = pn[0]
                project(lambda k: cqn[:, k, :], 4, T2)
                project(lambda k: ckvn[:, k, :], 2, T2)
                project(u2, DT, T2)
                in_ready[hd] = pn[0]

            def swap_q(hd):
                pe.wait_ge(S("proj_taken"), raw_ready[hd])
                nc.tensor.matmul(bank[2][:, 0:T2], C("perm"), qr[:, (hd // 2) % 2, 0, :], start=True, stop=True)\
                    .then_inc(S("qr_swapped"), 1)

            head_project(0)
            swap_q(0)
            pe.wait_ge(S("kr_ready"), 1)
            for hd in range(AH):
                q, k = hin[:, hd % 2, 0, :], hin[:, hd % 2, 1, :]
                r = slice(64 * (hd % 2), 64 * (hd % 2) + 64)
                qrot, krot = qr[r, (hd // 2) % 2, 2, :], kr[r, 1, :]
                pe.wait_ge(S("proj_taken"), in_ready[hd])
                pe.wait_ge(S("qr_ready"), hd // 2 + 1)
                if hd >= 1:
                    pe.wait_ge(S("at_masked"), hd)
                for o, q0, nq, nk in ((bank[3][:, 0:128], 0, P, 128), (bank[3][:, 128:384], P, P, 256), (bank[4][0:META, 0:T2], 2 * P, META, T2)):
                    nc.tensor.matmul(o, q[:, q0:q0 + nq], k[:, 0:nk], start=True, stop=False)
                    ins = nc.tensor.matmul(o, qrot[:, q0:q0 + nq], krot[:, 0:nk], start=False, stop=True)
                ins.then_inc(S("at_scores"), 1)
                if hd + 1 < AH:
                    head_project(hd + 1)
                    if (hd + 1) % 2 == 0:
                        swap_q(hd + 1)
                pe.wait_ge(S("at_probs"), hd + 1)
                pb = hd % 2
                for o, src, n in ((bank[6][:, 0:128], pr[:, pb, 0:128], P), (bank[6][:, 128:256], pr[:, pb, 128:256], P),
                                  (bank[6][:, 256:272], pr2[0:META, pb, 0:128], META),
                                  (bank[6][:, 272:400], pr[:, pb, 256:384], P), (bank[6][:, 400:416], pr2[0:META, pb, 128:256], META),
                                  (bank[6][0:META, 416:432], pr2[0:META, pb, 256:272], META)):
                    ins = nc.tensor.matmul(o, src, C("ident", n, n), start=True, stop=True)
                ins.then_inc(S("at_pT"), 1)
                pe.wait_ge(S("at_pT_taken"), hd + 1)
                if hd >= 1:
                    pe.wait_ge(S("at_o_taken"), hd)
                v = slice(hd * P, (hd + 1) * P)
                nc.tensor.matmul(bank[7][:, 0:T2], vt[:, 0, v], pT[:, pb, 0:T2], start=True, stop=False)
                nc.tensor.matmul(bank[7][:, P:T2], vt[:, 1, v], pT[:, pb, 272:416], start=False, stop=False)
                nc.tensor.matmul(bank[7][:, 2 * P:T2], vt[0:META, 2, v], pT[0:META, pb, 416:432], start=False, stop=True)\
                    .then_inc(S("at_o"), 1)
            pe.wait_ge(S("at_o_taken"), AH)
            for _m in range(8):
                project(lambda k: om[:, k, :], IT, T2)
            norm(DT, T2)
            assert blk[0] == NBLOCKS

        @block.scalar
        def _(act):
            taken_n = [0]
            chain = [0]

            def link(ins):
                chain[0] += 1
                ins.then_inc(S("act_chain"), 1)
                act.wait_ge(S("act_chain"), chain[0])

            def take(out, func=ACT.Copy, rows_=slice(0, P), n=T1, **kw):
                i = taken_n[0]
                taken_n[0] += 1
                act.wait_ge(S("proj_done"), order_ids[i])
                nc.scalar.activation(out, bank[i % 2][rows_, 0:n], func, **kw).then_inc(S("proj_taken"), 1)

            norm_n = [0]

            def norm(src, nt, T, width):
                norm_n[0] += 1
                nc.scalar.activation(sq[:, 0:nt, 0:T], src, ACT.Square).then_inc(S("norm_sq"), 1)
                act.wait_ge(S("norm_sum"), norm_n[0])
                nc.scalar.activation(sd[:, 0:T], bank[2][:, 0:T], ACT.Sqrt, bias=eps_col(0), scale=1.0 / width)\
                    .then_inc(S("norm_sd"), 1)

            act.dma_start(h[:, :, 0:META], metaT).then_inc(S("x_loaded"), 16)
            act.wait_ge(S("x_loaded"), 32)
            act.wait_ge(S("con_loaded"), 16)
            act.wait_ge(S("vec_loaded"), 16)
            norm(h[:, :, META:], DT, T1, D)
            for b in range(8):
                take(qkraw[:, b, :])
            for g in range(2):
                for t in range(2):
                    take(vtok[:, t, g * 512:(g + 1) * 512], n=512)
            act.wait_ge(S("raw_zeroed"), 1)
            for b in range(24):
                take(raw[:, b, 3:])
            act.wait_ge(S("dbda_done"), 1)
            nc.scalar.activation(rows[0:8, 0, :], bank[2][0:8, 0:T1], ACT.Sigmoid)
            nc.scalar.activation(rows[0:8, 1, :], bank[2][0:8, T1:2 * T1], ACT.Identity, bias=V("dt_bias", 0, 8))\
                .then_inc(S("row_y"), 1)
            act.wait_ge(S("row_abs"), 1)
            link(nc.scalar.activation(rows[0:8, 5, :], rows[0:8, 5, :], ACT.Exp))
            nc.scalar.activation(rows[0:8, 5, :], rows[0:8, 5, :], ACT.Ln, bias=1.0)
            nc.scalar.activation(sd[0:8, 0:1], V("a_log", 0, 8), ACT.Exp).then_inc(S("row_ln"), 1)
            for b in range(8):
                take(rgate[:, b, :], ACT.Silu)
            for s in range(3):
                act.wait_ge(S("conv_done"), s + 1)
                nc.scalar.activation(conv[:, 8 * s:8 * s + 8, :], conv[:, 8 * s:8 * s + 8, :], ACT.Silu)\
                    .then_inc(S("conv_silu"), 1)
            for hd in range(H1):
                act.wait_ge(S("ret_out"), hd + 1)
                nc.scalar.activation(ro[:, hd, :], bank[5 + hd % 2][:, 0:T1], ACT.Copy).then_inc(S("ret_out_taken"), 1)
            for g in range(4):
                act.wait_ge(S("ret_centered"), g + 1)
                nc.scalar.activation(sq2, bank[7][:, :], ACT.Square).then_inc(S("ret_sq"), 1)
                act.wait_ge(S("ret_var"), g + 1)
                if g >= 1:
                    act.wait_ge(S("ret_normed"), g)
                nc.scalar.activation(rn2, bank[2][:, :], ACT.Sqrt, bias=eps_col(1)).then_inc(S("ret_sd"), 1)
            act.wait_ge(S("conv_done"), 3)
            for b in range(8):
                take(dz[:, b, :], ACT.Silu)
            for b in range(8):
                take(gr[:, b, :], ACT.Sigmoid)
            for b in range(8):
                take(gd[:, b, :], ACT.Sigmoid)
            act.wait_ge(S("conv_silu"), 3)
            for n in range(8):
                nc.scalar.activation(sq2, conv[:, 2 * n:2 * n + 2, :].rearrange("p a b -> p (a b)"), ACT.Square)\
                    .then_inc(S("l2_sq"), 1)
                act.wait_ge(S("l2_sum"), n + 1)
                act.wait_ge(S("ret_normed"), 4)
                if n >= 1:
                    act.wait_ge(S("l2_done"), n)
                nc.scalar.activation(rn2, bank[3][:, :], ACT.Sqrt, bias=eps_col(0)).then_inc(S("l2_sd"), 1)
            act.wait_ge(S("rows_g"), 1)
            nc.scalar.activation(rows[0:8, 3, 0:CH], rows[0:8, 3, 0:CH], ACT.Exp)
            nc.scalar.activation(rows[0:8, 4, :], rows[0:8, 2, :], ACT.Exp).then_inc(S("rows_exp"), 1)
            act.wait_ge(S("cols_done"), 1)
            nc.scalar.activation(cols, bank[3][:, 0:48], ACT.Copy).then_inc(S("cols_taken"), 1)
            for g in range(4):
                act.wait_ge(S("dn_diff"), g + 1)
                nc.scalar.activation(Em, Em, ACT.Exp)
                if g >= 1:
                    act.wait_ge(S("dn_out"), g)
                for i in range(2):
                    ins = nc.scalar.activation(eg[:, i, :], bank[2][:, i * T1 + P:(i + 1) * T1], ACT.Exp)
                ins.then_inc(S("dn_exp"), 1)
                act.wait_ge(S("dn_grams"), g + 1)
                act.wait_ge(S("cols_taken"), 1)
                for i in range(2):
                    hd = 2 * g + i
                    for c in range(2):
                        m = 2 * i + c
                        nc.scalar.activation(vb[:, m, :], bank[6][:, m * P:(m + 1) * P], ACT.Copy, scale=cols[:, 8 * c + hd:8 * c + hd + 1])
                    nc.scalar.activation(kdec[:, i, :], bank[7][:, 2 * i * P:(2 * i + 1) * P], ACT.Copy, scale=cols[:, 32 + hd:33 + hd])
                    ins = nc.scalar.activation(kbg[:, i, :], bank[7][:, (2 * i + 1) * P:(2 * i + 2) * P], ACT.Copy,
                                               scale=cols[:, 40 + hd:41 + hd])
                ins.then_inc(S("dn_toks"), 1)
                for l in range(1, LEVELS):
                    act.wait_ge(S("dn_y"), 6 * g + l)
                    nc.scalar.activation(Yd, bank[2][:, :], ACT.Copy).then_inc(S("dn_y_taken"), 1)
                act.wait_ge(S("dn_wv"), g + 1)
                nc.scalar.activation(w1T, bank[2][:, 0:256], ACT.Copy)
                nc.scalar.activation(vn0, bank[2][:, 256:512], ACT.Copy).then_inc(S("dn_wv_taken"), 1)
                act.wait_ge(S("dn_s"), g + 1)
                nc.scalar.activation(S1, bank[3][:, 0:256], ACT.Copy).then_inc(S("dn_s_taken"), 1)
                act.wait_ge(S("dn_v1"), g + 1)
                nc.scalar.activation(vn1, bank[4][:, 0:256], ACT.Copy).then_inc(S("dn_v1_taken"), 1)
                act.wait_ge(S("dn_o"), g + 1)
                nc.scalar.activation(sq2, bank[5][:, :], ACT.Square).then_inc(S("dn_o_sq"), 1)
                act.wait_ge(S("dn_var"), g + 1)
                nc.scalar.activation(rn2, bank[6][:, :], ACT.Sqrt, bias=eps_col(0)).then_inc(S("dn_sd"), 1)
            for b in range(8):
                take(u[:, b, 0:T1])
            for b in range(8):
                take(sq[:, b, 0:T1])
            for b in range(8):
                take(conv[:, b, :])
            act.wait_ge(S("h_ready"), 1)
            norm(h[:, :, META:], DT, T1, D)
            act.wait_ge(S("up_zeroed"), 1)

            def up_silu(m):
                act.wait_ge(S("upc_ready"), m + 1)
                nc.scalar.activation(prod[:, m, :], upc[:, 2 * (m % 2), :], ACT.Silu).then_inc(S("up_silu"), 1)

            for m in range(FT):
                s = 2 * (m % 2)
                if m >= 2:
                    act.wait_ge(S("upc_ready"), m - 1)
                take(up[:, s, 2:])
                take(up[:, s + 1, 2:])
                if m >= 1:
                    up_silu(m - 1)
            up_silu(FT - 1)
            for b in range(8):
                take(down[:, b, :])
            act.wait_ge(S("h_ready"), 2)
            norm(h[:, :, META:], DT, T1, D)

            act.dma_start(wl, wlora).then_inc(S("wl_loaded"), 16)
            act.wait_ge(S("h_ready"), 3)
            norm(h[:, :, :], DT, T2, D)
            act.wait_ge(S("proj_done"), order_ids[taken_n[0]])
            i = taken_n[0]
            taken_n[0] += 1
            nc.scalar.activation(lo[0:64, :], bank[i % 2][0:64, 0:T2], ACT.Tanh)
            nc.scalar.activation(lo[64:128, :], bank[i % 2][64:128, 0:T2], ACT.Copy).then_inc(S("proj_taken"), 1)

            def take_rwkv(p, j):
                g = gin[:, p % 2, j, :]
                if j == 0 and p >= 2:
                    act.wait_ge(S("rw_pair_done"), p - 1)
                if j == 0:
                    take(g, ACT.Sigmoid, n=T2, bias=V("rwkv_w0_2", p))
                elif j == 1:
                    take(g, ACT.Sigmoid, n=T2, bias=V("rwkv_a0_2", p))
                elif j == 5:
                    take(g, ACT.Silu, n=T2)
                else:
                    take(g, n=T2)

            for j in range(6):
                take_rwkv(0, j)
            for p in range(PAIRS):
                g = gin[:, p % 2]
                act.wait_ge(S("proj_taken"), taken_n[0])
                if p >= 1:
                    act.wait_ge(S("rw_pair_done"), p)
                nc.scalar.activation(kk2, g[:, 2, :], ACT.Square, scale=V("rwkv_k_k_2", p)).then_inc(S("rw_kk2"), 1)
                act.wait_ge(S("rw_kksum"), p + 1)
                nc.scalar.activation(sdk, bank[2][:, 0:T2], ACT.Sqrt).then_inc(S("rw_kksd"), 1)
                act.wait_ge(S("rw_cs"), p + 1)
                nc.scalar.activation(Wc, cs, ACT.Exp, scale=-DECAY_C)
                nc.scalar.activation(Wi, cs, ACT.Exp, scale=DECAY_C)
                nc.scalar.activation(Wp, dd, ACT.Exp, scale=-DECAY_C).then_inc(S("rw_w"), 1)
                act.wait_ge(S("rw_bonus"), p + 1)
                nc.scalar.activation(bon, bank[2][:, 0:T2], ACT.Copy).then_inc(S("rw_bonus_taken"), 1)
                for c in range(NRC):
                    act.wait_ge(S("rw_toks"), 4 * p + c + 1)
                    nc.scalar.activation(tok[0:RC, c, 0:2, :], bank[7][0:RC, 0:256], ACT.Copy)
                    nc.scalar.activation(tok[0:RC, c, 2, :], bank[7][0:RC, 256:384], ACT.Copy, scale=-1.0)\
                        .then_inc(S("rw_toks_taken"), 1)
                for l in range(1, LEVELS):
                    act.wait_ge(S("rw_y"), 6 * p + l)
                    nc.scalar.activation(Yr[0:RC, 0:4, :], bank[3][0:RC, 0:4 * RC], ACT.Copy)
                    nc.scalar.activation(Yr[0:RC, 4:8, :], bank[4][0:RC, 0:4 * RC], ACT.Copy).then_inc(S("rw_y_taken"), 1)
                    if p + 1 < PAIRS:
                        take_rwkv(p + 1, l - 1)
                for c in range(NRC):
                    act.wait_ge(S("rw_z"), 4 * p + c + 1)
                    nc.scalar.activation(Zs[0:RC, :], bank[5][0:RC, 0:P], ACT.Copy).then_inc(S("rw_z_taken"), 1)
                    act.wait_ge(S("rw_sa"), 4 * p + c + 1)
                    if c >= 1:
                        act.wait_ge(S("rw_yc"), 4 * p + c)
                    nc.scalar.activation(nSA[0:RC, :], bank[6][0:RC, 0:P], ACT.Copy).then_inc(S("rw_sa_taken"), 1)
                act.wait_ge(S("rw_yc"), 4 * p + 4)
                nc.scalar.activation(ys, bank[7][:, 0:T2], ACT.Copy).then_inc(S("rw_ys"), 1)
                act.wait_ge(S("rw_centered"), p + 1)
                nc.scalar.activation(kk2, bank[3][:, 0:T2], ACT.Square).then_inc(S("rw_sq"), 1)
                act.wait_ge(S("rw_var"), p + 1)
                nc.scalar.activation(sdk, bank[4][:, 0:T2], ACT.Sqrt, bias=eps_col(2)).then_inc(S("rw_sd"), 1)
            act.wait_ge(S("rw_pair_done"), PAIRS)
            for b in range(8):
                take(mo[:, b, :], n=T2)
            act.wait_ge(S("proj_taken"), taken_n[0])
            norm(mo, DT, T2, D)

            act.wait_ge(S("h_ready"), 4)
            norm(h[:, :, :], DT, T2, D)
            for b in range(4):
                take(cq[:, b, :], n=T2)
            for b in range(2):
                take(ckv[:, b, :], n=T2)
            take(kr[:, 0, :], n=T2)
            act.wait_ge(S("proj_taken"), taken_n[0])
            norm(cq, 4, T2, 512)
            act.wait_ge(S("cq_done"), 1)
            norm(ckv, 2, T2, 256)
            for g in range(4):
                for t, n in ((0, P), (1, P), (2, META)):
                    take(vt[0:n, t, g * 512:(g + 1) * 512], rows_=slice(0, n), n=512)

            def take_head(hd):
                if hd >= 2:
                    act.wait_ge(S("at_o_taken"), hd - 1)
                g = hin[:, hd % 2]
                if hd % 2 == 0:
                    take(qr[:, (hd // 2) % 2, 0, :], n=T2)
                take(g[:, 0, :], n=T2)
                take(g[:, 1, :], n=T2)
                take(g[:, 2, :], ACT.Silu, n=T2)

            take_head(0)
            for hd in range(AH):
                if hd + 1 < AH:
                    take_head(hd + 1)
                act.wait_ge(S("at_max"), hd + 1)
                pb = hd % 2
                nc.scalar.activation(pr[:, pb, 0:128], pr[:, pb, 0:128], ACT.Exp, scale=SCALE_A, bias=nm[:, pb, 3:4], accum_out=nm[:, pb, 6:7])
                nc.scalar.activation(pr[:, pb, 128:384], pr[:, pb, 128:384], ACT.Exp, scale=SCALE_A, bias=nm[:, pb, 4:5], accum_out=nm[:, pb, 7:8])
                nc.scalar.activation(pr2[0:META, pb, :], pr2[0:META, pb, :], ACT.Exp, scale=SCALE_A, bias=nm[0:META, pb, 5:6],
                                     accum_out=nm[0:META, pb, 8:9]).then_inc(S("at_exp"), 1)
                act.wait_ge(S("at_pT"), hd + 1)
                nc.scalar.activation(pT[:, pb, 0:416], bank[6][:, 0:416], ACT.Copy)
                nc.scalar.activation(pT[0:META, pb, 416:432], bank[6][0:META, 416:432], ACT.Copy).then_inc(S("at_pT_taken"), 1)
            for b in range(8):
                take(mo[:, b, :], n=T2)
            act.wait_ge(S("proj_taken"), taken_n[0])
            norm(mo, DT, T2, D)

        @block.vector
        def _(dve):
            chain = [0]
            V_ = nc.vector

            def link(ins):
                chain[0] += 1
                ins.then_inc(S("dve_chain"), 1)
                dve.wait_ge(S("dve_chain"), chain[0])

            norm_n = [0]

            def norm(outs, srcs, gains, T, signal, **kw):
                norm_n[0] += 1
                dve.wait_ge(S("norm_sd"), norm_n[0])
                link(V_.reciprocal(rs[:, 0:T], sd[:, 0:T]))
                for o, s, g in zip(outs, srcs, gains):
                    ins = V_.scalar_tensor_tensor(out=o, in0=s, scalar=g, in1=rs[:, 0:T], op0=ALU.mult, op1=ALU.mult)
                if signal is None:
                    link(ins)
                else:
                    ins.then_inc(S(signal), 1)

            V_.memset(raw[:, :, 0:3], 0.0).then_inc(S("raw_zeroed"), 1)
            dve.wait_ge(S("vec_loaded"), 16)
            dve.wait_ge(S("con_loaded"), 16)
            norm([u[:, t, 0:T1] for t in range(DT)], [h[:, t, META:] for t in range(DT)],
                 [V("g_mix", t) for t in range(DT)], T1, "u_ready")
            for s, first in enumerate((8, 0, 16)):
                dve.wait_ge(S("proj_taken"), 12 + 8 * (s + 1))
                for tap in (3, 0, 1, 2):
                    for b in range(8):
                        w = V("dn_conv_w", tap * 24 + first + b)
                        src, dst = raw[:, 8 * s + b, tap:tap + T1], conv[:, 8 * s + b, :]
                        if tap == 3:
                            ins = V_.tensor_scalar(dst, src, w, None, ALU.mult)
                        else:
                            ins = V_.scalar_tensor_tensor(out=dst, in0=src, scalar=w, in1=dst, op0=ALU.mult, op1=ALU.add)
                    if tap != 2:
                        link(ins)
                ins.then_inc(S("conv_done"), 1)
            dve.wait_ge(S("row_y"), 1)
            link(V_.tensor_scalar(rows[0:8, 5, :], rows[0:8, 1, :], -1.0, None, ALU.mult))
            link(V_.tensor_tensor(rows[0:8, 5, :], rows[0:8, 5, :], rows[0:8, 1, :], ALU.min))
            V_.tensor_scalar(rows[0:8, 1, :], rows[0:8, 1, :], 0.0, None, ALU.max).then_inc(S("row_abs"), 1)
            dve.wait_ge(S("row_ln"), 1)
            dve.wait_ge(S("row_abs"), 1)
            link(V_.tensor_tensor(rows[0:8, 1, :], rows[0:8, 1, :], rows[0:8, 5, :], ALU.add))
            link(V_.tensor_scalar(rows[0:8, 1, :], rows[0:8, 1, :], sd[0:8, 0:1], -1.0, ALU.mult, ALU.mult))
            link(V_.memset(rows[0:8, 5, :], 1.0))
            for c in range(2):
                t = slice(c * CH, (c + 1) * CH)
                ins = V_.tensor_tensor_scan(rows[0:8, 2, t], rows[0:8, 5, t], rows[0:8, 1, t], 0.0, ALU.mult, ALU.add)
            link(ins)
            V_.tensor_scalar(rows[0:8, 3, 0:CH], rows[0:8, 2, 0:CH], rows[0:8, 2, CH - 1:CH], -1.0, ALU.subtract, ALU.mult)\
                .then_inc(S("rows_g"), 1)
            dve.wait_ge(S("swapped"), 1)
            cosb, sinb = C("cos", T1), C("sin", T1)
            link(V_.tensor_tensor(qk, qkraw, over(cosb, 8), ALU.mult))
            for g in range(4):
                ins = V_.tensor_tensor(qkraw[:, 2 * g:2 * g + 2, :], bank[3 + g][:, :].rearrange("p (a b) -> p a b", a=2),
                                       over(sinb, 2), ALU.mult)
            link(ins)
            V_.tensor_tensor(qk, qk, qkraw, ALU.add).then_inc(S("qk_ready"), 1)
            dve.wait_ge(S("decay_loaded"), 16)
            for hd in range(H1):
                dve.wait_ge(S("ret_scores"), hd + 1)
                if hd >= 2:
                    dve.wait_ge(S("ret_out"), hd - 1)
                V_.tensor_tensor(sT[:, hd % 2, 0:256], bank[3 + hd % 2][:, 0:256], decay[:, hd, :], ALU.mult)
                V_.tensor_tensor(sT[:, hd % 2, 256:384], bank[3 + hd % 2][:, 256:384], decay[:, hd, 0:128], ALU.mult)\
                    .then_inc(S("ret_decayed"), 1)
            for g in range(4):
                dve.wait_ge(S("ret_sd"), g + 1)
                link(V_.reciprocal(rn2, rn2))
                for i in range(2):
                    hd = 2 * g + i
                    ins = V_.scalar_tensor_tensor(out=ro[:, hd, :], in0=bank[7][:, i * T1:(i + 1) * T1], scalar=V("ret_norm_g", hd),
                                                  in1=rn2[:, i * T1:(i + 1) * T1], op0=ALU.mult, op1=ALU.mult)
                ins.then_inc(S("ret_normed"), 1)
            dve.wait_ge(S("ret_normed"), 4)
            dve.wait_ge(S("proj_taken"), 44)
            V_.tensor_tensor(ro, ro, rgate, ALU.mult).then_inc(S("ret_gated"), 1)
            for s, sc in ((0, 1.0), (1, float(DN_SCALE))):
                for g in range(4):
                    n = 4 * s + g
                    dve.wait_ge(S("l2_sd"), n + 1)
                    link(V_.reciprocal(rn2, rn2))
                    cc = conv[:, 8 * s + 2 * g:8 * s + 2 * g + 2, :]
                    V_.scalar_tensor_tensor(out=cc, in0=cc, scalar=sc, in1=rn2.rearrange("p (a b) -> p a b", a=2),
                                            op0=ALU.mult, op1=ALU.mult).then_inc(S("l2_done"), 1)
            dve.wait_ge(S("rows_exp"), 1)
            V_.scalar_tensor_tensor(out=rows[0:8, 4, :], in0=rows[0:8, 4, :], scalar=-1.0, in1=rows[0:8, 0, :],
                                    op0=ALU.mult, op1=ALU.mult).then_inc(S("rows_ready"), 1)
            dve.wait_ge(S("cols_taken"), 1)
            idd = over(C("ident"), 4)
            for g in range(4):
                dve.wait_ge(S("dn_bcast"), g + 1)
                for i in range(2):
                    hd = 2 * g + i
                    for c in range(2):
                        ins = V_.tensor_scalar(Em[:, 2 * i + c, :], bank[2][:, i * T1 + c * P:i * T1 + (c + 1) * P],
                                               cols[:, 16 + 8 * c + hd:17 + 8 * c + hd], 0.0, ALU.subtract, ALU.min)
                ins.then_inc(S("dn_diff"), 1)
                dve.wait_ge(S("dn_exp"), g + 1)
                link(V_.tensor_tensor(Ea, Em, over(C("strict"), 4), ALU.mult))
                V_.tensor_tensor(Ea, Ea, bank[3][:, :].rearrange("p (a b) -> p a b", a=4), ALU.mult)
                link(V_.tensor_tensor(Em, Em, over(C("causal"), 4), ALU.mult))
                dve.wait_ge(S("dn_grams"), g + 1)
                V_.tensor_tensor(ATd, bank[4][:, :].rearrange("p (a b) -> p a b", a=4), Ea, ALU.mult).then_inc(S("dn_A"), 1)
                V_.tensor_tensor(attn, bank[5][:, :].rearrange("p (a b) -> p a b", a=4), Em, ALU.mult)
                V_.tensor_tensor(qd, conv[:, 8 + 2 * g:10 + 2 * g, CH:], eg, ALU.mult).then_inc(S("dn_e_ready"), 1)
                dve.wait_ge(S("dn_mask"), 7 * g + 1)
                V_.tensor_tensor(Ud, idd, AMd[:, 0], ALU.subtract)
                dve.wait_ge(S("dn_first"), g + 1)
                V_.tensor_tensor(Td, idd, bank[3][:, :].rearrange("p (a b) -> p a b", a=4), ALU.subtract).then_inc(S("dn_step"), 1)
                dve.wait_ge(S("dn_step"), 7 * g + 1)
                for l in range(1, LEVELS):
                    dve.wait_ge(S("dn_delta"), 6 * g + l)
                    if l < LEVELS - 1:
                        V_.tensor_tensor(Td, Td, bank[3][:, :].rearrange("p (a b) -> p a b", a=4), ALU.subtract)
                    V_.tensor_tensor(Ud, Ud, bank[4][:, :].rearrange("p (a b) -> p a b", a=4), ALU.subtract).then_inc(S("dn_step"), 1)
                    dve.wait_ge(S("dn_step"), 7 * g + 1 + l)
                dve.wait_ge(S("dn_sd"), g + 1)
                link(V_.reciprocal(rn2, rn2))
                for i in range(2):
                    hd = 2 * g + i
                    ins = V_.scalar_tensor_tensor(out=conv[:, 16 + hd, :], in0=bank[5][:, i * T1:(i + 1) * T1], scalar=V("dn_norm_g", 0),
                                                  in1=rn2[:, i * T1:(i + 1) * T1], op0=ALU.mult, op1=ALU.mult)
                ins.then_inc(S("dn_out"), 1)
            dve.wait_ge(S("dn_out"), 4)
            dve.wait_ge(S("proj_taken"), 52)
            V_.tensor_tensor(conv[:, 16:24, :], conv[:, 16:24, :], dz, ALU.mult).then_inc(S("dn_gated"), 1)
            dve.wait_ge(S("proj_taken"), 68 + 8)
            V_.tensor_tensor(gr, gr, u[:, :, 0:T1], ALU.mult)
            dve.wait_ge(S("proj_taken"), 68 + 16)
            link(V_.tensor_tensor(gd, gd, sq[:, :, 0:T1], ALU.mult))
            V_.tensor_tensor(gr, gr, gd, ALU.add).then_inc(S("merged"), 1)
            dve.wait_ge(S("proj_taken"), 68 + 24)
            V_.tensor_tensor(h[:, :, META:], h[:, :, META:], conv[:, 0:8, :], ALU.add).then_inc(S("h_ready"), 1)
            dve.wait_ge(S("h_ready"), 1)
            norm([u[:, t, 0:T1] for t in range(DT)], [h[:, t, META:] for t in range(DT)],
                 [V("g_ffn", t) for t in range(DT)], T1, "u_ready")
            V_.memset(up[:, :, 0:2], 0.0).then_inc(S("up_zeroed"), 1)
            for m in range(FT + 1):
                if m < FT:
                    s = 2 * (m % 2)
                    dve.wait_ge(S("proj_taken"), 92 + 2 * m + 2)
                    if m >= 2:
                        dve.wait_ge(S("up_silu"), m - 1)
                        dve.wait_ge(S("ffn_prod"), m - 1)
                    for tap in (2, 0, 1):
                        for j in range(2):
                            w = V("ffn_conv_w", tap * 44 + j * FT + m)
                            src, dst = up[:, s + j, tap:tap + T1], upc[:, s + j, :]
                            if tap == 2:
                                ins = V_.tensor_scalar(dst, src, w, V("ffn_conv_b", j * FT + m), ALU.mult, ALU.add)
                            else:
                                ins = V_.scalar_tensor_tensor(out=dst, in0=src, scalar=w, in1=dst, op0=ALU.mult, op1=ALU.add)
                        if tap != 1:
                            link(ins)
                    ins.then_inc(S("upc_ready"), 1)
                if m >= 1:
                    dve.wait_ge(S("up_silu"), m)
                    dve.wait_ge(S("upc_ready"), m)
                    s = 2 * ((m - 1) % 2)
                    V_.tensor_tensor(prod[:, m - 1, :], prod[:, m - 1, :], upc[:, s + 1, :], ALU.mult).then_inc(S("ffn_prod"), 1)
            n0 = 92 + 2 * FT
            dve.wait_ge(S("proj_taken"), n0 + 8)
            V_.tensor_tensor(h[:, :, META:], h[:, :, META:], down, ALU.add).then_inc(S("h_ready"), 1)
            dve.wait_ge(S("h_ready"), 2)
            norm([h[:, t, META:] for t in range(DT)], [h[:, t, META:] for t in range(DT)],
                 [V("g_final", t) for t in range(DT)], T1, "h_ready")

            norm([u[:, t, :] for t in range(DT)], [h[:, t, :] for t in range(DT)],
                 [V("norm_pre_2", t) for t in range(DT)], T2, None)
            V_.tensor_scalar(dx[:, :, 0:1], u[:, :, 0:1], -1.0, None, ALU.mult)
            link(V_.tensor_tensor(dx[:, :, 1:], u[:, :, 0:T2 - 1], u[:, :, 1:], ALU.subtract))
            for row, dst in ((4, xs_wa[:, 0]), (5, xs_wa[:, 1]), (1, xs[:, 0]), (0, xs[:, 1]), (2, xs[:, 2]), (3, xs[:, 3])):
                for t in range(DT):
                    ins = V_.scalar_tensor_tensor(out=dst[:, t, :], in0=dx[:, t, :], scalar=V("rwkv_mu_2", row * 8 + t),
                                                  in1=u[:, t, :], op0=ALU.mult, op1=ALU.add)
            ins.then_inc(S("lerped"), 1)
            link(V_.memset(S0, 0.0))
            p0 = n0 + 8 + 1
            for p in range(PAIRS):
                sg, a, k, r, v, g = [gin[:, p % 2, j, :] for j in range(6)]
                dve.wait_ge(S("proj_taken"), p0 + 6 * p + 6)
                link(V_.tensor_tensor_scan(cs, C("reset", T2), sg, 0.0, ALU.mult, ALU.add))
                V_.tensor_tensor(dd, cs, sg, ALU.subtract).then_inc(S("rw_cs"), 1)
                link(V_.tensor_scalar(kp, a, 1.0, V("rwkv_k_a_2", p), ALU.subtract, ALU.mult))
                link(V_.scalar_tensor_tensor(out=kp, in0=kp, scalar=1.0, in1=k, op0=ALU.add, op1=ALU.mult))
                dve.wait_ge(S("rw_kksd"), p + 1)
                link(V_.tensor_scalar(kkn, sdk, 1e-12, None, ALU.max))
                link(V_.reciprocal(kkn, kkn))
                link(V_.scalar_tensor_tensor(out=kkn, in0=k, scalar=V("rwkv_k_k_2", p), in1=kkn, op0=ALU.mult, op1=ALU.mult))
                dve.wait_ge(S("rw_w"), p + 1)
                V_.tensor_tensor(ar[:, 0, :], kkn, Wp, ALU.mult)
                V_.tensor_tensor(ar[:, 1, :], r, Wc, ALU.mult)
                V_.tensor_tensor(bk[:, 1, :], kp, Wi, ALU.mult)
                link(V_.tensor_tensor(bk[:, 0, :], kkn, a, ALU.mult))
                V_.tensor_tensor(bk[:, 0, :], bk[:, 0, :], Wi, ALU.mult)
                V_.scalar_tensor_tensor(out=tk, in0=r, scalar=V("rwkv_r_k_2", p), in1=kp, op0=ALU.mult, op1=ALU.mult)\
                    .then_inc(S("rw_feats"), 1)
                for c in range(NRC):
                    dve.wait_ge(S("rw_grams"), 4 * p + c + 1)
                    for j in range(2):
                        ins = V_.tensor_tensor(GG[0:RC, c, j, :], bank[3 + j][0:RC, 0:4 * RC], C("mask_bk", 4 * RC, RC), ALU.mult)
                    ins.then_inc(S("rw_grams_taken"), 1)
                idr = over(C("ident", RC, RC), 8)
                dve.wait_ge(S("rw_mask"), 7 * p + 1)
                V_.tensor_tensor(Ur[0:RC], idr, AMr[0:RC], ALU.subtract)
                dve.wait_ge(S("rw_first"), p + 1)
                for q in range(2):
                    ins = V_.tensor_tensor(Tr[0:RC, 4 * q:4 * q + 4], idr[:, 0:4], bank[5 + q][0:RC, 0:4 * RC].rearrange("p (a b) -> p a b", a=4), ALU.subtract)
                ins.then_inc(S("rw_step"), 1)
                dve.wait_ge(S("rw_step"), 7 * p + 1)
                for l in range(1, LEVELS):
                    dve.wait_ge(S("rw_delta"), 6 * p + l)
                    for M, b in (((Tr, 5), (Ur, 3)) if l < LEVELS - 1 else ((Ur, 3),)):
                        for q in range(2):
                            m4 = M[0:RC, 4 * q:4 * q + 4]
                            ins = V_.tensor_tensor(m4, m4, bank[b + q][0:RC, 0:4 * RC].rearrange("p (a b) -> p a b", a=4), ALU.subtract)
                    ins.then_inc(S("rw_step"), 1)
                    dve.wait_ge(S("rw_step"), 7 * p + 1 + l)
                for c in range(NRC - 1):
                    dve.wait_ge(S("rw_state"), 3 * p + c + 1)
                    end = (c + 1) * RC - 1
                    for j in range(2):
                        r2 = slice(64 * j, 64 * j + 64)
                        if c == 0:
                            pass
                        else:
                            ins = V_.tensor_tensor(S0[r2, r2], S0[r2, r2], bank[3][r2, r2], ALU.add)
                    if c > 0:
                        link(ins)
                    for j in range(2):
                        r2 = slice(64 * j, 64 * j + 64)
                        src = bank[3] if c == 0 else S0
                        ins = V_.tensor_scalar(S0[r2, r2], src[r2, r2], Wc[r2, end:end + 1], None, ALU.mult)
                    ins.then_inc(S("rw_state_taken"), 1)
                    dve.wait_ge(S("rw_state_taken"), 3 * p + c + 1)
                dve.wait_ge(S("rw_sd"), p + 1)
                link(V_.reciprocal(sdk, sdk))
                link(V_.scalar_tensor_tensor(out=kkn, in0=bank[3][:, 0:T2], scalar=V("rwkv_ln_w_2", p), in1=sdk, op0=ALU.mult, op1=ALU.mult))
                link(V_.tensor_tensor(kp, bon, v, ALU.mult))
                link(V_.scalar_tensor_tensor(out=kp, in0=kkn, scalar=V("rwkv_ln_b_2", p), in1=kp, op0=ALU.add, op1=ALU.add))
                V_.tensor_tensor(yo[:, p, :], kp, g, ALU.mult).then_inc(S("rw_pair_done"), 1)
            n1 = p0 + 6 * PAIRS

            def post(layer, out_signal):
                norm([mo[:, t, :] for t in range(DT)], [mo[:, t, :] for t in range(DT)],
                     [V("norm_post_2", 8 * layer + t) for t in range(DT)], T2, None)
                V_.tensor_tensor(h[:, :, :], h[:, :, :], mo, ALU.add).then_inc(S(out_signal), 1)

            post(0, "h_ready")
            dve.wait_ge(S("h_ready"), 4)
            norm([u[:, t, :] for t in range(DT)], [h[:, t, :] for t in range(DT)],
                 [V("norm_pre_2", 8 + t) for t in range(DT)], T2, "u_ready")
            norm([cqn[:, t, :] for t in range(4)], [cq[:, t, :] for t in range(4)],
                 [V("mla_q_norm_2", t) for t in range(4)], T2, "cq_done")
            norm([ckvn[:, t, :] for t in range(2)], [ckv[:, t, :] for t in range(2)],
                 [V("mla_kv_norm_2", t) for t in range(2)], T2, "lat_ready")
            cosb, sinb = C("cos", T2), C("sin", T2)
            dve.wait_ge(S("kr_swapped"), 1)
            link(V_.tensor_tensor(kr[:, 1, :], kr[:, 0, :], cosb, ALU.mult))
            link(V_.tensor_tensor(kr[:, 0, :], bank[3][:, 0:T2], sinb, ALU.mult))
            V_.tensor_tensor(kr[:, 1, :], kr[:, 1, :], kr[:, 0, :], ALU.add).then_inc(S("kr_ready"), 1)

            def rotate_q(hd):
                q = qr[:, (hd // 2) % 2]
                dve.wait_ge(S("qr_swapped"), hd // 2 + 1)
                link(V_.tensor_tensor(q[:, 1, :], q[:, 0, :], cosb, ALU.mult))
                link(V_.tensor_tensor(q[:, 0, :], bank[2][:, 0:T2], sinb, ALU.mult))
                V_.tensor_tensor(q[:, 2, :], q[:, 1, :], q[:, 0, :], ALU.add).then_inc(S("qr_ready"), 1)

            rotate_q(0)
            for hd in range(AH):
                pb = hd % 2
                if hd >= 1 and hd + 1 < AH and (hd + 1) % 2 == 0:
                    pass
                dve.wait_ge(S("at_scores"), hd + 1)
                if hd >= 2:
                    dve.wait_ge(S("at_pT"), hd - 1)
                V_.tensor_tensor(pr[:, pb, :], bank[3][:, 0:384], C("amask", 384), ALU.add)
                V_.tensor_tensor(pr2[0:META, pb, :], bank[4][0:META, 0:T2], C("amask2", T2, META), ALU.add).then_inc(S("at_masked"), 1)
                dve.wait_ge(S("at_masked"), hd + 1)
                V_.reduce_max(nm[:, pb, 0:1], pr[:, pb, 0:128], axis=AX_X)
                V_.reduce_max(nm[:, pb, 1:2], pr[:, pb, 128:384], axis=AX_X)
                link(V_.reduce_max(nm[0:META, pb, 2:3], pr2[0:META, pb, :], axis=AX_X))
                V_.tensor_scalar(nm[:, pb, 3:5], nm[:, pb, 0:2], -SCALE_A, None, ALU.mult)
                V_.tensor_scalar(nm[0:META, pb, 5:6], nm[0:META, pb, 2:3], -SCALE_A, None, ALU.mult).then_inc(S("at_max"), 1)
                dve.wait_ge(S("at_exp"), hd + 1)
                V_.reciprocal(nm[:, pb, 9:11], nm[:, pb, 6:8])
                link(V_.reciprocal(nm[0:META, pb, 11:12], nm[0:META, pb, 8:9]))
                V_.tensor_scalar(pr[:, pb, 0:128], pr[:, pb, 0:128], nm[:, pb, 9:10], None, ALU.mult)
                V_.tensor_scalar(pr[:, pb, 128:384], pr[:, pb, 128:384], nm[:, pb, 10:11], None, ALU.mult)
                V_.tensor_scalar(pr2[0:META, pb, :], pr2[0:META, pb, :], nm[0:META, pb, 11:12], None, ALU.mult).then_inc(S("at_probs"), 1)
                if hd + 1 < AH and (hd + 1) % 2 == 0:
                    rotate_q(hd + 1)
                dve.wait_ge(S("at_o"), hd + 1)
                V_.tensor_tensor(om[:, hd, :], bank[7][:, 0:T2], hin[:, pb, 2, :], ALU.mult).then_inc(S("at_o_taken"), 1)
            post(1, "out_ready")

        @block.gpsimd
        def _(pool):
            for g in range(4):
                pool.wait_ge(S("dn_A"), g + 1)
                for l in range(LEVELS):
                    if l >= 2:
                        pool.wait_ge(S("dn_y"), 6 * g + l - 2) if l >= 3 else pool.wait_ge(S("dn_step"), 7 * g + 1)
                    elif g >= 1:
                        pool.wait_ge(S("dn_out"), g)
                    nc.gpsimd.tensor_tensor(AMd[:, l % 2], ATd, over(levels[:, l, :], 4), ALU.mult).then_inc(S("dn_mask"), 1)
            for p in range(PAIRS):
                pool.wait_ge(S("rw_grams_taken"), 4 * p + 4)
                for l in range(LEVELS):
                    if l >= 2:
                        pool.wait_ge(S("rw_y"), 6 * p + l - 2) if l >= 3 else pool.wait_ge(S("rw_step"), 7 * p + 1)
                    nc.gpsimd.tensor_tensor((AMr, AMr2)[l % 2][0:RC], GG[0:RC, :, :, 0:RC].rearrange("p c j t -> p (c j) t"),
                                            over(levels[0:RC, l, 0:RC], 8), ALU.mult).then_inc(S("rw_mask"), 1)


DN_SCALE = 128 ** -0.5


def gemm_sizes():
    n = [DT] * 8 + [0, 4 * DT] * 2 + [DT] * 56 + [DT] * 24 + [DT] * (2 * FT) + [FT] * 8
    n += [DT]
    for p in range(PAIRS):
        n += [0, 0, DT, DT, DT, DT]
    n += [IT] * 8 + [DT] * 7 + [0, 0, 8] * 4
    for hd in range(AH):
        n += ([4] if hd % 2 == 0 else []) + [4, 2, DT]
    return n + [IT] * 8


def gemm_signal_ids():
    return [i + 1 for i in range(len(gemm_sizes()))]


def kernel(**inputs):
    import concourse.bacc as _bacc
    from concourse.bass_utils import run_bass_kernel_spmd as _run

    a = {k: np.asarray(v) for k, v in inputs.items()}
    two = {k: (v[0] if v.ndim == 3 else v) for k, v in a.items()}
    stream = np.zeros((NCHUNKS, P, CB, P), np.float32)
    for b, (w, r0, pieces) in enumerate(weight_order()):
        at = 0
        for c0, n in pieces:
            stream[b // CB, :, b % CB, at:at + n] = two[w][r0:r0 + P, c0:c0 + n]
            at += n
    vecs = np.zeros((P, NVEC), np.float32)
    for name, n in VECTORS:
        if name == "a_log":
            vecs[:H1, VOFF[name]] = a["dn_a_log"].reshape(-1)
        elif name == "dt_bias":
            vecs[:H1, VOFF[name]] = a["dn_dt_bias"].reshape(-1)
        else:
            vecs[:, VOFF[name]:VOFF[name] + n] = a[name].reshape(n, P).T
    consts = np.concatenate([v.astype(np.float32) for v in CONST.values()], axis=1)
    arrays = {
        "xT": a["x"].reshape(T1, DT, P).transpose(2, 1, 0),
        "metaT": a["meta_tokens_2"].reshape(META, DT, P).transpose(2, 1, 0),
        "wstream": stream.reshape(NCHUNKS, P, CB * P),
        "vecs": vecs,
        "consts": consts,
        "decays": decay_table(),
        "wdbda": two["w_in"][:, O_DB:O_DB + 16].reshape(DT, P, 16).transpose(1, 0, 2).reshape(P, DT * 16),
        "wlora": np.concatenate([a["rwkv_w2_2"][0], a["rwkv_a2_2"][0]], axis=0),
    }
    arrays = {k: np.ascontiguousarray(v) for k, v in arrays.items()}
    nc = _bacc.Bacc("TRN2", target_bir_lowering=False, num_devices=1, dynamic_dma_scratch_size=1024)
    args = [nc.dram_tensor(k, v.shape, F32, kind="ExternalInput").ap() for k, v in arrays.items()]
    out = nc.dram_tensor("outT", (P, DT, T1), F32, kind="ExternalOutput").ap()
    build(nc, *args, out)
    r = _run(nc, [arrays], core_ids=[0])
    got = np.asarray(r.results[0]["outT"])
    return np.ascontiguousarray(got.transpose(2, 1, 0).reshape(1, T1, D))
```

```python
from contextlib import ExitStack

import numpy as np

import concourse.bass as bass
from concourse import mybir

F32 = mybir.dt.float32
ALU = mybir.AluOpType
ACT = mybir.ActivationFunctionType
AX_X = mybir.AxisListType.X

P = 128
D = 1024
DT = D // P
T1 = 256
META = 16
T2 = T1 + META
H1 = 8
CH = 128
DFF = 2816
FT = DFF // P
RH = 32
RN = 64
PAIRS = RH // 2
RCH = [(0, META), (META, CH), (META + CH, CH)]
INNER = 2048
IT = INNER // P
AH = 16
LEVELS = 7
EPS = 1e-6
GN_EPS = 1e-5
GN_EPS_2 = 64e-5
DECAY_C = float(np.exp(-0.5))
SCALE_A = float(192 ** -0.5)

ARENA = 31860
CB = 16
SLOTS = 6

SPLITS = (512, 512, 1024, 1024, 1024, 1024, 1024, 1024, 8, 8, 1024, 1024)
OFF = [int(v) for v in np.cumsum((0,) + SPLITS)]
O_RQ, O_RK, O_RV, O_RG, O_DQ, O_DK, O_DV, O_DZ, O_DB, O_DA, O_GR, O_GD = OFF[:12]
RW_G, RW_WLO = 3 * INNER, 4 * INNER
MLA_CKV, MLA_ROPE, MLA_G = 512, 768, 832


def weight_order():
    def tile(w, k, m, off=0):
        return (w, k * P, [(off + m * P, P)])

    def outs(w, off, ms, kt):
        return [tile(w, k, m, off) for m in ms for k in range(kt)]

    def wide(w, k, off):
        return [(w, k * P, [(off + j * P, P)]) for j in range(4)]

    order = []
    for off, n in ((O_RQ, 4), (O_RK, 4)):
        order += outs("w_in", off, range(n), DT)
    for g in range(2):
        for k in range(DT):
            order += wide("w_in", k, O_RV + 512 * g)
    for off in (O_DK, O_DQ, O_DV, O_RG, O_DZ, O_GR, O_GD):
        order += outs("w_in", off, range(8), DT)
    order += outs("w_ret_br", 0, range(8), DT)
    order += outs("w_dn_br", 0, range(8), DT)
    order += outs("w_o", 0, range(8), DT)
    for m in range(FT):
        order += outs("w_up", 0, [m], DT) + outs("w_up", DFF, [m], DT)
    order += outs("w_down", 0, range(8), FT)
    order += [("rwkv_w_in_2", k * P, [(RW_WLO, P)]) for k in range(DT)]
    for p in range(PAIRS):
        for off in (INNER, 0, 2 * INNER, RW_G):
            order += outs("rwkv_w_in_2", off, [p], DT)
    order += outs("rwkv_w_out_2", 0, range(8), IT)
    order += outs("mla_w_in_2", 0, range(4), DT) + outs("mla_w_in_2", MLA_CKV, range(2), DT)
    order += [("mla_w_in_2", k * P, [(MLA_ROPE, 64), (MLA_ROPE, 64)]) for k in range(DT)]
    for g in range(4):
        for k in range(2):
            order += [("mla_w_kv_up_2", k * P, [((4 * g + j) * 256 + 128, P)]) for j in range(4)]
    for h in range(AH):
        if h % 2 == 0:
            order += [("mla_w_q_up_2", k * P, [(h * 192 + 128, 64), (h * 192 + 320, 64)]) for k in range(4)]
        order += [("mla_w_q_up_2", k * P, [(h * 192, P)]) for k in range(4)]
        order += [("mla_w_kv_up_2", k * P, [(h * 256, P)]) for k in range(2)]
        order += outs("mla_w_in_2", MLA_G, [h], DT)
    order += outs("mla_w_out_2", 0, range(8), IT)
    return order


R_K, R_W, R_A, R_KK, R_R, R_V, R_BONUS, R_G = range(8)
RW_OUTS = (8, 1, 1, 1, 8, 8, 1, 8)
RW_AHEAD = 8 + 1 + 1 + 1 + 8 + 3
FILL = {"start1": 2, "start2": 3, "bonus": 1, "grams": 4, "gram0": 4, "first": 4, "y1": 1, "delta1": 2, "y2": 1, "delta2": 2,
        "y3": 0, "delta3": 3, "y4": 1, "delta4": 2, "y5": 1, "delta5": 2, "y6": 1, "delta6": 2}
assert sum(FILL.values()) == sum(RW_OUTS), sum(FILL.values())


def fill_end(p, slot):
    names = list(FILL)
    n = RW_AHEAD + sum(RW_OUTS) * p + sum(FILL[x] for x in names[:names.index(slot) + 1])
    return min(n, sum(RW_OUTS) * PAIRS)


def outs_at(n):
    q, r = divmod(n, sum(RW_OUTS))
    return 8 * q + sum(1 for i in range(8) if sum(RW_OUTS[:i + 1]) <= r)


NBLOCKS = len(weight_order())
NCHUNKS = -(-NBLOCKS // CB)

VECTORS = [("g_mix", 8), ("ret_norm_g", 8), ("dn_conv_w", 96), ("dn_norm_g", 1), ("g_ffn", 8),
           ("ffn_conv_w", 132), ("ffn_conv_b", 44), ("g_final", 8), ("norm_pre_2", 16), ("norm_post_2", 16),
           ("rwkv_mu_2", 48), ("rwkv_w0_2", 16), ("rwkv_a0_2", 16), ("rwkv_k_k_2", 16), ("rwkv_k_a_2", 16),
           ("rwkv_r_k_2", 16), ("rwkv_ln_w_2", 16), ("rwkv_ln_b_2", 16), ("mla_q_norm_2", 4),
           ("mla_kv_norm_2", 2), ("a_log", 1), ("dt_bias", 1)]
VOFF, _at = {}, 0
for _name, _n in VECTORS:
    VOFF[_name] = _at
    _at += _n
NVEC = _at


def constants():
    f = np.float32
    i, j = np.arange(P)[None, :], np.arange(P)[:, None]
    out = {"ident": np.eye(P), "ones": np.ones((P, P)), "mean128": np.full((P, P), 1 / 128)}
    out["center128"] = np.eye(P) - 1 / 128
    half = (i // 64) == (j // 64)
    out["ones64"] = half * 1.0
    out["mean64"] = half / 64
    out["center64"] = np.eye(P) - half / 64
    out["perm"] = ((i ^ 32) == j) * 1.0
    out["strict"] = (i > j) * 1.0
    out["causal"] = (i >= j) * 1.0
    lv = np.zeros((LEVELS, P, P))
    for l in range(LEVELS):
        s = 1 << l
        lv[l] = ((i // s) % 2 == 1) & ((j // s) == (i // s) - 1)
    out["levels"] = lv.transpose(1, 0, 2).reshape(P, -1)
    sel = np.zeros((P, H1, P))
    for h in range(H1):
        sel[h, h] = 1
    out["sel"] = sel.reshape(P, -1)
    for name, n in (("mask_rw", P), ("mask_rw0", META)):
        m = np.zeros((P, 4, n))
        m[:n, 0] = m[:n, 2] = (i > j)[:n, :n]
        m[:n, 3] = (i >= j)[:n, :n]
        m[:, 1] = -m[:, 3]
        out[name] = m.reshape(P, -1)
    starts = [t for t, _ in RCH]
    out["reset"] = np.broadcast_to(~np.isin(np.arange(T2), starts) * 1.0, (P, T2))
    out["eps"] = np.broadcast_to(np.array([EPS, GN_EPS, GN_EPS_2]), (P, 3))
    inv = (f(10000.0) ** (-np.arange(0, 64, 2, dtype=f) / f(64))).astype(f)
    lane = np.arange(P) % 64
    ang = (np.arange(T2, dtype=f)[None, :] * inv[lane % 32][:, None]).astype(f).astype(np.float64)
    sign = np.where(lane < 32, -1.0, 1.0)[:, None]
    out["cos"], out["sin"] = np.cos(ang), np.sin(ang) * sign
    neg = -3.0e38
    m = np.zeros((P, 384))
    m[:, 0:128] = np.where(j >= i, 0, neg)
    m[:, 256:384] = m[:, 0:128]
    out["amask"] = m
    m = np.zeros((P, T2))
    m[:META, 256:] = np.where(j >= i, 0, neg)[:META, :META]
    out["amask2"] = m
    return out


def decay_table():
    g = 1.0 - 2.0 ** (-5.0 - np.arange(H1, dtype=np.float32))
    lg = np.log(g.astype(np.float64))
    d = np.arange(T1)[None, :] - np.arange(P)[:, None]
    t = np.where(d >= 0, np.exp(lg[:, None, None] * np.maximum(d, 0)), 0) * 0.125
    return t.transpose(1, 0, 2).reshape(P, -1).astype(np.float32)


CONST = constants()
COFF, _at = {}, 0
for _name, _v in CONST.items():
    COFF[_name] = _at
    _at += _v.shape[1]
NCONST = _at


def build(nc, xT, metaT, wstream, vecs, consts, decays, wdbda, wlora, outT):
    ctx = ExitStack()
    with ctx:
        def sb(name, shape):
            return ctx.enter_context(nc.sbuf_tensor(name, shape, F32))

        sems = {}

        def S(name):
            if name not in sems:
                sems[name] = ctx.enter_context(nc.semaphore(name))
            return sems[name]

        loaded = [S(f"weights_loaded{i}") for i in range(SLOTS)]

        ring = sb("ring", [P, SLOTS * CB * P])
        h = sb("h", [P, DT, T2])
        u = sb("u", [P, DT, T2])
        vec = sb("vec", [P, NVEC])
        con = sb("con", [P, NCONST])
        sq = sb("sq", [P, DT, T2])
        sd = sb("sd", [P, T2])
        rs = sb("rs", [P, T2])
        arena = sb("arena", [P, ARENA])
        taken = [0]

        def area(at, *dims):
            n = int(np.prod(dims))
            assert at + n <= ARENA, (at, n)
            v = arena[:, at:at + n]
            if len(dims) == 2:
                v = v.rearrange("p (a b) -> p a b", a=dims[0])
            elif len(dims) == 3:
                v = v.rearrange("p (a b c) -> p a b c", a=dims[0], b=dims[1])
            elif len(dims) == 4:
                v = v.rearrange("p (a b c d) -> p a b c d", a=dims[0], b=dims[1], c=dims[2])
            taken[0] = at + n
            return v

        raw = area(0, 24, T1 + 3)
        dz, gr, gd = area(0, 8, T1), area(2048, 8, T1), area(4096, 8, T1)
        conv = area(6216, 24, T1)
        qkraw = area(taken[0], 8, T1)
        ro = qkraw
        qk = area(taken[0], 8, T1)
        vtok = area(taken[0], 2, D)
        rgate = area(taken[0], 8, T1)
        sT = area(taken[0], 2, 384)
        rn2 = area(taken[0], 512)
        sq2 = area(taken[0], 512)
        decay = area(taken[0], 8, T1)
        wdb = area(taken[0], 8, 16)
        rows = area(taken[0], 6, T1)
        cols = area(taken[0], 48)
        base = 6216 + 6144 + 2048
        Em = area(base, 4, P)
        Ea = area(taken[0], 4, P)
        ATd = area(taken[0], 4, P)
        attn = area(taken[0], 4, P)
        Td = area(taken[0], 4, P)
        Ud = area(taken[0], 4, P)
        Yd = area(taken[0], 4, P)
        vb = area(taken[0], 4, P)
        at_decay = 6216 + 6144 + 2048 * 4 + 768 + 1024
        AMd = area(at_decay, 2, 4, P)
        kbg = area(taken[0], 2, P)
        kdec = area(taken[0], 2, P)
        eg = area(taken[0], 2, P)
        qd = area(taken[0], 2, P)
        w1T = area(6216 + 6144 + 2048 * 4, 2, P)
        vn0 = area(taken[0], 2, P)
        S1 = area(taken[0], 2, P)
        vn1 = Em[:, 0:2, :]
        up = area(0, 4, T1 + 2)
        upc = area(1040, 4, T1)
        prod = area(2064, FT, T1)
        down = area(taken[0], 8, T1)
        xs = area(0, 4, DT, T2)
        dx = area(8704, DT, T2)
        xs_wa = area(8704 + 2176, 2, DT, T2)
        yo = area(8704, PAIRS, T2)
        cs, dd, Wc, kk2, sdk, kp = [area(13056 + i * T2, T2) for i in range(6)]
        Wi, Wp, tk, kkn = cs, dd, kk2, sdk
        bonv = area(14688, 3, T2)
        lo = area(taken[0], T2)
        gin = area(taken[0], 2, 5, T2)
        gate = area(taken[0], 3, T2)
        wl = area(taken[0], INNER)
        ar = area(taken[0], 2, 2, T2)
        bk = area(taken[0], 2, T2)
        GG = area(taken[0], 2, 4, 4 * P)
        G0 = area(taken[0], 2, 2, 4 * META)
        tok = area(taken[0], 2, 3, 3, P)
        sqr, sdn = rs[:, :], sd[:, :]
        mids, fcol = area(taken[0], 2), area(taken[0], 3, 2)
        sqf = sq[:, :, :].rearrange("p a b -> p (a b)")
        uf = u[:, :, :].rearrange("p a b -> p (a b)")

        def four(flat, at):
            return flat[:, at:at + 4 * P].rearrange("p (a b) -> p a b", a=4)

        Ur = [four(uf, 0), four(uf, 512)]
        Tr = four(uf, 1024)
        Yr = [four(uf, 1536), four(sqf, 0)]
        AMr = [four(sqf, 512), four(sqf, 1024)]
        Zs, nSA = sqf[:, 1536:1664], sqf[:, 1664:1792]
        S0 = uf[:, 2048:2176]
        ys = sqf[:, 1792:1792 + T2]
        half_bias = sqf[:, 2064:2064 + 2 * PAIRS]
        gtanh = area(taken[0], T2)
        T0, Y0, = [area(taken[0], 2, META) for _ in range(2)]
        U0 = [area(taken[0], 2, META) for _ in range(2)]
        AM0 = [area(taken[0], 2, META) for _ in range(2)]
        cq = area(0, 4, T2)
        ckv = area(taken[0], 2, T2)
        cqn = area(taken[0], 4, T2)
        ckvn = area(taken[0], 2, T2)
        kr = area(taken[0], 2, T2)
        vt = area(taken[0], 3, INNER)
        om = area(taken[0], AH, T2)
        qr = area(taken[0], 2, 3, T2)
        hin = area(taken[0], 2, 3, T2)
        pr = area(taken[0], 2, 384)
        pr2 = area(taken[0], 2, T2)
        pT = area(taken[0], 2, 432)
        nm = area(taken[0], 2, 12)
        atanh = area(22200, T2)
        mo = area(20000, DT, T2)

        bank = [ctx.enter_context(nc.psum_tensor(f"bank{i}", [P, 512], F32)) for i in range(8)]

        def C(name, n=P, rows_=P):
            return con[0:rows_, COFF[name]:COFF[name] + n]

        def V(name, t, rows_=P):
            return vec[0:rows_, VOFF[name] + t:VOFF[name] + t + 1]

        def eps_col(i):
            return con[:, COFF["eps"] + i:COFF["eps"] + i + 1]

        levels = con[:, COFF["levels"]:COFF["levels"] + LEVELS * P].rearrange("p (l n) -> p l n", l=LEVELS)
        sel = con[:, COFF["sel"]:COFF["sel"] + H1 * P].rearrange("p (l n) -> p l n", l=H1)

        def parts(ap, l, odd):
            return ap.rearrange("p m (b e s) -> p m b e s", e=2, s=1 << l)[:, :, :, odd, :]

        def packed(ap, l):
            return ap.rearrange("p (m b s) -> p m b s", m=4, s=1 << l)

        def over(ap, n):
            r, c = ap.shape
            return ap.unsqueeze(1).to_broadcast([r, n, c])

        block = ctx.enter_context(nc.Block())

        outputs = gemm_sizes()
        starts = np.cumsum([0] + outputs)
        assert starts[-1] == NBLOCKS, (starts[-1], NBLOCKS)
        last_reader = [int(np.searchsorted(starts, min((c + 1) * CB, NBLOCKS), side="left")) for c in range(NCHUNKS)]
        BLOCK_STARTS = starts
        
        @block.sync
        def _(sp):
            sp.dma_start(h[:, :, META:], xT).then_inc(S("x_loaded"), 16)
            sp.dma_start(vec[:, :], vecs).then_inc(S("vec_loaded"), 16)
            sp.dma_start(con[:, :], consts).then_inc(S("con_loaded"), 16)
            for c in range(NCHUNKS):
                if c >= SLOTS:
                    sp.wait_ge(S("proj_done"), last_reader[c - SLOTS])
                sp.dma_start(ring[:, (c % SLOTS) * CB * P:(c % SLOTS + 1) * CB * P], wstream[c])\
                  .then_inc(loaded[c % SLOTS], 16)
                if c == 1:
                    sp.dma_start(decay, decays.rearrange("p (a b) -> p a b", a=8)).then_inc(S("decay_loaded"), 16)
                    sp.dma_start(wdb, wdbda.rearrange("p (a b) -> p a b", a=8)).then_inc(S("wdb_loaded"), 16)
            sp.wait_ge(S("out_ready"), 1)
            sp.dma_start(outT, h[:, :, META:]).then_inc(S("out_stored"), 16)
            sp.wait_ge(S("out_stored"), 16)

        @block.tensor
        def _(pe):
            blk = [0]
            pn = [0]
            seen = [-1]

            def weights(width=1):
                b = blk[0]
                c = b // CB
                if c > seen[0]:
                    seen[0] = c
                    pe.wait_ge(loaded[c % SLOTS], 16 * (c // SLOTS + 1))
                at = (b % (CB * SLOTS)) * P
                blk[0] += width
                return ring[:, at:at + width * P]

            def free_bank():
                if pn[0] >= 2:
                    pe.wait_ge(S("proj_taken"), pn[0] - 1)
                b = bank[pn[0] % 2]
                pn[0] += 1
                return b

            def project(rhs, kt, T):
                b = free_bank()
                for k in range(kt):
                    ins = nc.tensor.matmul(b[:, 0:T], weights(), rhs(k), start=k == 0, stop=k == kt - 1)
                ins.then_inc(S("proj_done"), 1)

            def project_tokens(lhs, kt, spans):
                b0 = blk[0]
                for t, (a, n) in enumerate(spans):
                    blk[0] = b0
                    b = free_bank()
                    for k in range(kt):
                        ins = nc.tensor.matmul(b[0:n, :], lhs(k)[:, a:a + n], weights(4), start=k == 0, stop=k == kt - 1)
                    ins.then_inc(S("proj_done"), 1)

            norm_n = [0]

            def norm(nt, T):
                norm_n[0] += 1
                pe.wait_ge(S("norm_sq"), norm_n[0])
                for t in range(nt):
                    ins = nc.tensor.matmul(bank[2][:, 0:T], C("ones"), sq[:, t, 0:T], start=t == 0, stop=t == nt - 1)
                ins.then_inc(S("norm_sum"), 1)

            pe.wait_ge(S("con_loaded"), 16)
            norm(DT, T1)
            pe.wait_ge(S("u_ready"), 1)
            uT = lambda k: u[:, k, 0:T1]
            for _m in range(8):
                project(uT, DT, T1)
            for _g in range(2):
                project_tokens(uT, DT, [(0, P), (P, P)])
            for _m in range(24):
                project(uT, DT, T1)
            pe.wait_ge(S("wdb_loaded"), 16)
            for j in range(2):
                for k in range(DT):
                    ins = nc.tensor.matmul(bank[2][0:8, j * T1:(j + 1) * T1], wdb[:, k, 8 * j:8 * j + 8], uT(k),
                                           start=k == 0, stop=k == DT - 1)
            ins.then_inc(S("dbda_done"), 1)
            for _m in range(8):
                project(uT, DT, T1)
            pe.wait_ge(S("proj_taken"), 8)
            for b in range(8):
                ins = nc.tensor.matmul(bank[3 + b // 2][:, (b % 2) * T1:(b % 2 + 1) * T1], C("perm"), qkraw[:, b, :],
                                       start=True, stop=True)
            ins.then_inc(S("swapped"), 1)
            pe.wait_ge(S("qk_ready"), 1)

            def ret_scores(hd):
                r = slice(64 * (hd % 2), 64 * (hd % 2) + 64)
                q, k = qk[r, hd // 2, :], qk[r, 4 + hd // 2, :]
                if hd >= 2:
                    pe.wait_ge(S("ret_decayed"), hd - 1)
                nc.tensor.matmul(bank[3 + hd % 2][:, 0:256], k[:, 0:128], q, start=True, stop=True)
                nc.tensor.matmul(bank[3 + hd % 2][:, 256:384], k[:, 128:256], q[:, 128:256], start=True, stop=True)\
                    .then_inc(S("ret_scores"), 1)

            ret_scores(0)
            for hd in range(H1):
                if hd + 1 < H1:
                    ret_scores(hd + 1)
                pe.wait_ge(S("ret_decayed"), hd + 1)
                if hd >= 2:
                    pe.wait_ge(S("ret_out_taken"), hd - 1)
                o = bank[5 + hd % 2]
                nc.tensor.matmul(o[:, 0:256], vtok[:, 0, hd * P:(hd + 1) * P], sT[:, hd % 2, 0:256], start=True, stop=False)
                nc.tensor.matmul(o[:, 128:256], vtok[:, 1, hd * P:(hd + 1) * P], sT[:, hd % 2, 256:384], start=False, stop=True)\
                    .then_inc(S("ret_out"), 1)
            for g in range(4):
                pe.wait_ge(S("ret_out_taken"), 2 * g + 2)
                if g >= 1:
                    pe.wait_ge(S("ret_normed"), g)
                nc.tensor.matmul(bank[7][:, :], C("center128"), ro[:, 2 * g:2 * g + 2, :], start=True, stop=True)\
                    .then_inc(S("ret_centered"), 1)
                pe.wait_ge(S("ret_sq"), g + 1)
                nc.tensor.matmul(bank[2][:, :], C("mean128"), sq2, start=True, stop=True).then_inc(S("ret_var"), 1)

            for _m in range(24):
                project(uT, DT, T1)

            for n in range(8):
                pe.wait_ge(S("l2_sq"), n + 1)
                nc.tensor.matmul(bank[3][:, :], C("ones"), sq2, start=True, stop=True).then_inc(S("l2_sum"), 1)
            pe.wait_ge(S("rows_ready"), 1)
            for j, (r, c) in enumerate(((0, 0), (0, 1), (2, 0), (2, 1), (3, 0), (4, 1))):
                ins = nc.tensor.matmul(bank[3][:, 8 * j:8 * j + 8], rows[0:8, r, c * CH:(c + 1) * CH], C("ident", 8, 8),
                                       start=True, stop=True)
            ins.then_inc(S("cols_done"), 1)
            pe.wait_ge(S("l2_done"), 8)
            for g in range(4):
                hs = (2 * g, 2 * g + 1)
                if g >= 1:
                    pe.wait_ge(S("dn_out"), g)
                else:
                    pe.wait_ge(S("cols_taken"), 1)
                for i, hd in enumerate(hs):
                    nc.tensor.matmul(bank[2][:, i * T1:(i + 1) * T1], sel[0:8, hd, :], rows[0:8, 2, :], start=True, stop=True)
                for i, hd in enumerate(hs):
                    ins = nc.tensor.matmul(bank[3][:, i * T1:(i + 1) * T1], sel[0:8, hd, :], rows[0:8, 0, :], start=True, stop=True)
                ins.then_inc(S("dn_bcast"), 1)
                for i, hd in enumerate(hs):
                    for c in range(2):
                        m, t = 2 * i + c, slice(c * CH, (c + 1) * CH)
                        nc.tensor.matmul(bank[4][:, m * P:(m + 1) * P], conv[:, hd, t], conv[:, hd, t], start=True, stop=True)
                        nc.tensor.matmul(bank[5][:, m * P:(m + 1) * P], conv[:, hd, t], conv[:, 8 + hd, t], start=True, stop=True)
                        nc.tensor.matmul(bank[6][:, m * P:(m + 1) * P], conv[:, 16 + hd, t], C("ident"), start=True, stop=True)
                        ins = nc.tensor.matmul(bank[7][:, m * P:(m + 1) * P], conv[:, hd, t], C("ident"), start=True, stop=True)
                ins.then_inc(S("dn_grams"), 1)
                pe.wait_ge(S("dn_mask"), 7 * g + 1)
                pe.wait_ge(S("dn_e_ready"), g + 1)
                for m in range(4):
                    ins = nc.tensor.matmul(bank[3][:, m * P:(m + 1) * P], AMd[:, 0, m, :], C("ident"), start=True, stop=True)
                ins.then_inc(S("dn_first"), 1)
                for l in range(1, LEVELS):
                    pe.wait_ge(S("dn_mask"), 7 * g + l + 1)
                    pe.wait_ge(S("dn_step"), 7 * g + l)
                    for m in range(4):
                        ins = nc.tensor.matmul(bank[2][:, m * P:(m + 1) * P], AMd[:, l % 2, m, :], Td[:, m, :], start=True, stop=True)
                    ins.then_inc(S("dn_y"), 1)
                    pe.wait_ge(S("dn_y_taken"), 6 * g + l)
                    if l < LEVELS - 1:
                        for m in range(4):
                            nc.tensor.matmul(bank[3][:, m * P:(m + 1) * P], Ud[:, m, :], Yd[:, m, :], start=True, stop=True)
                    for m in range(4):
                        ins = nc.tensor.matmul(bank[4][:, m * P:(m + 1) * P], Yd[:, m, :], Ud[:, m, :], start=True, stop=True)
                    ins.then_inc(S("dn_delta"), 1)
                pe.wait_ge(S("dn_step"), 7 * g + 7)
                pe.wait_ge(S("dn_toks"), g + 1)
                for i in range(2):
                    nc.tensor.matmul(bank[2][:, i * P:(i + 1) * P], kbg[:, i, :], Ud[:, 2 * i + 1, :], start=True, stop=True)
                for i in range(2):
                    ins = nc.tensor.matmul(bank[2][:, (2 + i) * P:(3 + i) * P], Ud[:, 2 * i, :], vb[:, 2 * i, :], start=True, stop=True)
                ins.then_inc(S("dn_wv"), 1)
                pe.wait_ge(S("dn_wv_taken"), g + 1)
                for i in range(2):
                    ins = nc.tensor.matmul(bank[3][:, i * P:(i + 1) * P], kdec[:, i, :], vn0[:, i, :], start=True, stop=True)
                ins.then_inc(S("dn_s"), 1)
                pe.wait_ge(S("dn_s_taken"), g + 1)
                for i in range(2):
                    nc.tensor.matmul(bank[4][:, i * P:(i + 1) * P], Ud[:, 2 * i + 1, :], vb[:, 2 * i + 1, :], start=True, stop=False)
                    ins = nc.tensor.matmul(bank[4][:, i * P:(i + 1) * P], w1T[:, i, :], S1[:, i, :], start=False, stop=True)
                ins.then_inc(S("dn_v1"), 1)
                pe.wait_ge(S("dn_v1_taken"), g + 1)
                for i in range(2):
                    nc.tensor.matmul(bank[5][:, i * T1:i * T1 + P], vn0[:, i, :], attn[:, 2 * i, :], start=True, stop=True)
                    nc.tensor.matmul(bank[5][:, i * T1 + P:(i + 1) * T1], S1[:, i, :], qd[:, i, :], start=True, stop=False)
                    ins = nc.tensor.matmul(bank[5][:, i * T1 + P:(i + 1) * T1], vn1[:, i, :], attn[:, 2 * i + 1, :],
                                           start=False, stop=True)
                ins.then_inc(S("dn_o"), 1)
                pe.wait_ge(S("dn_o_sq"), g + 1)
                nc.tensor.matmul(bank[6][:, :], C("mean128"), sq2, start=True, stop=True).then_inc(S("dn_var"), 1)

            pe.wait_ge(S("ret_gated"), 1)
            for _m in range(8):
                project(lambda k: ro[:, k, :], DT, T1)
            pe.wait_ge(S("dn_gated"), 1)
            for _m in range(8):
                project(lambda k: conv[:, 16 + k, :], DT, T1)
            pe.wait_ge(S("merged"), 1)
            for _m in range(8):
                project(lambda k: gr[:, k, :], DT, T1)
            norm(DT, T1)
            pe.wait_ge(S("u_ready"), 2)
            for _m in range(2 * FT):
                project(uT, DT, T1)
            pe.wait_ge(S("ffn_prod"), FT)
            for _m in range(8):
                project(lambda k: prod[:, k, :], FT, T1)
            norm(DT, T1)

            norm(DT, T2)
            pe.wait_ge(S("lerped"), 1)
            b = free_bank()
            wb = []
            for k in range(DT):
                wb.append(weights())
                for j in range(2):
                    ins = nc.tensor.matmul(b[64 * j:64 * j + 64, 0:T2], wb[k][:, 64 * j:64 * j + 64], xs_wa[:, j, k, :],
                                           start=k == 0, stop=k == DT - 1)
            ins.then_inc(S("proj_done"), 1)

            filled = [0]
            current = [None]

            def fill(upto):
                while filled[0] < upto:
                    q, k = divmod(filled[0], sum(RW_OUTS))
                    j = 0
                    while k >= RW_OUTS[j]:
                        k -= RW_OUTS[j]
                        j += 1
                    if k == 0:
                        if j == R_KK:
                            pe.wait_ge(S("rw_kk2"), q + 1)
                        if j == R_BONUS:
                            pe.wait_ge(S("rw_feats"), q + 1)
                        current[0] = free_bank()
                    b = current[0]
                    if j in (R_W, R_A):
                        r = slice(64 * (j - R_W), 64 * (j - R_W) + 64)
                        ins = nc.tensor.matmul(b[:, 0:T2], wl[r, q * P:(q + 1) * P], lo[r, :], start=True, stop=True)
                    elif j in (R_KK, R_BONUS):
                        ins = nc.tensor.matmul(b[:, 0:T2], C("ones64"), kk2 if j == R_KK else tk, start=True, stop=True)
                    else:
                        x = xs[:, {R_K: 0, R_R: 1, R_V: 2, R_G: 3}[j], k, :]
                        ins = nc.tensor.matmul(b[:, 0:T2], weights(), x, start=k == 0, stop=k == DT - 1)
                    if k == RW_OUTS[j] - 1:
                        ins.then_inc(S("proj_done"), 1)
                    filled[0] += 1

            def grams(p, c):
                t0, n = RCH[c]
                t = slice(t0, t0 + n)
                banks = ((5, 6), (2, 3), (4, 7))[c]
                for i in range(2):
                    for j in range(2):
                        r = slice(64 * j, 64 * j + 64)
                        ins = nc.tensor.matmul(bank[banks[j]][0:n, i * 2 * n:(i + 1) * 2 * n], bk[r, i, t], ar[r, p % 2, :, t],
                                               start=True, stop=True)
                ins.then_inc(S("rw_grams"), 1)

            def to_tokens(p, c, b):
                t0, n = RCH[c]
                for j, src in enumerate((gin[:, p % 2, 4, :], bk[:, 1, :], bk[:, 0, :])):
                    ins = nc.tensor.transpose(bank[b][0:n, j * P:(j + 1) * P], src[:, t0:t0 + n], C("ident"))
                ins.then_inc(S("rw_toks"), 1)

            def gram_of(p, c, j, i):
                n = RCH[c][1]
                g = G0[0:n, p % 2, j, :] if c == 0 else GG[:, p % 2, 2 * (c - 1) + j, :]
                return g[:, i * n:(i + 1) * n]

            def chain_z(p, c):
                t0, n = RCH[c]
                t = slice(t0, t0 + n)
                if c >= 1:
                    pe.wait_ge(S("rw_state_taken"), 2 * p + c)
                    nc.tensor.matmul(bank[5][0:n, 0:P], ar[:, p % 2, 0, t], S0, start=True, stop=False)
                for j in range(2):
                    f = slice(64 * j, 64 * j + 64)
                    ins = nc.tensor.matmul(bank[5][0:n, f], gram_of(p, c, j, 2), tok[0:n, p % 2, c, 0, f],
                                           start=c == 0, stop=c == 0 or j == 1)
                ins.then_inc(S("rw_z"), 1)
                if c >= 1:
                    nc.tensor.matmul(bank[7][:, t], S0, ar[:, p % 2, 1, t], start=True, stop=False).then_inc(S("rw_s0_read"), 1)

            def chain_sa(p, c):
                n = RCH[c][1]
                pe.wait_ge(S("rw_z_taken"), 3 * p + c + 1)
                for j in range(2):
                    f = slice(64 * j, 64 * j + 64)
                    inv = U0[p % 2][0:n, j, :] if c == 0 else Ur[p % 2][:, 2 * (c - 1) + j, :]
                    ins = nc.tensor.matmul(bank[6][0:n, f], inv, Zs[0:n, f], start=True, stop=True)
                ins.then_inc(S("rw_sa"), 1)

            def chain_y(p, c):
                t0, n = RCH[c]
                t = slice(t0, t0 + n)
                pe.wait_ge(S("rw_sa_taken"), 3 * p + c + 1)
                if c < 2:
                    nc.tensor.matmul(bank[5][:, 0:P], tok[0:n, p % 2, c, 1, :], tok[0:n, p % 2, c, 0, :], start=True, stop=False)
                    nc.tensor.matmul(bank[5][:, 0:P], tok[0:n, p % 2, c, 2, :], nSA[0:n, :], start=False, stop=True)\
                        .then_inc(S("rw_state"), 1)
                for j in range(2):
                    f = slice(64 * j, 64 * j + 64)
                    nc.tensor.matmul(bank[7][f, t], nSA[0:n, f], gram_of(p, c, j, 1), start=c == 0, stop=False)
                    ins = nc.tensor.matmul(bank[7][f, t], tok[0:n, p % 2, c, 0, f], gram_of(p, c, j, 3), start=False, stop=True)
                ins.then_inc(S("rw_yc"), 1)

            def center(p):
                pe.wait_ge(S("rw_ys"), p + 1)
                nc.tensor.matmul(bank[5][:, 0:T2], C("center64"), ys, start=True, stop=True).then_inc(S("rw_centered"), 1)

            def variance(p):
                pe.wait_ge(S("rw_sq"), p + 1)
                nc.tensor.matmul(bank[6][:, 0:T2], C("mean64"), sqr, start=True, stop=True).then_inc(S("rw_var"), 1)

            pe.wait_ge(S("proj_taken"), pn[0])
            pe.wait_ge(S("wl_loaded"), 16)
            fill(RW_AHEAD)
            for p in range(PAIRS):
                fill(fill_end(p, "start1"))
                if p >= 2:
                    variance(p - 2)
                fill(fill_end(p, "start2"))
                fill(fill_end(p, "bonus"))
                pe.wait_ge(S("rw_feats"), p + 1)
                grams(p, 1)
                grams(p, 2)
                fill(fill_end(p, "grams"))
                if p >= 2:
                    pe.wait_ge(S("rw_normed"), p - 1)
                grams(p, 0)
                fill(fill_end(p, "gram0"))
                am, T, U, Y = AMr, Tr, Ur[p % 2], Yr
                pe.wait_ge(S("rw_mask"), 7 * p + 1)
                pe.wait_ge(S("rw_grams_taken"), 3 * p + 3)
                for m in range(4):
                    nc.tensor.transpose(bank[2][:, m * P:(m + 1) * P], am[0][:, m, :], C("ident"))
                for j in range(2):
                    ins = nc.tensor.transpose(bank[3][0:META, j * META:(j + 1) * META], AM0[0][0:META, j, :], C("ident", META, META))
                ins.then_inc(S("rw_first"), 1)
                to_tokens(p, 1, 5)
                to_tokens(p, 2, 6)
                fill(fill_end(p, "first"))
                pe.wait_ge(S("rw_toks_taken"), 3 * p + 1)
                to_tokens(p, 0, 5)
                for l in range(1, LEVELS):
                    short = l < 4
                    pe.wait_ge(S("rw_mask"), 7 * p + l + 1)
                    pe.wait_ge(S("rw_step"), 7 * p + l)
                    for m in range(4):
                        ins = nc.tensor.matmul(bank[2][:, m * 64:(m + 1) * 64], am[l % 2][:, m, :],
                                               parts(T[:, m:m + 1, :], l, 0)[:, 0], start=True, stop=True)
                    if short:
                        for j in range(2):
                            ins = nc.tensor.matmul(bank[2][0:META, 256 + j * META:256 + (j + 1) * META], AM0[l % 2][0:META, j, :],
                                                   T0[0:META, j, :], start=True, stop=True)
                    ins.then_inc(S("rw_y"), 1)
                    if l == 1:
                        pe.wait_ge(S("rw_toks_taken"), 3 * p + 3)
                    if p >= 1:
                        (chain_z, chain_y)[(l - 1) % 2](p - 1, (l - 1) // 2)
                    fill(fill_end(p, f"y{l}"))
                    pe.wait_ge(S("rw_y_taken"), 6 * p + l)
                    if l < LEVELS - 1:
                        for m in range(4):
                            nc.tensor.matmul(bank[3][:, m * 64:(m + 1) * 64], U[:, m, :],
                                             parts(Y[l % 2][:, m:m + 1, :], l, 0)[:, 0], start=True, stop=True)
                        if short:
                            for j in range(2):
                                nc.tensor.matmul(bank[3][0:META, 256 + j * META:256 + (j + 1) * META], U0[p % 2][0:META, j, :],
                                                 Y0[0:META, j, :], start=True, stop=True)
                    for m in range(4):
                        ins = nc.tensor.matmul(bank[4][:, m * 64:(m + 1) * 64], Y[l % 2][:, m, :],
                                               parts(U[:, m:m + 1, :], l, 1)[:, 0], start=True, stop=True)
                    if short:
                        for j in range(2):
                            ins = nc.tensor.matmul(bank[4][0:META, 256 + j * META:256 + (j + 1) * META], Y0[0:META, j, :],
                                                   U0[p % 2][0:META, j, :], start=True, stop=True)
                    ins.then_inc(S("rw_delta"), 1)
                    if p >= 1 and l % 2 == 1:
                        chain_sa(p - 1, (l - 1) // 2)
                    fill(fill_end(p, f"delta{l}"))
                if p >= 1:
                    center(p - 1)
            pe.wait_ge(S("rw_step"), 7 * PAIRS)
            variance(PAIRS - 2)
            pe.wait_ge(S("rw_pair_done"), PAIRS - 1)
            for c in range(3):
                chain_z(PAIRS - 1, c)
                chain_sa(PAIRS - 1, c)
                chain_y(PAIRS - 1, c)
            center(PAIRS - 1)
            variance(PAIRS - 1)
            pe.wait_ge(S("rw_pair_done"), PAIRS)
            for _m in range(8):
                project(lambda k: yo[:, k, :], IT, T2)
            norm(DT, T2)

            norm(DT, T2)
            pe.wait_ge(S("u_ready"), 3)
            u2 = lambda k: u[:, k, :]
            for _m in range(4 + 2 + 1):
                project(u2, DT, T2)
            norm(4, T2)
            norm(2, T2)
            pe.wait_ge(S("proj_taken"), pn[0])
            nc.tensor.matmul(bank[3][:, 0:T2], C("perm"), kr[:, 0, :], start=True, stop=True).then_inc(S("kr_swapped"), 1)
            pe.wait_ge(S("lat_ready"), 1)
            for g in range(4):
                project_tokens(lambda k: ckvn[:, k, :], 2, [(0, P), (P, P), (2 * P, META)])

            in_ready = {}

            def project_q(hd):
                if hd % 2 == 0:
                    project(lambda k: cqn[:, k, :], 4, T2)
                    raw = pn[0]
                project(lambda k: cqn[:, k, :], 4, T2)
                if hd % 2 == 0:
                    pe.wait_ge(S("proj_taken"), raw)
                    nc.tensor.matmul(bank[2][:, 0:T2], C("perm"), qr[:, (hd // 2) % 2, 0, :], start=True, stop=True)\
                        .then_inc(S("qr_swapped"), 1)

            def project_k(hd):
                project(lambda k: ckvn[:, k, :], 2, T2)
                in_ready[hd] = pn[0]

            def scores(hd):
                q, k = hin[:, hd % 2, 0, :], hin[:, hd % 2, 1, :]
                r = slice(64 * (hd % 2), 64 * (hd % 2) + 64)
                qrot, krot = qr[r, (hd // 2) % 2, 2, :], kr[r, 1, :]
                pe.wait_ge(S("proj_taken"), in_ready[hd])
                pe.wait_ge(S("qr_ready"), hd // 2 + 1)
                if hd >= 1:
                    pe.wait_ge(S("at_masked"), hd)
                for o, q0, nq, nk in ((bank[3][:, 0:128], 0, P, 128), (bank[3][:, 128:384], P, P, 256), (bank[4][0:META, 0:T2], 2 * P, META, T2)):
                    nc.tensor.matmul(o, q[:, q0:q0 + nq], k[:, 0:nk], start=True, stop=False)
                    ins = nc.tensor.matmul(o, qrot[:, q0:q0 + nq], krot[:, 0:nk], start=False, stop=True)
                ins.then_inc(S("at_scores"), 1)

            def transpose_probs(hd):
                pb = hd % 2
                pe.wait_ge(S("at_probs"), hd + 1)
                if hd >= 1:
                    pe.wait_ge(S("at_pT_taken"), hd)
                for o, src, n in ((bank[6][:, 0:128], pr[:, pb, 0:128], P), (bank[6][:, 128:256], pr[:, pb, 128:256], P),
                                  (bank[6][:, 256:272], pr2[0:META, pb, 0:128], META),
                                  (bank[6][:, 272:400], pr[:, pb, 256:384], P), (bank[6][:, 400:416], pr2[0:META, pb, 128:256], META),
                                  (bank[6][0:META, 416:432], pr2[0:META, pb, 256:272], META)):
                    ins = nc.tensor.transpose(o, src, C("ident", n, n))
                ins.then_inc(S("at_pT"), 1)

            def values(hd):
                pb = hd % 2
                pe.wait_ge(S("at_pT_taken"), hd + 1)
                if hd >= 1:
                    pe.wait_ge(S("at_o_taken"), hd)
                v = slice(hd * P, (hd + 1) * P)
                nc.tensor.matmul(bank[7][:, 0:T2], vt[:, 0, v], pT[:, pb, 0:T2], start=True, stop=False)
                nc.tensor.matmul(bank[7][:, P:T2], vt[:, 1, v], pT[:, pb, 272:416], start=False, stop=False)
                nc.tensor.matmul(bank[7][:, 2 * P:T2], vt[0:META, 2, v], pT[0:META, pb, 416:432], start=False, stop=True)\
                    .then_inc(S("at_o"), 1)

            project_q(0)
            project_k(0)
            project(u2, DT, T2)
            pe.wait_ge(S("kr_ready"), 1)
            for hd in range(AH):
                scores(hd)
                if hd >= 1:
                    transpose_probs(hd - 1)
                if hd + 1 < AH:
                    project_q(hd + 1)
                if hd >= 1:
                    values(hd - 1)
                if hd + 1 < AH:
                    project_k(hd + 1)
                    project(u2, DT, T2)
            transpose_probs(AH - 1)
            values(AH - 1)
            pe.wait_ge(S("at_o_taken"), AH)
            for _m in range(8):
                project(lambda k: om[:, k, :], IT, T2)
            norm(DT, T2)
            assert blk[0] == NBLOCKS

        @block.scalar
        def _(act):
            taken_n = [0]
            chain = [0]

            def link(ins):
                chain[0] += 1
                ins.then_inc(S("act_chain"), 1)
                act.wait_ge(S("act_chain"), chain[0])

            def take(out, func=ACT.Copy, rows_=slice(0, P), n=T1, **kw):
                i = taken_n[0]
                taken_n[0] += 1
                act.wait_ge(S("proj_done"), i + 1)
                nc.scalar.activation(out, bank[i % 2][rows_, 0:n], func, **kw).then_inc(S("proj_taken"), 1)

            norm_n = [0]

            def norm(src, nt, T, width):
                norm_n[0] += 1
                nc.scalar.activation(sq[:, 0:nt, 0:T], src, ACT.Square).then_inc(S("norm_sq"), 1)
                act.wait_ge(S("norm_sum"), norm_n[0])
                nc.scalar.activation(sd[:, 0:T], bank[2][:, 0:T], ACT.Sqrt, bias=eps_col(0), scale=1.0 / width)\
                    .then_inc(S("norm_sd"), 1)

            act.dma_start(h[:, :, 0:META], metaT).then_inc(S("x_loaded"), 16)
            act.wait_ge(S("x_loaded"), 32)
            act.wait_ge(S("con_loaded"), 16)
            act.wait_ge(S("vec_loaded"), 16)
            norm(h[:, :, META:], DT, T1, D)
            for b in range(8):
                take(qkraw[:, b, :])
            for g in range(2):
                for t in range(2):
                    take(vtok[:, t, g * 512:(g + 1) * 512], n=512)
            act.wait_ge(S("raw_zeroed"), 1)
            for b in range(24):
                take(raw[:, b, 3:])
            act.wait_ge(S("dbda_done"), 1)
            nc.scalar.activation(rows[0:8, 0, :], bank[2][0:8, 0:T1], ACT.Sigmoid)
            nc.scalar.activation(rows[0:8, 1, :], bank[2][0:8, T1:2 * T1], ACT.Identity, bias=V("dt_bias", 0, 8))\
                .then_inc(S("row_y"), 1)
            act.wait_ge(S("row_abs"), 1)
            link(nc.scalar.activation(rows[0:8, 5, :], rows[0:8, 5, :], ACT.Exp))
            nc.scalar.activation(rows[0:8, 5, :], rows[0:8, 5, :], ACT.Ln, bias=1.0)
            nc.scalar.activation(sd[0:8, 0:1], V("a_log", 0, 8), ACT.Exp).then_inc(S("row_ln"), 1)
            for b in range(8):
                take(rgate[:, b, :], ACT.Silu)
            for s in range(3):
                act.wait_ge(S("conv_done"), s + 1)
                nc.scalar.activation(conv[:, 8 * s:8 * s + 8, :], conv[:, 8 * s:8 * s + 8, :], ACT.Silu)\
                    .then_inc(S("conv_silu"), 1)
            for hd in range(H1):
                act.wait_ge(S("ret_out"), hd + 1)
                nc.scalar.activation(ro[:, hd, :], bank[5 + hd % 2][:, 0:T1], ACT.Copy).then_inc(S("ret_out_taken"), 1)
            for g in range(4):
                act.wait_ge(S("ret_centered"), g + 1)
                nc.scalar.activation(sq2, bank[7][:, :], ACT.Square).then_inc(S("ret_sq"), 1)
                act.wait_ge(S("ret_var"), g + 1)
                if g >= 1:
                    act.wait_ge(S("ret_normed"), g)
                nc.scalar.activation(rn2, bank[2][:, :], ACT.Sqrt, bias=eps_col(1)).then_inc(S("ret_sd"), 1)
            act.wait_ge(S("conv_done"), 3)
            for b in range(8):
                take(dz[:, b, :], ACT.Silu)
            for b in range(8):
                take(gr[:, b, :], ACT.Sigmoid)
            for b in range(8):
                take(gd[:, b, :], ACT.Sigmoid)
            act.wait_ge(S("conv_silu"), 3)
            for n in range(8):
                nc.scalar.activation(sq2, conv[:, 2 * n:2 * n + 2, :].rearrange("p a b -> p (a b)"), ACT.Square)\
                    .then_inc(S("l2_sq"), 1)
                act.wait_ge(S("l2_sum"), n + 1)
                act.wait_ge(S("ret_normed"), 4)
                if n >= 1:
                    act.wait_ge(S("l2_done"), n)
                nc.scalar.activation(rn2, bank[3][:, :], ACT.Sqrt, bias=eps_col(0)).then_inc(S("l2_sd"), 1)
            act.wait_ge(S("rows_g"), 1)
            nc.scalar.activation(rows[0:8, 3, 0:CH], rows[0:8, 3, 0:CH], ACT.Exp)
            nc.scalar.activation(rows[0:8, 4, :], rows[0:8, 2, :], ACT.Exp).then_inc(S("rows_exp"), 1)
            act.wait_ge(S("cols_done"), 1)
            nc.scalar.activation(cols, bank[3][:, 0:48], ACT.Copy).then_inc(S("cols_taken"), 1)
            for g in range(4):
                act.wait_ge(S("dn_diff"), g + 1)
                nc.scalar.activation(Em, Em, ACT.Exp)
                if g >= 1:
                    act.wait_ge(S("dn_out"), g)
                for i in range(2):
                    ins = nc.scalar.activation(eg[:, i, :], bank[2][:, i * T1 + P:(i + 1) * T1], ACT.Exp)
                ins.then_inc(S("dn_exp"), 1)
                act.wait_ge(S("dn_grams"), g + 1)
                act.wait_ge(S("cols_taken"), 1)
                for i in range(2):
                    hd = 2 * g + i
                    for c in range(2):
                        m = 2 * i + c
                        nc.scalar.activation(vb[:, m, :], bank[6][:, m * P:(m + 1) * P], ACT.Copy, scale=cols[:, 8 * c + hd:8 * c + hd + 1])
                    nc.scalar.activation(kdec[:, i, :], bank[7][:, 2 * i * P:(2 * i + 1) * P], ACT.Copy, scale=cols[:, 32 + hd:33 + hd])
                    ins = nc.scalar.activation(kbg[:, i, :], bank[7][:, (2 * i + 1) * P:(2 * i + 2) * P], ACT.Copy,
                                               scale=cols[:, 40 + hd:41 + hd])
                ins.then_inc(S("dn_toks"), 1)
                for l in range(1, LEVELS):
                    act.wait_ge(S("dn_y"), 6 * g + l)
                    nc.scalar.activation(Yd, bank[2][:, :], ACT.Copy).then_inc(S("dn_y_taken"), 1)
                act.wait_ge(S("dn_wv"), g + 1)
                nc.scalar.activation(w1T, bank[2][:, 0:256], ACT.Copy)
                nc.scalar.activation(vn0, bank[2][:, 256:512], ACT.Copy).then_inc(S("dn_wv_taken"), 1)
                act.wait_ge(S("dn_s"), g + 1)
                nc.scalar.activation(S1, bank[3][:, 0:256], ACT.Copy).then_inc(S("dn_s_taken"), 1)
                act.wait_ge(S("dn_v1"), g + 1)
                nc.scalar.activation(vn1, bank[4][:, 0:256], ACT.Copy).then_inc(S("dn_v1_taken"), 1)
                act.wait_ge(S("dn_o"), g + 1)
                nc.scalar.activation(sq2, bank[5][:, :], ACT.Square).then_inc(S("dn_o_sq"), 1)
                act.wait_ge(S("dn_var"), g + 1)
                nc.scalar.activation(rn2, bank[6][:, :], ACT.Sqrt, bias=eps_col(0)).then_inc(S("dn_sd"), 1)
            for b in range(8):
                take(u[:, b, 0:T1])
            for b in range(8):
                take(sq[:, b, 0:T1])
            for b in range(8):
                take(conv[:, b, :])
            act.wait_ge(S("h_ready"), 1)
            norm(h[:, :, META:], DT, T1, D)
            act.wait_ge(S("up_zeroed"), 1)

            def up_silu(m):
                act.wait_ge(S("upc_ready"), m + 1)
                nc.scalar.activation(prod[:, m, :], upc[:, 2 * (m % 2), :], ACT.Silu).then_inc(S("up_silu"), 1)

            for m in range(FT):
                s = 2 * (m % 2)
                if m >= 2:
                    act.wait_ge(S("upc_ready"), m - 1)
                take(up[:, s, 2:])
                take(up[:, s + 1, 2:])
                if m >= 1:
                    up_silu(m - 1)
            up_silu(FT - 1)
            for b in range(8):
                take(down[:, b, :])
            act.wait_ge(S("h_ready"), 2)
            norm(h[:, :, META:], DT, T1, D)

            act.dma_start(wl, wlora).then_inc(S("wl_loaded"), 16)
            act.wait_ge(S("h_ready"), 3)
            norm(h[:, :, :], DT, T2, D)
            act.wait_ge(S("proj_done"), taken_n[0] + 1)
            i = taken_n[0]
            taken_n[0] += 1
            nc.scalar.activation(lo[0:64, :], bank[i % 2][0:64, 0:T2], ACT.Tanh)
            nc.scalar.activation(lo[64:128, :], bank[i % 2][64:128, 0:T2], ACT.Copy).then_inc(S("proj_taken"), 1)

            took = [0]

            def take_rwkv(q, j):
                if j == R_K:
                    if q >= 2:
                        act.wait_ge(S("rw_toks_taken"), 3 * q - 3)
                        act.wait_ge(S("rw_bonus_taken"), q - 1)
                    take(gin[:, q % 2, 2, :], n=T2)
                    act.wait_ge(S("proj_taken"), taken_n[0])
                    nc.scalar.activation(kk2, gin[:, q % 2, 2, :], ACT.Square, scale=V("rwkv_k_k_2", q)).then_inc(S("rw_kk2"), 1)
                elif j in (R_W, R_A):
                    i = j - R_W
                    take(gin[:, q % 2, i, :], ACT.Tanh, n=T2, bias=half_bias[:, i * PAIRS + q:i * PAIRS + q + 1], scale=0.5)
                elif j == R_KK:
                    if q >= 1:
                        act.wait_ge(S("rw_feats"), q)
                    take(sdk, ACT.Sqrt, n=T2)
                elif j in (R_R, R_V):
                    take(gin[:, q % 2, 3 if j == R_R else 4, :], n=T2)
                elif j == R_BONUS:
                    if q >= 3:
                        act.wait_ge(S("rw_pair_done"), q - 2)
                    take(bonv[:, q % 3, :], n=T2)
                else:
                    i = taken_n[0]
                    taken_n[0] += 1
                    act.wait_ge(S("proj_done"), i + 1)
                    nc.scalar.activation(gate[:, q % 3, :], bank[i % 2][:, 0:T2], ACT.Copy)
                    if q >= 1:
                        act.wait_ge(S("rw_gated"), q)
                    nc.scalar.activation(gtanh, bank[i % 2][:, 0:T2], ACT.Tanh, scale=0.5).then_inc(S("proj_taken"), 1)

            def take_until(n):
                while took[0] < outs_at(n):
                    take_rwkv(*divmod(took[0], 8))
                    took[0] += 1

            def exponentials(q):
                act.wait_ge(S("rw_cs"), q + 1)
                link(nc.scalar.activation(Wc, cs, ACT.Exp, scale=-DECAY_C))
                nc.scalar.activation(Wi, cs, ACT.Exp, scale=DECAY_C)
                nc.scalar.activation(fcol[:, q % 3], fcol[:, q % 3], ACT.Exp, scale=-DECAY_C)
                nc.scalar.activation(Wp, dd, ACT.Exp, scale=-DECAY_C).then_inc(S("rw_w"), 1)

            def chain_z(p, c):
                n = RCH[c][1]
                act.wait_ge(S("rw_z"), 3 * p + c + 1)
                nc.scalar.activation(Zs[0:n, :], bank[5][0:n, 0:P], ACT.Copy).then_inc(S("rw_z_taken"), 1)

            def chain_sa(p, c):
                n = RCH[c][1]
                act.wait_ge(S("rw_sa"), 3 * p + c + 1)
                if c >= 1 or p >= 1:
                    act.wait_ge(S("rw_yc"), 3 * p + c)
                nc.scalar.activation(nSA[0:n, :], bank[6][0:n, 0:P], ACT.Copy).then_inc(S("rw_sa_taken"), 1)

            def take_ys(p):
                act.wait_ge(S("rw_yc"), 3 * p + 3)
                if p >= 1:
                    act.wait_ge(S("rw_centered"), p)
                nc.scalar.activation(ys, bank[7][:, 0:T2], ACT.Copy).then_inc(S("rw_ys"), 1)

            def square(p):
                act.wait_ge(S("rw_centered"), p + 1)
                if p >= 1:
                    act.wait_ge(S("rw_var"), p)
                nc.scalar.activation(sqr, bank[5][:, 0:T2], ACT.Square).then_inc(S("rw_sq"), 1)

            def deviation(p):
                act.wait_ge(S("rw_var"), p + 1)
                if p >= 1:
                    act.wait_ge(S("rw_pair_done"), p)
                nc.scalar.activation(sdn, bank[6][:, 0:T2], ACT.Sqrt, bias=eps_col(2)).then_inc(S("rw_sd"), 1)

            act.wait_ge(S("half_bias_ready"), 1)
            take_until(10)
            exponentials(0)
            take_until(RW_AHEAD)
            for p in range(PAIRS):
                if p >= 2:
                    square(p - 2)
                take_until(fill_end(p, "start1"))
                if p >= 2:
                    deviation(p - 2)
                take_until(fill_end(p, "gram0"))
                for i, c in enumerate((1, 2, 0)):
                    n = RCH[c][1]
                    if c == 0:
                        take_until(fill_end(p, "first"))
                    act.wait_ge(S("rw_toks"), 3 * p + i + 1)
                    b = bank[(5, 6, 5)[i]]
                    nc.scalar.activation(tok[0:n, p % 2, c, 0:2, :], b[0:n, 0:256], ACT.Copy)
                    nc.scalar.activation(tok[0:n, p % 2, c, 2, :], b[0:n, 256:384], ACT.Copy, scale=-1.0)\
                        .then_inc(S("rw_toks_taken"), 1)
                for l in range(1, LEVELS):
                    act.wait_ge(S("rw_y"), 6 * p + l)
                    act.wait_ge(S("rw_y_zero"), 6 * p + l)
                    if l < 4:
                        nc.scalar.activation(Y0[0:META].rearrange("p a b -> p (a b)"), bank[2][0:META, 256:288], ACT.Copy)
                    nc.scalar.activation(parts(Yr[l % 2], l, 0), packed(bank[2][:, 0:256], l), ACT.Copy).then_inc(S("rw_y_taken"), 1)
                    if p >= 1 and l % 2 == 1:
                        chain_z(p - 1, (l - 1) // 2)
                    take_until(fill_end(p, f"y{l}"))
                    if l == 3 and p + 1 < PAIRS:
                        exponentials(p + 1)
                    if p >= 1 and l % 2 == 1:
                        chain_sa(p - 1, (l - 1) // 2)
                    take_until(fill_end(p, f"delta{l}"))
                if p >= 1:
                    take_ys(p - 1)
            square(PAIRS - 2)
            deviation(PAIRS - 2)
            for c in range(3):
                chain_z(PAIRS - 1, c)
                chain_sa(PAIRS - 1, c)
            take_ys(PAIRS - 1)
            square(PAIRS - 1)
            deviation(PAIRS - 1)
            act.wait_ge(S("rw_pair_done"), PAIRS)
            for b in range(8):
                take(mo[:, b, :], n=T2)
            act.wait_ge(S("proj_taken"), taken_n[0])
            norm(mo, DT, T2, D)

            act.wait_ge(S("h_ready"), 4)
            norm(h[:, :, :], DT, T2, D)
            for b in range(4):
                take(cq[:, b, :], n=T2)
            for b in range(2):
                take(ckv[:, b, :], n=T2)
            take(kr[:, 0, :], n=T2)
            act.wait_ge(S("proj_taken"), taken_n[0])
            norm(cq, 4, T2, 512)
            act.wait_ge(S("cq_done"), 1)
            norm(ckv, 2, T2, 256)
            for g in range(4):
                for t, n in ((0, P), (1, P), (2, META)):
                    take(vt[0:n, t, g * 512:(g + 1) * 512], rows_=slice(0, n), n=512)

            def take_q(hd):
                if hd % 2 == 0:
                    take(qr[:, (hd // 2) % 2, 0, :], n=T2)
                take(hin[:, hd % 2, 0, :], n=T2)

            def take_k_gate(hd):
                take(hin[:, hd % 2, 1, :], n=T2)
                if hd >= 2:
                    act.wait_ge(S("at_o_taken"), hd - 1)
                i = taken_n[0]
                taken_n[0] += 1
                act.wait_ge(S("proj_done"), i + 1)
                nc.scalar.activation(hin[:, hd % 2, 2, :], bank[i % 2][:, 0:T2], ACT.Copy)
                if hd >= 1:
                    act.wait_ge(S("at_gated"), hd)
                nc.scalar.activation(atanh, bank[i % 2][:, 0:T2], ACT.Tanh, scale=0.5).then_inc(S("proj_taken"), 1)

            def take_pT(hd):
                pb = hd % 2
                act.wait_ge(S("at_pT"), hd + 1)
                nc.scalar.activation(pT[:, pb, 0:416], bank[6][:, 0:416], ACT.Copy)
                nc.scalar.activation(pT[0:META, pb, 416:432], bank[6][0:META, 416:432], ACT.Copy).then_inc(S("at_pT_taken"), 1)

            take_q(0)
            take_k_gate(0)
            for hd in range(AH):
                pb = hd % 2
                if hd >= 1:
                    take_pT(hd - 1)
                if hd + 1 < AH:
                    take_q(hd + 1)
                act.wait_ge(S("at_max"), hd + 1)
                nc.scalar.activation(pr[:, pb, 0:128], pr[:, pb, 0:128], ACT.Exp, scale=SCALE_A, bias=nm[:, pb, 3:4], accum_out=nm[:, pb, 6:7])
                nc.scalar.activation(pr[:, pb, 128:384], pr[:, pb, 128:384], ACT.Exp, scale=SCALE_A, bias=nm[:, pb, 4:5], accum_out=nm[:, pb, 7:8])
                nc.scalar.activation(pr2[0:META, pb, :], pr2[0:META, pb, :], ACT.Exp, scale=SCALE_A, bias=nm[0:META, pb, 5:6],
                                     accum_out=nm[0:META, pb, 8:9]).then_inc(S("at_exp"), 1)
                if hd + 1 < AH:
                    take_k_gate(hd + 1)
            take_pT(AH - 1)
            for b in range(8):
                take(mo[:, b, :], n=T2)
            act.wait_ge(S("proj_taken"), taken_n[0])
            norm(mo, DT, T2, D)

        @block.vector
        def _(dve):
            chain = [0]
            V_ = nc.vector

            def link(ins):
                chain[0] += 1
                ins.then_inc(S("dve_chain"), 1)
                dve.wait_ge(S("dve_chain"), chain[0])

            norm_n = [0]

            def norm(outs, srcs, gains, T, signal, **kw):
                norm_n[0] += 1
                dve.wait_ge(S("norm_sd"), norm_n[0])
                link(V_.reciprocal(rs[:, 0:T], sd[:, 0:T]))
                for o, s, g in zip(outs, srcs, gains):
                    ins = V_.scalar_tensor_tensor(out=o, in0=s, scalar=g, in1=rs[:, 0:T], op0=ALU.mult, op1=ALU.mult)
                if signal is None:
                    link(ins)
                else:
                    ins.then_inc(S(signal), 1)

            V_.memset(raw[:, :, 0:3], 0.0).then_inc(S("raw_zeroed"), 1)
            dve.wait_ge(S("vec_loaded"), 16)
            dve.wait_ge(S("con_loaded"), 16)
            norm([u[:, t, 0:T1] for t in range(DT)], [h[:, t, META:] for t in range(DT)],
                 [V("g_mix", t) for t in range(DT)], T1, "u_ready")
            for s, first in enumerate((8, 0, 16)):
                dve.wait_ge(S("proj_taken"), 12 + 8 * (s + 1))
                for tap in (3, 0, 1, 2):
                    for b in range(8):
                        w = V("dn_conv_w", tap * 24 + first + b)
                        src, dst = raw[:, 8 * s + b, tap:tap + T1], conv[:, 8 * s + b, :]
                        if tap == 3:
                            ins = V_.tensor_scalar(dst, src, w, None, ALU.mult)
                        else:
                            ins = V_.scalar_tensor_tensor(out=dst, in0=src, scalar=w, in1=dst, op0=ALU.mult, op1=ALU.add)
                    if tap != 2:
                        link(ins)
                ins.then_inc(S("conv_done"), 1)
            dve.wait_ge(S("row_y"), 1)
            link(V_.tensor_scalar(rows[0:8, 5, :], rows[0:8, 1, :], -1.0, None, ALU.mult))
            link(V_.tensor_tensor(rows[0:8, 5, :], rows[0:8, 5, :], rows[0:8, 1, :], ALU.min))
            V_.tensor_scalar(rows[0:8, 1, :], rows[0:8, 1, :], 0.0, None, ALU.max).then_inc(S("row_abs"), 1)
            dve.wait_ge(S("row_ln"), 1)
            dve.wait_ge(S("row_abs"), 1)
            link(V_.tensor_tensor(rows[0:8, 1, :], rows[0:8, 1, :], rows[0:8, 5, :], ALU.add))
            link(V_.tensor_scalar(rows[0:8, 1, :], rows[0:8, 1, :], sd[0:8, 0:1], -1.0, ALU.mult, ALU.mult))
            link(V_.memset(rows[0:8, 5, :], 1.0))
            for c in range(2):
                t = slice(c * CH, (c + 1) * CH)
                ins = V_.tensor_tensor_scan(rows[0:8, 2, t], rows[0:8, 5, t], rows[0:8, 1, t], 0.0, ALU.mult, ALU.add)
            link(ins)
            V_.tensor_scalar(rows[0:8, 3, 0:CH], rows[0:8, 2, 0:CH], rows[0:8, 2, CH - 1:CH], -1.0, ALU.subtract, ALU.mult)\
                .then_inc(S("rows_g"), 1)
            dve.wait_ge(S("swapped"), 1)
            cosb, sinb = C("cos", T1), C("sin", T1)
            link(V_.tensor_tensor(qk, qkraw, over(cosb, 8), ALU.mult))
            for g in range(4):
                ins = V_.tensor_tensor(qkraw[:, 2 * g:2 * g + 2, :], bank[3 + g][:, :].rearrange("p (a b) -> p a b", a=2),
                                       over(sinb, 2), ALU.mult)
            link(ins)
            V_.tensor_tensor(qk, qk, qkraw, ALU.add).then_inc(S("qk_ready"), 1)
            dve.wait_ge(S("decay_loaded"), 16)
            for hd in range(H1):
                dve.wait_ge(S("ret_scores"), hd + 1)
                if hd >= 2:
                    dve.wait_ge(S("ret_out"), hd - 1)
                V_.tensor_tensor(sT[:, hd % 2, 0:256], bank[3 + hd % 2][:, 0:256], decay[:, hd, :], ALU.mult)
                V_.tensor_tensor(sT[:, hd % 2, 256:384], bank[3 + hd % 2][:, 256:384], decay[:, hd, 0:128], ALU.mult)\
                    .then_inc(S("ret_decayed"), 1)
            for g in range(4):
                dve.wait_ge(S("ret_sd"), g + 1)
                link(V_.reciprocal(rn2, rn2))
                for i in range(2):
                    hd = 2 * g + i
                    ins = V_.scalar_tensor_tensor(out=ro[:, hd, :], in0=bank[7][:, i * T1:(i + 1) * T1], scalar=V("ret_norm_g", hd),
                                                  in1=rn2[:, i * T1:(i + 1) * T1], op0=ALU.mult, op1=ALU.mult)
                ins.then_inc(S("ret_normed"), 1)
            dve.wait_ge(S("ret_normed"), 4)
            dve.wait_ge(S("proj_taken"), 44)
            V_.tensor_tensor(ro, ro, rgate, ALU.mult).then_inc(S("ret_gated"), 1)
            for s, sc in ((0, 1.0), (1, float(DN_SCALE))):
                for g in range(4):
                    n = 4 * s + g
                    dve.wait_ge(S("l2_sd"), n + 1)
                    link(V_.reciprocal(rn2, rn2))
                    cc = conv[:, 8 * s + 2 * g:8 * s + 2 * g + 2, :]
                    V_.scalar_tensor_tensor(out=cc, in0=cc, scalar=sc, in1=rn2.rearrange("p (a b) -> p a b", a=2),
                                            op0=ALU.mult, op1=ALU.mult).then_inc(S("l2_done"), 1)
            dve.wait_ge(S("rows_exp"), 1)
            V_.scalar_tensor_tensor(out=rows[0:8, 4, :], in0=rows[0:8, 4, :], scalar=-1.0, in1=rows[0:8, 0, :],
                                    op0=ALU.mult, op1=ALU.mult).then_inc(S("rows_ready"), 1)
            dve.wait_ge(S("cols_taken"), 1)
            idd = over(C("ident"), 4)
            for g in range(4):
                dve.wait_ge(S("dn_bcast"), g + 1)
                for i in range(2):
                    hd = 2 * g + i
                    for c in range(2):
                        ins = V_.tensor_scalar(Em[:, 2 * i + c, :], bank[2][:, i * T1 + c * P:i * T1 + (c + 1) * P],
                                               cols[:, 16 + 8 * c + hd:17 + 8 * c + hd], 0.0, ALU.subtract, ALU.min)
                ins.then_inc(S("dn_diff"), 1)
                dve.wait_ge(S("dn_exp"), g + 1)
                link(V_.tensor_tensor(Ea, Em, over(C("strict"), 4), ALU.mult))
                V_.tensor_tensor(Ea, Ea, bank[3][:, :].rearrange("p (a b) -> p a b", a=4), ALU.mult)
                link(V_.tensor_tensor(Em, Em, over(C("causal"), 4), ALU.mult))
                dve.wait_ge(S("dn_grams"), g + 1)
                V_.tensor_tensor(ATd, bank[4][:, :].rearrange("p (a b) -> p a b", a=4), Ea, ALU.mult).then_inc(S("dn_A"), 1)
                V_.tensor_tensor(attn, bank[5][:, :].rearrange("p (a b) -> p a b", a=4), Em, ALU.mult)
                V_.tensor_tensor(qd, conv[:, 8 + 2 * g:10 + 2 * g, CH:], eg, ALU.mult).then_inc(S("dn_e_ready"), 1)
                dve.wait_ge(S("dn_mask"), 7 * g + 1)
                V_.tensor_tensor(Ud, idd, AMd[:, 0], ALU.subtract)
                dve.wait_ge(S("dn_first"), g + 1)
                V_.tensor_tensor(Td, idd, bank[3][:, :].rearrange("p (a b) -> p a b", a=4), ALU.subtract).then_inc(S("dn_step"), 1)
                dve.wait_ge(S("dn_step"), 7 * g + 1)
                for l in range(1, LEVELS):
                    dve.wait_ge(S("dn_delta"), 6 * g + l)
                    if l < LEVELS - 1:
                        V_.tensor_tensor(Td, Td, bank[3][:, :].rearrange("p (a b) -> p a b", a=4), ALU.subtract)
                    V_.tensor_tensor(Ud, Ud, bank[4][:, :].rearrange("p (a b) -> p a b", a=4), ALU.subtract).then_inc(S("dn_step"), 1)
                    dve.wait_ge(S("dn_step"), 7 * g + 1 + l)
                dve.wait_ge(S("dn_sd"), g + 1)
                link(V_.reciprocal(rn2, rn2))
                for i in range(2):
                    hd = 2 * g + i
                    ins = V_.scalar_tensor_tensor(out=conv[:, 16 + hd, :], in0=bank[5][:, i * T1:(i + 1) * T1], scalar=V("dn_norm_g", 0),
                                                  in1=rn2[:, i * T1:(i + 1) * T1], op0=ALU.mult, op1=ALU.mult)
                ins.then_inc(S("dn_out"), 1)
            dve.wait_ge(S("dn_out"), 4)
            dve.wait_ge(S("proj_taken"), 52)
            V_.tensor_tensor(conv[:, 16:24, :], conv[:, 16:24, :], dz, ALU.mult).then_inc(S("dn_gated"), 1)
            dve.wait_ge(S("proj_taken"), 68 + 8)
            V_.tensor_tensor(gr, gr, u[:, :, 0:T1], ALU.mult)
            dve.wait_ge(S("proj_taken"), 68 + 16)
            link(V_.tensor_tensor(gd, gd, sq[:, :, 0:T1], ALU.mult))
            V_.tensor_tensor(gr, gr, gd, ALU.add).then_inc(S("merged"), 1)
            dve.wait_ge(S("proj_taken"), 68 + 24)
            V_.tensor_tensor(h[:, :, META:], h[:, :, META:], conv[:, 0:8, :], ALU.add).then_inc(S("h_ready"), 1)
            dve.wait_ge(S("h_ready"), 1)
            norm([u[:, t, 0:T1] for t in range(DT)], [h[:, t, META:] for t in range(DT)],
                 [V("g_ffn", t) for t in range(DT)], T1, "u_ready")
            V_.memset(up[:, :, 0:2], 0.0).then_inc(S("up_zeroed"), 1)
            for m in range(FT + 1):
                if m < FT:
                    s = 2 * (m % 2)
                    dve.wait_ge(S("proj_taken"), 92 + 2 * m + 2)
                    if m >= 2:
                        dve.wait_ge(S("up_silu"), m - 1)
                        dve.wait_ge(S("ffn_prod"), m - 1)
                    for tap in (2, 0, 1):
                        for j in range(2):
                            w = V("ffn_conv_w", tap * 44 + j * FT + m)
                            src, dst = up[:, s + j, tap:tap + T1], upc[:, s + j, :]
                            if tap == 2:
                                ins = V_.tensor_scalar(dst, src, w, V("ffn_conv_b", j * FT + m), ALU.mult, ALU.add)
                            else:
                                ins = V_.scalar_tensor_tensor(out=dst, in0=src, scalar=w, in1=dst, op0=ALU.mult, op1=ALU.add)
                        if tap != 1:
                            link(ins)
                    ins.then_inc(S("upc_ready"), 1)
                if m >= 1:
                    dve.wait_ge(S("up_silu"), m)
                    dve.wait_ge(S("upc_ready"), m)
                    s = 2 * ((m - 1) % 2)
                    V_.tensor_tensor(prod[:, m - 1, :], prod[:, m - 1, :], upc[:, s + 1, :], ALU.mult).then_inc(S("ffn_prod"), 1)
            n0 = 92 + 2 * FT
            dve.wait_ge(S("proj_taken"), n0 + 8)
            V_.tensor_tensor(h[:, :, META:], h[:, :, META:], down, ALU.add).then_inc(S("h_ready"), 1)
            dve.wait_ge(S("h_ready"), 2)
            norm([h[:, t, META:] for t in range(DT)], [h[:, t, META:] for t in range(DT)],
                 [V("g_final", t) for t in range(DT)], T1, "h_ready")

            norm([u[:, t, :] for t in range(DT)], [h[:, t, :] for t in range(DT)],
                 [V("norm_pre_2", t) for t in range(DT)], T2, None)
            V_.tensor_scalar(dx[:, :, 0:1], u[:, :, 0:1], -1.0, None, ALU.mult)
            link(V_.tensor_tensor(dx[:, :, 1:], u[:, :, 0:T2 - 1], u[:, :, 1:], ALU.subtract))
            for row, dst in ((4, xs_wa[:, 0]), (5, xs_wa[:, 1]), (1, xs[:, 0]), (0, xs[:, 1]), (2, xs[:, 2]), (3, xs[:, 3])):
                for t in range(DT):
                    ins = V_.scalar_tensor_tensor(out=dst[:, t, :], in0=dx[:, t, :], scalar=V("rwkv_mu_2", row * 8 + t),
                                                  in1=u[:, t, :], op0=ALU.mult, op1=ALU.add)
            ins.then_inc(S("lerped"), 1)
            V_.tensor_scalar(half_bias, vec[:, VOFF["rwkv_w0_2"]:VOFF["rwkv_w0_2"] + 2 * PAIRS], 0.5, None, ALU.mult)\
                .then_inc(S("half_bias_ready"), 1)
            dve.wait_ge(S("lerped"), 1)
            p0 = n0 + 8 + 1

            def scale_norm(p):
                dve.wait_ge(S("rw_sd"), p + 1)
                link(V_.reciprocal(sdn, sdn))
                V_.scalar_tensor_tensor(out=sdn, in0=bank[5][:, 0:T2], scalar=V("rwkv_ln_w_2", p), in1=sdn, op0=ALU.mult, op1=ALU.mult)\
                    .then_inc(S("rw_normed"), 1)

            def finish(p):
                dve.wait_ge(S("rw_normed"), p + 1)
                link(V_.scalar_tensor_tensor(out=sdn, in0=sdn, scalar=V("rwkv_ln_b_2", p), in1=bonv[:, p % 3, :], op0=ALU.add, op1=ALU.add))
                V_.scalar_tensor_tensor(out=yo[:, p, :], in0=sdn, scalar=0.5, in1=gate[:, p % 3, :], op0=ALU.mult, op1=ALU.mult).then_inc(S("rw_pair_done"), 1)

            def chain_state(p, c):
                dve.wait_ge(S("rw_state"), 2 * p + c + 1)
                if c == 1:
                    link(V_.tensor_tensor(S0, S0, bank[5][:, 0:P], ALU.add))
                elif p >= 1:
                    dve.wait_ge(S("rw_s0_read"), 2 * p)
                V_.scalar_tensor_tensor(out=S0, in0=S0 if c else bank[5][:, 0:P], scalar=fcol[:, p % 3, c:c + 1], in1=C("ones64"),
                                        op0=ALU.mult, op1=ALU.mult).then_inc(S("rw_state_taken"), 1)

            def feats_decay(q):
                sg = gin[:, q % 2, 0, :]
                dve.wait_ge(S("proj_taken"), p0 + 8 * q + R_A + 1)
                link(V_.tensor_scalar(gin[:, q % 2, 0:2, :], gin[:, q % 2, 0:2, :], 0.5, 0.5, ALU.mult, ALU.add))
                link(V_.tensor_tensor_scan(cs, C("reset", T2), sg, 0.0, ALU.mult, ALU.add))
                link(V_.tensor_copy(mids, cs[:, META + 63:META + 63 + CH + 1:CH]))
                long_cs = cs[:, META:].rearrange("p (c t) -> p c t", c=2)
                link(V_.tensor_tensor(long_cs, long_cs, mids.unsqueeze(2).to_broadcast([P, 2, CH]), ALU.subtract))
                V_.tensor_tensor(fcol[:, q % 3], cs[:, META - 1:META + CH:CH], mids, ALU.add)
                V_.tensor_tensor(dd, cs, sg, ALU.subtract).then_inc(S("rw_cs"), 1)

            def feats_key(q):
                a, k = gin[:, q % 2, 1, :], gin[:, q % 2, 2, :]
                link(V_.tensor_scalar(kp, a, 1.0, V("rwkv_k_a_2", q), ALU.subtract, ALU.mult))
                link(V_.scalar_tensor_tensor(out=kp, in0=kp, scalar=1.0, in1=k, op0=ALU.add, op1=ALU.mult))

            def feats_norm(q):
                dve.wait_ge(S("proj_taken"), p0 + 8 * q + R_KK + 1)
                link(V_.tensor_scalar(kkn, sdk, 1e-12, None, ALU.max))
                link(V_.reciprocal(kkn, kkn))

            def feats_products(q):
                a, k = gin[:, q % 2, 1, :], gin[:, q % 2, 2, :]
                link(V_.scalar_tensor_tensor(out=kkn, in0=k, scalar=V("rwkv_k_k_2", q), in1=kkn, op0=ALU.mult, op1=ALU.mult))
                if q >= 1:
                    dve.wait_ge(S("rw_toks"), 3 * q)
                link(V_.tensor_tensor(bk[:, 0, :], kkn, a, ALU.mult))
                dve.wait_ge(S("rw_w"), q + 1)
                V_.tensor_tensor(bk[:, 1, :], kp, Wi, ALU.mult)
                V_.tensor_tensor(bk[:, 0, :], bk[:, 0, :], Wi, ALU.mult)
                if q >= 2:
                    dve.wait_ge(S("rw_s0_read"), 2 * (q - 1))
                V_.tensor_tensor(ar[:, q % 2, 0, :], kkn, Wp, ALU.mult)

            def feats_receptance(q):
                r = gin[:, q % 2, 3, :]
                dve.wait_ge(S("proj_taken"), p0 + 8 * q + R_R + 1)
                V_.scalar_tensor_tensor(out=tk, in0=r, scalar=V("rwkv_r_k_2", q), in1=kp, op0=ALU.mult, op1=ALU.mult)
                V_.tensor_tensor(ar[:, q % 2, 1, :], r, Wc, ALU.mult).then_inc(S("rw_feats"), 1)

            for part in (feats_decay, feats_key, feats_norm, feats_products, feats_receptance):
                part(0)
            for p in range(PAIRS):
                if p >= 2:
                    dve.wait_ge(S("rw_yc"), 3 * (p - 1))
                    scale_norm(p - 2)
                for i, c in enumerate((1, 2, 0)):
                    n = RCH[c][1]
                    dve.wait_ge(S("rw_grams"), 3 * p + i + 1)
                    for j in range(2):
                        if c == 0:
                            ins = V_.tensor_tensor(G0[0:n, p % 2, j, :], bank[5 + j][0:n, 0:4 * n], C("mask_rw0", 4 * n, n), ALU.mult)
                        else:
                            b = ((2, 3), (4, 7))[c - 1][j]
                            ins = V_.tensor_tensor(GG[:, p % 2, 2 * (c - 1) + j, :], bank[b][:, :], C("mask_rw", 4 * P), ALU.mult)
                    ins.then_inc(S("rw_grams_taken"), 1)
                if p >= 2:
                    finish(p - 2)
                dve.wait_ge(S("proj_taken"), p0 + 8 * p + R_BONUS + 1)
                V_.tensor_tensor(bonv[:, p % 3, :], bonv[:, p % 3, :], gin[:, p % 2, 4, :], ALU.mult).then_inc(S("rw_bonus_taken"), 1)
                U = Ur[p % 2]
                dve.wait_ge(S("rw_mask"), 7 * p + 1)
                V_.tensor_tensor(U, over(C("ident"), 4), AMr[0], ALU.subtract)
                id0 = over(C("ident", META, META), 2)
                V_.tensor_tensor(U0[p % 2][0:META], id0, AM0[0][0:META], ALU.subtract)
                dve.wait_ge(S("rw_first"), p + 1)
                V_.tensor_tensor(T0[0:META], id0, bank[3][0:META, 0:2 * META].rearrange("p (a b) -> p a b", a=2), ALU.subtract)
                V_.tensor_tensor(Tr, over(C("ident"), 4), bank[2][:, :].rearrange("p (a b) -> p a b", a=4), ALU.subtract)\
                    .then_inc(S("rw_step"), 1)
                dve.wait_ge(S("rw_step"), 7 * p + 1)
                for l in range(1, LEVELS):
                    dve.wait_ge(S("rw_delta"), 6 * p + l)
                    if l < 4:
                        for M, b in ((T0, 3), (U0[p % 2], 4)):
                            V_.tensor_tensor(M[0:META], M[0:META], bank[b][0:META, 256:256 + 2 * META].rearrange("p (a b) -> p a b", a=2),
                                             ALU.subtract)
                    if l < LEVELS - 1:
                        V_.tensor_tensor(parts(Tr, l, 0), parts(Tr, l, 0), packed(bank[3][:, 0:256], l), ALU.subtract)
                    V_.tensor_tensor(parts(U, l, 1), parts(U, l, 1), packed(bank[4][:, 0:256], l), ALU.subtract).then_inc(S("rw_step"), 1)
                    if p >= 1 and l in (2, 4):
                        chain_state(p - 1, l // 2 - 1)
                    if l == 1:
                        dve.wait_ge(S("proj_taken"), p0 + 8 * p + R_G + 1)
                        V_.scalar_tensor_tensor(out=gate[:, p % 3, :], in0=gtanh, scalar=1.0, in1=gate[:, p % 3, :],
                                                op0=ALU.add, op1=ALU.mult).then_inc(S("rw_gated"), 1)
                    elif p + 1 < PAIRS:
                        (feats_decay, feats_key, feats_norm, feats_products, feats_receptance)[l - 2](p + 1)
                    dve.wait_ge(S("rw_step"), 7 * p + 1 + l)
            scale_norm(PAIRS - 2)
            finish(PAIRS - 2)
            for c in range(2):
                chain_state(PAIRS - 1, c)
            scale_norm(PAIRS - 1)
            finish(PAIRS - 1)
            n1 = p0 + 8 * PAIRS

            def post(layer, out_signal):
                norm([mo[:, t, :] for t in range(DT)], [mo[:, t, :] for t in range(DT)],
                     [V("norm_post_2", 8 * layer + t) for t in range(DT)], T2, None)
                V_.tensor_tensor(h[:, :, :], h[:, :, :], mo, ALU.add).then_inc(S(out_signal), 1)

            post(0, "h_ready")
            dve.wait_ge(S("h_ready"), 4)
            norm([u[:, t, :] for t in range(DT)], [h[:, t, :] for t in range(DT)],
                 [V("norm_pre_2", 8 + t) for t in range(DT)], T2, "u_ready")
            norm([cqn[:, t, :] for t in range(4)], [cq[:, t, :] for t in range(4)],
                 [V("mla_q_norm_2", t) for t in range(4)], T2, "cq_done")
            norm([ckvn[:, t, :] for t in range(2)], [ckv[:, t, :] for t in range(2)],
                 [V("mla_kv_norm_2", t) for t in range(2)], T2, "lat_ready")
            cosb, sinb = C("cos", T2), C("sin", T2)
            dve.wait_ge(S("kr_swapped"), 1)
            link(V_.tensor_tensor(kr[:, 1, :], kr[:, 0, :], cosb, ALU.mult))
            link(V_.tensor_tensor(kr[:, 0, :], bank[3][:, 0:T2], sinb, ALU.mult))
            V_.tensor_tensor(kr[:, 1, :], kr[:, 1, :], kr[:, 0, :], ALU.add).then_inc(S("kr_ready"), 1)

            def rotate_q(hd):
                q = qr[:, (hd // 2) % 2]
                dve.wait_ge(S("qr_swapped"), hd // 2 + 1)
                link(V_.tensor_tensor(q[:, 1, :], q[:, 0, :], cosb, ALU.mult))
                link(V_.tensor_tensor(q[:, 0, :], bank[2][:, 0:T2], sinb, ALU.mult))
                V_.tensor_tensor(q[:, 2, :], q[:, 1, :], q[:, 0, :], ALU.add).then_inc(S("qr_ready"), 1)

            def gated(hd):
                g = hin[:, hd % 2, 2, :]
                dve.wait_ge(S("proj_taken"), gate_taken[hd])
                V_.scalar_tensor_tensor(out=g, in0=atanh, scalar=1.0, in1=g, op0=ALU.add, op1=ALU.mult).then_inc(S("at_gated"), 1)

            def output(hd):
                dve.wait_ge(S("at_o"), hd + 1)
                dve.wait_ge(S("at_gated"), hd + 1)
                V_.scalar_tensor_tensor(out=om[:, hd, :], in0=bank[7][:, 0:T2], scalar=0.5, in1=hin[:, hd % 2, 2, :],
                                        op0=ALU.mult, op1=ALU.mult).then_inc(S("at_o_taken"), 1)

            first_head = n1 + 8 + 7 + 12
            gate_taken = [first_head + 3 * (hd + 1) + hd // 2 + 1 for hd in range(AH)]
            rotate_q(0)
            for hd in range(AH):
                pb = hd % 2
                dve.wait_ge(S("at_scores"), hd + 1)
                if hd >= 2:
                    dve.wait_ge(S("at_pT"), hd - 1)
                V_.tensor_tensor(pr[:, pb, :], bank[3][:, 0:384], C("amask", 384), ALU.add)
                V_.tensor_tensor(pr2[0:META, pb, :], bank[4][0:META, 0:T2], C("amask2", T2, META), ALU.add).then_inc(S("at_masked"), 1)
                dve.wait_ge(S("at_masked"), hd + 1)
                V_.reduce_max(nm[:, pb, 0:1], pr[:, pb, 0:128], axis=AX_X)
                V_.reduce_max(nm[:, pb, 1:2], pr[:, pb, 128:384], axis=AX_X)
                link(V_.reduce_max(nm[0:META, pb, 2:3], pr2[0:META, pb, :], axis=AX_X))
                V_.tensor_scalar(nm[:, pb, 3:5], nm[:, pb, 0:2], -SCALE_A, None, ALU.mult)
                V_.tensor_scalar(nm[0:META, pb, 5:6], nm[0:META, pb, 2:3], -SCALE_A, None, ALU.mult).then_inc(S("at_max"), 1)
                if hd + 1 < AH and (hd + 1) % 2 == 0:
                    rotate_q(hd + 1)
                if hd >= 1:
                    output(hd - 1)
                gated(hd)
                dve.wait_ge(S("at_exp"), hd + 1)
                V_.reciprocal(nm[:, pb, 9:11], nm[:, pb, 6:8])
                link(V_.reciprocal(nm[0:META, pb, 11:12], nm[0:META, pb, 8:9]))
                V_.tensor_scalar(pr[:, pb, 0:128], pr[:, pb, 0:128], nm[:, pb, 9:10], None, ALU.mult)
                V_.tensor_scalar(pr[:, pb, 128:384], pr[:, pb, 128:384], nm[:, pb, 10:11], None, ALU.mult)
                V_.tensor_scalar(pr2[0:META, pb, :], pr2[0:META, pb, :], nm[0:META, pb, 11:12], None, ALU.mult).then_inc(S("at_probs"), 1)
            output(AH - 1)
            post(1, "out_ready")

        @block.gpsimd
        def _(pool):
            for g in range(4):
                pool.wait_ge(S("dn_A"), g + 1)
                for l in range(LEVELS):
                    if l >= 2:
                        pool.wait_ge(S("dn_y"), 6 * g + l - 2) if l >= 3 else pool.wait_ge(S("dn_step"), 7 * g + 1)
                    elif g >= 1:
                        pool.wait_ge(S("dn_out"), g)
                    nc.gpsimd.tensor_tensor(AMd[:, l % 2], ATd, over(levels[:, l, :], 4), ALU.mult).then_inc(S("dn_mask"), 1)
            for p in range(PAIRS):
                pool.wait_ge(S("rw_grams_taken"), 3 * p + 2)
                for l in range(LEVELS):
                    if l == 2:
                        pool.wait_ge(S("rw_step"), 7 * p + 1)
                    if l >= 3:
                        pool.wait_ge(S("rw_y"), 6 * p + l - 2)
                    if l == 0:
                        nc.gpsimd.tensor_tensor(AMr[0], GG[:, p % 2, :, 0:P], over(levels[:, 0, :], 4), ALU.mult)
                        pool.wait_ge(S("rw_grams_taken"), 3 * p + 3)
                    if l < 4:
                        ins = nc.gpsimd.tensor_tensor(AM0[l % 2][0:META], G0[0:META, p % 2, :, 0:META],
                                                over(levels[0:META, l, 0:META], 2), ALU.mult)
                    if l >= 1:
                        ins = nc.gpsimd.tensor_tensor(AMr[l % 2], GG[:, p % 2, :, 0:P], over(levels[:, l, :], 4), ALU.mult)
                    ins.then_inc(S("rw_mask"), 1)
                    if l >= 1:
                        if l >= 3:
                            pool.wait_ge(S("rw_delta"), 6 * p + l - 2)
                        nc.gpsimd.memset(parts(Yr[l % 2], l, 1), 0.0).then_inc(S("rw_y_zero"), 1)


DN_SCALE = 128 ** -0.5


def gemm_sizes():
    n = [DT] * 8 + [0, 4 * DT] * 2 + [DT] * 56 + [DT] * 24 + [DT] * (2 * FT) + [FT] * 8
    n += [DT]
    for p in range(PAIRS):
        n += [DT, 0, 0, 0, DT, DT, 0, DT]
    n += [IT] * 8 + [DT] * 7 + [0, 0, 8] * 4
    for hd in range(AH):
        n += ([4] if hd % 2 == 0 else []) + [4, 2, DT]
    return n + [IT] * 8


def kernel(**inputs):
    import concourse.bacc as _bacc
    from concourse.bass_utils import run_bass_kernel_spmd as _run

    a = {k: np.asarray(v) for k, v in inputs.items()}
    two = {k: (v[0] if v.ndim == 3 else v) for k, v in a.items()}
    stream = np.zeros((NCHUNKS, P, CB, P), np.float32)
    for b, (w, r0, pieces) in enumerate(weight_order()):
        at = 0
        for c0, n in pieces:
            stream[b // CB, :, b % CB, at:at + n] = two[w][r0:r0 + P, c0:c0 + n]
            at += n
    vecs = np.zeros((P, NVEC), np.float32)
    for name, n in VECTORS:
        if name == "a_log":
            vecs[:H1, VOFF[name]] = a["dn_a_log"].reshape(-1)
        elif name == "dt_bias":
            vecs[:H1, VOFF[name]] = a["dn_dt_bias"].reshape(-1)
        else:
            vecs[:, VOFF[name]:VOFF[name] + n] = a[name].reshape(n, P).T
    consts = np.concatenate([v.astype(np.float32) for v in CONST.values()], axis=1)
    arrays = {
        "xT": a["x"].reshape(T1, DT, P).transpose(2, 1, 0),
        "metaT": a["meta_tokens_2"].reshape(META, DT, P).transpose(2, 1, 0),
        "wstream": stream.reshape(NCHUNKS, P, CB * P),
        "vecs": vecs,
        "consts": consts,
        "decays": decay_table(),
        "wdbda": two["w_in"][:, O_DB:O_DB + 16].reshape(DT, P, 16).transpose(1, 0, 2).reshape(P, DT * 16),
        "wlora": np.concatenate([a["rwkv_w2_2"][0], a["rwkv_a2_2"][0]], axis=0),
    }
    arrays = {k: np.ascontiguousarray(v) for k, v in arrays.items()}
    nc = _bacc.Bacc("TRN2", target_bir_lowering=False, num_devices=1, dynamic_dma_scratch_size=1024)
    args = [nc.dram_tensor(k, v.shape, F32, kind="ExternalInput").ap() for k, v in arrays.items()]
    out = nc.dram_tensor("outT", (P, DT, T1), F32, kind="ExternalOutput").ap()
    build(nc, *args, out)
    r = _run(nc, [arrays], core_ids=[0])
    got = np.asarray(r.results[0]["outT"])
    return np.ascontiguousarray(got.transpose(2, 1, 0).reshape(1, T1, D))
```

```python
from contextlib import ExitStack

import numpy as np

import concourse.bass as bass
from concourse import mybir

F32 = mybir.dt.float32
F32R = mybir.dt.float32r
ALU = mybir.AluOpType
ACT = mybir.ActivationFunctionType
AX_X = mybir.AxisListType.X

P = 128
D = 1024
DT = D // P
T1 = 256
META = 16
T2 = T1 + META
H1 = 8
CH = 128
DFF = 2816
FT = DFF // P
RH = 32
RN = 64
PAIRS = RH // 2
RCH = [(0, META), (META, CH), (META + CH, CH)]
INNER = 2048
IT = INNER // P
AH = 16
LEVELS = 7
EPS = 1e-6
GN_EPS = 1e-5
GN_EPS_2 = 64e-5
DECAY_C = float(np.exp(-0.5))
SCALE_A = float(192 ** -0.5)

ARENA = 31860
AT_QK, AT_SCORES, AT_COLS = 14408, 20552, 26104
MLA_END = 16240
FFN_END = 2064 + (FT + DT) * T1
CB = 16
UB = 8
HALVES = 3
SLOTS = 6

SPLITS = (512, 512, 1024, 1024, 1024, 1024, 1024, 1024, 8, 8, 1024, 1024)
OFF = [int(v) for v in np.cumsum((0,) + SPLITS)]
O_RQ, O_RK, O_RV, O_RG, O_DQ, O_DK, O_DV, O_DZ, O_DB, O_DA, O_GR, O_GD = OFF[:12]
RW_G, RW_WLO = 3 * INNER, 4 * INNER
MLA_CKV, MLA_ROPE, MLA_G = 512, 768, 832


def weight_order():
    def tile(w, k, m, off=0):
        return (w, k * P, [(off + m * P, P)])

    def outs(w, off, ms, kt):
        return [tile(w, k, m, off) for m in ms for k in range(kt)]

    def wide(w, k, off):
        return [(w, k * P, [(off + j * P, P)]) for j in range(4)]

    order = []
    for off, n in ((O_RQ, 4), (O_RK, 4)):
        order += outs("w_in", off, range(n), DT)
    for g in range(2):
        for k in range(DT):
            order += wide("w_in", k, O_RV + 512 * g)
    for off in (O_DK, O_DQ, O_DV, O_RG, O_DZ, O_GR, O_GD):
        order += outs("w_in", off, range(8), DT)
    order += outs("w_ret_br", 0, range(8), DT)
    order += outs("w_dn_br", 0, range(8), DT)
    order += outs("w_o", 0, range(8), DT)
    for m in range(FT):
        order += outs("w_up", 0, [m], DT) + outs("w_up", DFF, [m], DT)
    order += outs("w_down", 0, range(8), FT)
    order += [("rwkv_w_in_2", k * P, [(RW_WLO, P)]) for k in range(DT)]
    for p in range(PAIRS):
        for off in (INNER, 0, 2 * INNER, RW_G):
            order += outs("rwkv_w_in_2", off, [p], DT)
    order += outs("rwkv_w_out_2", 0, range(8), IT)
    order += outs("mla_w_in_2", MLA_CKV, range(2), DT)
    order += [("mla_w_in_2", k * P, [(MLA_ROPE, 64), (MLA_ROPE, 64)]) for k in range(DT)]
    order += outs("mla_w_in_2", 0, range(4), DT)
    for g in range(4):
        for k in range(2):
            order += [("mla_w_kv_up_2", k * P, [((4 * g + j) * 256 + 128, P)]) for j in range(4)]
    for h in range(AH):
        if h % 2 == 0:
            order += [("mla_w_q_up_2", k * P, [(h * 192 + 128, 64), (h * 192 + 320, 64)]) for k in range(4)]
        order += [("mla_w_q_up_2", k * P, [(h * 192, P)]) for k in range(4)]
        order += [("mla_w_kv_up_2", k * P, [(h * 256, P)]) for k in range(2)]
        order += outs("mla_w_in_2", MLA_G, [h], DT)
    order += outs("mla_w_out_2", 0, range(8), IT)
    return order


R_K, R_W, R_A, R_R, R_KK, R_V, R_BONUS, R_G = range(8)
RW_OUTS = (8, 1, 1, 8, 1, 8, 1, 8)
RW_AHEAD = 8 + 1 + 1 + 1 + 8 + 3
FILL = {"start1": 2, "start2": 3, "bonus": 1, "grams": 4, "gram0": 4, "first": 4}
for _l in range(1, LEVELS):
    FILL.update({f"t{_l}": 2, f"y{_l}": 0, f"delta{_l}": 1})
assert sum(FILL.values()) == sum(RW_OUTS), sum(FILL.values())


def fill_end(p, slot):
    names = list(FILL)
    n = RW_AHEAD + sum(RW_OUTS) * p + sum(FILL[x] for x in names[:names.index(slot) + 1])
    return min(n, sum(RW_OUTS) * PAIRS)


def outs_at(n):
    q, r = divmod(n, sum(RW_OUTS))
    return 8 * q + sum(1 for i in range(8) if sum(RW_OUTS[:i + 1]) <= r)


DN_BLOCKS = (8 + 8) * DT // 4
DN_FILL = {"keys": 3, "grams": 5, "first": 1}
for _l in range(1, LEVELS):
    DN_FILL.update({f"t{_l}": 1, f"y{_l}": 1, f"delta{_l}": 1})
DN_FILL.update({"wv": 1, "s": 1, "v1": 1, "o": 1, "var": 1})
assert sum(DN_FILL.values()) == DN_BLOCKS, sum(DN_FILL.values())


def dn_fill_end(g, slot):
    names = list(DN_FILL)
    return DN_BLOCKS * g + sum(DN_FILL[x] for x in names[:names.index(slot) + 1])


NBLOCKS = len(weight_order())
NCHUNKS = -(-NBLOCKS // CB)

VECTORS = [("g_mix", 8), ("ret_norm_g", 8), ("dn_conv_w", 96), ("dn_norm_g", 1), ("g_ffn", 8),
           ("ffn_conv_w", 132), ("ffn_conv_b", 44), ("g_final", 8), ("norm_pre_2", 16), ("norm_post_2", 16),
           ("rwkv_mu_2", 48), ("rwkv_w0_2", 16), ("rwkv_a0_2", 16), ("rwkv_k_k_2", 16), ("rwkv_k_a_2", 16),
           ("rwkv_r_k_2", 16), ("rwkv_ln_w_2", 16), ("rwkv_ln_b_2", 16), ("mla_q_norm_2", 4),
           ("mla_kv_norm_2", 2), ("a_log", 1), ("dt_bias", 1)]
VOFF, _at = {}, 0
for _name, _n in VECTORS:
    VOFF[_name] = _at
    _at += _n
NVEC = _at


def constants():
    f = np.float32
    i, j = np.arange(P)[None, :], np.arange(P)[:, None]
    out = {"ident": np.eye(P), "ones": np.ones((P, P))}
    out["eps"] = np.broadcast_to(np.array([EPS, GN_EPS, GN_EPS_2]), (P, 3))
    out["mean128"] = np.full((P, P), 1 / 128)
    out["center128"] = np.eye(P) - 1 / 128
    half = (i // 64) == (j // 64)
    out["ones64"] = half * 1.0
    out["mean64"] = half / 64
    out["center64"] = np.eye(P) - half / 64
    out["perm"] = ((i ^ 32) == j) * 1.0
    out["strict"] = (i > j) * 1.0
    out["causal"] = (i >= j) * 1.0
    lv = np.zeros((LEVELS, P, P))
    for l in range(LEVELS):
        s = 1 << l
        lv[l] = ((i // s) % 2 == 1) & ((j // s) == (i // s) - 1)
    out["levels"] = lv.transpose(1, 0, 2).reshape(P, -1)
    sel = np.zeros((P, H1, P))
    for h in range(H1):
        sel[h, h] = 1
    out["sel"] = sel.reshape(P, -1)
    for name, n in (("mask_rw", P), ("mask_rw0", META)):
        m = np.zeros((P, 4, n))
        m[:n, 0] = m[:n, 2] = (i > j)[:n, :n]
        m[:n, 3] = (i >= j)[:n, :n]
        m[:, 1] = -m[:, 3]
        out[name] = m.reshape(P, -1)
    starts = [t for t, _ in RCH]
    out["reset"] = np.broadcast_to(~np.isin(np.arange(T2), starts) * 1.0, (P, T2))
    inv = (f(10000.0) ** (-np.arange(0, 64, 2, dtype=f) / f(64))).astype(f)
    lane = np.arange(P) % 64
    ang = (np.arange(T2, dtype=f)[None, :] * inv[lane % 32][:, None]).astype(f).astype(np.float64)
    sign = np.where(lane < 32, -1.0, 1.0)[:, None]
    out["cos"], out["sin"] = np.cos(ang), np.sin(ang) * sign
    neg = -3.0e38
    m = np.zeros((P, 384))
    m[:, 0:128] = np.where(j >= i, 0, neg)
    m[:, 256:384] = m[:, 0:128]
    out["amask"] = m
    m = np.zeros((P, T2))
    m[:META, 256:] = np.where(j >= i, 0, neg)[:META, :META]
    out["amask2"] = m
    return out


def decay_table():
    g = 1.0 - 2.0 ** (-5.0 - np.arange(H1, dtype=np.float32))
    lg = np.log(g.astype(np.float64))
    d = np.arange(T1)[None, :] - np.arange(P)[:, None]
    t = np.where(d >= 0, np.exp(lg[:, None, None] * np.maximum(d, 0)), 0) * 0.125
    return t.transpose(1, 0, 2).reshape(P, -1).astype(np.float32)


CONST = constants()
COFF, _at = {}, 0
for _name, _v in CONST.items():
    COFF[_name] = _at
    _at += _v.shape[1]
NCONST = _at


def build(nc, xT, metaT, wstream, vecs, consts, decays, wdbda, wlora, outT):
    ctx = ExitStack()
    with ctx:
        def sb(name, shape):
            return ctx.enter_context(nc.sbuf_tensor(name, shape, F32))

        sems = {}

        def S(name):
            if name not in sems:
                sems[name] = ctx.enter_context(nc.semaphore(name))
            return sems[name]

        loaded = [S(f"weights_loaded{i}") for i in range(SLOTS)]

        ring = sb("ring", [P, SLOTS * CB * P])
        h = sb("h", [P, DT, T2])
        u = sb("u", [P, DT, T2])
        vec = sb("vec", [P, NVEC])
        con = sb("con", [P, NCONST])
        sq = sb("sq", [P, DT, T2])
        sd = sb("sd", [P, T2])
        rs = sb("rs", [P, T2])
        with ExitStack() as over_arena:
            arena = over_arena.enter_context(nc.sbuf_tensor("arena", [P, ARENA], F32))
        def part(name, shape, dtype=F32R):
            return over_arena.enter_context(nc.sbuf_tensor(name, shape, dtype))

        with ExitStack() as over_arena:
            part("up_to_qk", [P, AT_QK], F32)
            in_hi = part("in_hi", [P, DT, T1])
            part("up_to_scores", [P, AT_SCORES - AT_QK - DT * T1], F32)
            w_lo1 = part("w_lo1", [P, HALVES, UB * P])
            part("up_to_cols", [P, AT_COLS - AT_SCORES - HALVES * UB * P], F32)
            in_lo = part("in_lo", [P, DT, T1])
            w_hi1 = part("w_hi1", [P, HALVES, UB * P])
        with ExitStack() as over_arena:
            part("arena_start", [P, FFN_END], F32)
            w_hi2, w_lo2 = part("w_hi2", [P, HALVES, UB * P]), part("w_lo2", [P, HALVES, UB * P])
            u_hi, u_lo = part("u_hi", [P, DT, T1]), part("u_lo", [P, DT, T1])
            prod_hi, prod_lo = part("prod_hi", [P, FT, T1]), part("prod_lo", [P, FT, T1])
        with ExitStack() as over_arena:
            part("arena_start2", [P, MLA_END], F32)
            w_hi3, w_lo3 = part("w_hi3", [P, HALVES, UB * P]), part("w_lo3", [P, HALVES, UB * P])
            cqn_hi, cqn_lo = part("cqn_hi", [P, 4, T2]), part("cqn_lo", [P, 4, T2])
            ckvn_hi, ckvn_lo = part("ckvn_hi", [P, 2, T2]), part("ckvn_lo", [P, 2, T2])
            u2_hi, u2_lo = part("u2_hi", [P, DT, T2]), part("u2_lo", [P, DT, T2])
        taken = [0]

        def area(at, *dims):
            n = int(np.prod(dims))
            assert at + n <= ARENA, (at, n)
            v = arena[:, at:at + n]
            if len(dims) == 2:
                v = v.rearrange("p (a b) -> p a b", a=dims[0])
            elif len(dims) == 3:
                v = v.rearrange("p (a b c) -> p a b c", a=dims[0], b=dims[1])
            elif len(dims) == 4:
                v = v.rearrange("p (a b c d) -> p a b c d", a=dims[0], b=dims[1], c=dims[2])
            taken[0] = at + n
            return v

        raw = area(0, 24, T1 + 3)
        dz, gr, gd = area(0, 8, T1), area(2048, 8, T1), area(4096, 8, T1)
        conv = area(6216, 24, T1)
        qkraw = area(taken[0], 8, T1)
        ro = qkraw
        assert taken[0] == AT_QK
        qk = area(taken[0], 8, T1)
        vtok = area(taken[0], 2, D)
        rgate = area(taken[0], 8, T1)
        assert taken[0] == AT_SCORES
        sT = area(taken[0], 2, 384)
        rn2 = area(taken[0], 512)
        sq2 = area(taken[0], 512)
        decay = area(taken[0], 8, T1)
        wdb = area(taken[0], 8, 16)
        rows = area(taken[0], 6, T1)
        cols = area(taken[0], 48)
        assert taken[0] == AT_COLS
        base = 6216 + 6144 + 2048
        Em = area(base, 4, P)
        Ea = area(taken[0], 4, P)
        ATd = area(taken[0], 4, P)
        attn = area(taken[0], 4, P)
        Td = area(taken[0], 4, 64)
        Ud = area(base + 5 * 512, 4, P)
        Yd = [area(taken[0], 4, P), area(26200, 4, P)]
        rn2b = area(26712, 512)
        vb = area(base + 7 * 512, 4, P)
        at_decay = 6216 + 6144 + 2048 * 4 + 768 + 1024
        AMd = area(at_decay, 2, 4, P)
        kbg = area(taken[0], 2, P)
        kdec = area(taken[0], 2, P)
        eg = area(taken[0], 2, P)
        qd = area(taken[0], 2, P)
        w1T = area(6216 + 6144 + 2048 * 4, 2, P)
        vn0 = area(taken[0], 2, P)
        S1 = area(taken[0], 2, P)
        vn1 = Em[:, 0:2, :]
        up = area(0, 4, T1 + 2)
        upc = area(1040, 4, T1)
        prod = area(2064, FT, T1)
        down = area(taken[0], 8, T1)
        assert taken[0] == FFN_END
        xs = area(0, 4, DT, T2)
        dx = area(8704, DT, T2)
        xs_wa = area(8704 + 2176, 2, DT, T2)
        yo = area(8704, PAIRS, T2)
        cs, dd, Wc, kk2, sdk, kp = [area(13056 + i * T2, T2) for i in range(6)]
        Wi, Wp, tk, kkn = cs, dd, kk2, sdk
        bonv = area(14688, 3, T2)
        lo = area(taken[0], T2)
        gin = area(taken[0], 2, 5, T2)
        gate = area(taken[0], 3, T2)
        wl = area(taken[0], INNER)
        ar = area(taken[0], 2, 2, T2)
        bk = area(taken[0], 2, T2)
        GG = area(taken[0], 2, 4, 4 * P)
        G0 = area(taken[0], 2, 2, 4 * META)
        tok = area(taken[0], 2, 3, 3, P)
        sqr, sdn = rs[:, :], sd[:, :]
        mids, fcol = area(taken[0], 2), area(taken[0], 3, 2)
        sqf = sq[:, :, :].rearrange("p a b -> p (a b)")
        uf = u[:, :, :].rearrange("p a b -> p (a b)")

        def four(flat, at):
            return flat[:, at:at + 4 * P].rearrange("p (a b) -> p a b", a=4)

        Ur = [four(uf, 0), four(uf, 512)]
        Tr = uf[:, 1024:1280].rearrange("p (a b) -> p a b", a=4)
        Yr = [four(uf, 1536), four(sqf, 0)]
        AMr = [four(sqf, 512), four(sqf, 1024)]
        Zs, nSA = sqf[:, 1536:1664], sqf[:, 1664:1792]
        S0 = uf[:, 2048:2176]
        ys = sqf[:, 1792:1792 + T2]
        half_bias = sqf[:, 2064:2064 + 2 * PAIRS]
        gtanh = area(taken[0], T2)
        T0, Y0, = [area(taken[0], 2, META) for _ in range(2)]
        U0 = [area(taken[0], 2, META) for _ in range(2)]
        AM0 = [area(taken[0], 2, META) for _ in range(2)]
        cq = area(0, 4, T2)
        ckv = area(taken[0], 2, T2)
        cqn = area(taken[0], 4, T2)
        ckvn = area(taken[0], 2, T2)
        kr = area(taken[0], 2, T2)
        vt = area(taken[0], 3, INNER)
        om = area(taken[0], AH, T2)
        qr = area(taken[0], 2, 3, T2)
        nm = area(taken[0], 2, 12)
        atanh = area(taken[0], T2)
        assert taken[0] <= MLA_END
        hin = uf[:, 0:6 * T2].rearrange("p (a b c) -> p a b c", a=2, b=3)
        pr = sqf[:, 0:768].rearrange("p (a b) -> p a b", a=2)
        pr2 = sqf[:, 768:768 + 2 * T2].rearrange("p (a b) -> p a b", a=2)
        pT = sqf[:, 768 + 2 * T2:768 + 2 * T2 + 864].rearrange("p (a b) -> p a b", a=2)
        mo2 = area(3808, DT, T2)
        mo = area(20000, DT, T2)

        bank = [ctx.enter_context(nc.psum_tensor(f"bank{i}", [P, 512], F32)) for i in range(8)]

        def C(name, n=P, rows_=P):
            return con[0:rows_, COFF[name]:COFF[name] + n]

        def V(name, t, rows_=P):
            return vec[0:rows_, VOFF[name] + t:VOFF[name] + t + 1]

        def eps_col(i):
            return con[:, COFF["eps"] + i:COFF["eps"] + i + 1]

        levels = con[:, COFF["levels"]:COFF["levels"] + LEVELS * P].rearrange("p (l n) -> p l n", l=LEVELS)
        sel = con[:, COFF["sel"]:COFF["sel"] + H1 * P].rearrange("p (l n) -> p l n", l=H1)

        def parts(ap, l, odd):
            return ap.rearrange("p m (b e s) -> p m b e s", e=2, s=1 << l)[:, :, :, odd, :]

        def packed(ap, l):
            return ap.rearrange("p (m b s) -> p m b s", m=4, s=1 << l)

        def over(ap, n):
            r, c = ap.shape
            return ap.unsqueeze(1).to_broadcast([r, n, c])

        block = ctx.enter_context(nc.Block())

        outputs = gemm_sizes()
        starts = np.cumsum([0] + outputs)
        assert starts[-1] == NBLOCKS, (starts[-1], NBLOCKS)
        last_reader = [int(np.searchsorted(starts, min((c + 1) * CB, NBLOCKS), side="left")) for c in range(NCHUNKS)]
        unit_start = list(range(0, int(starts[8]), UB)) + list(range(int(starts[12]), int(starts[44]), UB))
        first_units = len(unit_start)
        ffn_block = int(starts[92])
        ffn_units = (2 * FT * DT + DT * FT) // UB
        unit_start += [ffn_block + i * UB for i in range(ffn_units)]
        ffn_end = len(unit_start)
        head_block = NBLOCKS - 8 * IT - sum([4 * (hd % 2 == 0) + 4 + 2 + DT for hd in range(AH)])
        unit_start += list(range(head_block, NBLOCKS - 8 * IT, UB))
        assert head_block % CB == 0 and ffn_end % 2 == 0
        unit_at = {b: i for i, b in enumerate(unit_start)}

        def head_units(block):
            return min(ffn_end + (block - head_block) // UB + HALVES, len(unit_start))

        def down_units(b):
            return min(first_units + 2 * FT + 3 + FT * (b + 1) // UB, ffn_end)

        def ends_output(i):
            end = unit_start[i] + UB
            return int(np.searchsorted(starts, end)) if end in starts else None

        def unit_used(i):
            if end_of_unit[i] is not None:
                return S("proj_done"), end_of_unit[i]
            return S("unit_used"), sum(1 for n in range(i + 1) if end_of_unit[n] is None)

        end_of_unit = [ends_output(i) for i in range(len(unit_start))]

        def unit(i):
            at = unit_start[i] % (CB * SLOTS) * P
            hi, lo = (w_hi1, w_lo1) if i < first_units else (w_hi2, w_lo2) if i < ffn_end else (w_hi3, w_lo3)
            return ring[:, at:at + UB * P], hi[:, i % HALVES, :], lo[:, i % HALVES, :], unit_start[i] // CB

        def split_lo(engine, ops, i, signal):
            whole, hi, lo, c = unit(i)
            engine.wait_ge(loaded[c % SLOTS], 16 * (c // SLOTS + 1))
            engine.wait_ge(S("w_hi_ready"), i + 1)
            ops.tensor_tensor(lo, whole, hi.bitcast(F32), ALU.subtract).then_inc(S(signal), 1)

        @block.sync
        def _(sp):
            sp.dma_start(h[:, :, META:], xT).then_inc(S("x_loaded"), 16)
            first = COFF["mean128"]
            sp.dma_start(con[:, 0:first], consts[:, 0:first]).then_inc(S("con_first"), 16)
            sp.dma_start(vec[:, :], vecs).then_inc(S("vec_loaded"), 16)
            for c in range(NCHUNKS):
                if c == starts[44] // CB + SLOTS:
                    sp.wait_ge(S("proj_done"), 44)
                    sp.dma_start(decay, decays.rearrange("p (a b) -> p a b", a=8)).then_inc(S("decay_loaded"), 16)
                before = (c - SLOTS) * CB
                if before in unit_at:
                    sp.wait_ge(S("w_lo_even"), unit_at[before] // 2 + 1)
                    sp.wait_ge(S("w_lo_odd"), unit_at[before] // 2 + 1)
                elif c >= SLOTS:
                    sp.wait_ge(S("proj_done"), last_reader[c - SLOTS])
                sp.dma_start(ring[:, (c % SLOTS) * CB * P:(c % SLOTS + 1) * CB * P], wstream[c])\
                  .then_inc(loaded[c % SLOTS], 16)
                if c == 1:
                    sp.dma_start(con[:, first:], consts[:, first:]).then_inc(S("con_loaded"), 16)
                    sp.dma_start(wdb, wdbda.rearrange("p (a b) -> p a b", a=8)).then_inc(S("wdb_loaded"), 16)
            for half in range(2):
                sp.wait_ge(S("h_tile"), 32 + 4 * (half + 1))
                sp.dma_start(outT[:, 4 * half:4 * half + 4, :], h[:, 4 * half:4 * half + 4, META:]).then_inc(S("out_stored"), 16)
            sp.wait_ge(S("out_stored"), 32)

        @block.tensor
        def _(pe):
            blk = [0]
            pn = [0]
            seen = [-1]

            def weights(width=1):
                b = blk[0]
                c = b // CB
                if c > seen[0]:
                    seen[0] = c
                    pe.wait_ge(loaded[c % SLOTS], 16 * (c // SLOTS + 1))
                at = (b % (CB * SLOTS)) * P
                blk[0] += width
                return ring[:, at:at + width * P]

            def free_bank():
                if pn[0] >= 2:
                    pe.wait_ge(S("proj_taken"), pn[0] - 1)
                b = bank[pn[0] % 2]
                pn[0] += 1
                return b

            def project(rhs, kt, T, signal=None, base=0):
                b = free_bank()
                for k in range(kt):
                    if signal is not None:
                        pe.wait_ge(S(signal), base + k + 1)
                    ins = nc.tensor.matmul(b[:, 0:T], weights(), rhs(k), start=k == 0, stop=k == kt - 1)
                ins.then_inc(S("proj_done"), 1)

            def project_split(x_hi, x_lo, kt, signal=None, base=0, T=T1):
                b = free_bank()
                for k in range(kt):
                    j = (blk[0] - unit_start[0]) % UB
                    i = unit_at[blk[0] - j]
                    if j == 0:
                        pe.wait_ge(S(("w_lo_even", "w_lo_odd")[i % 2]), i // 2 + 1)
                    blk[0] += 1
                    if signal is not None:
                        pe.wait_ge(S(signal), base + k + 1)
                    hi, lo = [x[:, j * P:(j + 1) * P] for x in unit(i)[1:3]]
                    nc.tensor.matmul(b[:, 0:T], hi, x_hi[:, k, :], start=k == 0, stop=False)
                    nc.tensor.matmul(b[:, 0:T], hi, x_lo[:, k, :], start=False, stop=False)
                    ins = nc.tensor.matmul(b[:, 0:T], lo, x_hi[:, k, :], start=False, stop=k == kt - 1)
                    if j == UB - 1 and k != kt - 1:
                        ins.then_inc(S("unit_used"), 1)
                ins.then_inc(S("proj_done"), 1)

            def project_tokens(lhs, kt, spans):
                b0 = blk[0]
                for t, (a, n) in enumerate(spans):
                    blk[0] = b0
                    b = free_bank()
                    for k in range(kt):
                        ins = nc.tensor.matmul(b[0:n, :], lhs(k)[:, a:a + n], weights(4), start=k == 0, stop=k == kt - 1)
                    ins.then_inc(S("proj_done"), 1)

            squares = [0]

            def sum_tile(t, nt, T, slot=0):
                squares[0] += 1
                pe.wait_ge(S("norm_sq"), squares[0])
                ins = nc.tensor.matmul(bank[2][:, 0:T], C("ones"), sq[:, slot + t, 0:T], start=t == 0, stop=t == nt - 1)
                if t == nt - 1:
                    ins.then_inc(S("norm_sum"), 1)

            def norm(nt, T, slot=0):
                for t in range(nt):
                    sum_tile(t, nt, T, slot)

            def project_and_sum(rhs, kt, T):
                for m in range(DT + 2):
                    if m < DT:
                        project(rhs, kt, T)
                    if m >= 2:
                        sum_tile(m - 2, DT, T)

            pe.wait_ge(S("con_first"), 16)
            norm(DT, T1)
            uT = lambda k: u[:, k, 0:T1]
            for m in range(8):
                project_split(in_hi, in_lo, DT, None if m else "u_lo_ready")
            for _g in range(2):
                project_tokens(uT, DT, [(0, P), (P, P)])
            for _m in range(24):
                project_split(in_hi, in_lo, DT)
            pe.wait_ge(S("wdb_loaded"), 16)
            for j in range(2):
                for k in range(DT):
                    ins = nc.tensor.matmul(bank[2][0:8, j * T1:(j + 1) * T1], wdb[:, k, 8 * j:8 * j + 8], uT(k),
                                           start=k == 0, stop=k == DT - 1)
            ins.then_inc(S("dbda_done"), 1)
            for _m in range(8):
                project_split(in_hi, in_lo, DT)
            pe.wait_ge(S("proj_taken"), 8)
            pe.wait_ge(S("con_loaded"), 16)
            for b in range(8):
                ins = nc.tensor.matmul(bank[3 + b // 2][:, (b % 2) * T1:(b % 2 + 1) * T1], C("perm"), qkraw[:, b, :],
                                       start=True, stop=True)
            ins.then_inc(S("swapped"), 1)
            pe.wait_ge(S("qk_ready"), 1)

            def ret_scores(hd):
                r = slice(64 * (hd % 2), 64 * (hd % 2) + 64)
                q, k = qk[r, hd // 2, :], qk[r, 4 + hd // 2, :]
                if hd >= 2:
                    pe.wait_ge(S("ret_decayed"), hd - 1)
                nc.tensor.matmul(bank[3 + hd % 2][:, 0:256], k[:, 0:128], q, start=True, stop=True)
                nc.tensor.matmul(bank[3 + hd % 2][:, 256:384], k[:, 128:256], q[:, 128:256], start=True, stop=True)\
                    .then_inc(S("ret_scores"), 1)

            ret_scores(0)
            for hd in range(H1):
                if hd + 1 < H1:
                    ret_scores(hd + 1)
                pe.wait_ge(S("ret_decayed"), hd + 1)
                if hd >= 2:
                    pe.wait_ge(S("ret_out_taken"), hd - 1)
                o = bank[5 + hd % 2]
                nc.tensor.matmul(o[:, 0:256], vtok[:, 0, hd * P:(hd + 1) * P], sT[:, hd % 2, 0:256], start=True, stop=False)
                nc.tensor.matmul(o[:, 128:256], vtok[:, 1, hd * P:(hd + 1) * P], sT[:, hd % 2, 256:384], start=False, stop=True)\
                    .then_inc(S("ret_out"), 1)
            for g in range(4):
                pe.wait_ge(S("ret_out_taken"), 2 * g + 2)
                if g >= 1:
                    pe.wait_ge(S("ret_normed"), g)
                nc.tensor.matmul(bank[7][:, :], C("center128"), ro[:, 2 * g:2 * g + 2, :], start=True, stop=True)\
                    .then_inc(S("ret_centered"), 1)
                pe.wait_ge(S("ret_sq"), g + 1)
                nc.tensor.matmul(bank[2][:, :], C("mean128"), sq2, start=True, stop=True).then_inc(S("ret_var"), 1)
                for _m in range(2):
                    project(uT, DT, T1)

            for n in range(8):
                pe.wait_ge(S("l2_sq"), n + 1)
                nc.tensor.matmul(bank[3][:, :], C("ones"), sq2, start=True, stop=True).then_inc(S("l2_sum"), 1)
                project(uT, DT, T1)
            pe.wait_ge(S("rows_ready"), 1)
            for j, (r, c) in enumerate(((0, 0), (0, 1), (2, 0), (2, 1), (3, 0), (4, 1))):
                ins = nc.tensor.matmul(bank[3][:, 8 * j:8 * j + 8], rows[0:8, r, c * CH:(c + 1) * CH], C("ident", 8, 8),
                                       start=True, stop=True)
            ins.then_inc(S("cols_done"), 1)
            dn_filled = [0]
            dn_current = [None]

            def dn_fill(upto):
                while dn_filled[0] < upto:
                    j, k = divmod(dn_filled[0], DT)
                    if k == 0:
                        if j == 8:
                            pe.wait_ge(S("ret_gated"), 1)
                        dn_current[0] = free_bank()
                    x = u[:, k, 0:T1] if j < 8 else ro[:, k, :]
                    ins = nc.tensor.matmul(dn_current[0][:, 0:T1], weights(), x, start=k == 0, stop=k == DT - 1)
                    if k == DT - 1:
                        ins.then_inc(S("proj_done"), 1)
                    dn_filled[0] += 1

            pe.wait_ge(S("l2_done"), 8)
            for g in range(4):
                hs = (2 * g, 2 * g + 1)
                if g == 0:
                    pe.wait_ge(S("cols_taken"), 1)
                for i, hd in enumerate(hs):
                    nc.tensor.matmul(bank[2][:, i * T1:(i + 1) * T1], sel[0:8, hd, :], rows[0:8, 2, :], start=True, stop=True)
                for i, hd in enumerate(hs):
                    ins = nc.tensor.matmul(bank[3][:, i * T1:(i + 1) * T1], sel[0:8, hd, :], rows[0:8, 0, :], start=True, stop=True)
                ins.then_inc(S("dn_bcast"), 1)
                tiles = [(2 * i + c, hd, slice(c * CH, (c + 1) * CH)) for i, hd in enumerate(hs) for c in range(2)]
                for m, hd, t in tiles:
                    ins = nc.tensor.matmul(bank[4][:, m * P:(m + 1) * P], conv[:, hd, t], conv[:, hd, t], start=True, stop=True)
                ins.then_inc(S("dn_keys"), 1)
                for m, hd, t in tiles:
                    nc.tensor.transpose(bank[7][:, m * P:(m + 1) * P], conv[:, hd, t], C("ident"))
                dn_fill(dn_fill_end(g, "keys"))
                if g >= 1:
                    pe.wait_ge(S("dn_out"), g)
                for m, hd, t in tiles:
                    nc.tensor.matmul(bank[5][:, m * P:(m + 1) * P], conv[:, hd, t], conv[:, 8 + hd, t], start=True, stop=True)
                    ins = nc.tensor.transpose(bank[6][:, m * P:(m + 1) * P], conv[:, 16 + hd, t], C("ident"))
                ins.then_inc(S("dn_grams"), 1)
                dn_fill(dn_fill_end(g, "grams"))
                pe.wait_ge(S("dn_e_ready"), g + 1)
                dn_fill(dn_fill_end(g, "first"))
                for l in range(1, LEVELS):
                    pe.wait_ge(S("dn_step"), 7 * g + l)
                    for m in range(4):
                        ins = nc.tensor.transpose(bank[3][:, m * P:(m + 1) * P], Ud[:, m, :], C("ident"))
                    ins.then_inc(S("dn_t"), 1)
                    dn_fill(dn_fill_end(g, f"t{l}"))
                    pe.wait_ge(S("dn_mask"), 7 * g + l + 1)
                    pe.wait_ge(S("dn_t_taken"), 6 * g + l)
                    for m in range(4):
                        ins = nc.tensor.matmul(bank[2][:, m * 64:(m + 1) * 64], AMd[:, l % 2, m, :], Td[:, m, :], start=True, stop=True)
                    ins.then_inc(S("dn_y"), 1)
                    dn_fill(dn_fill_end(g, f"y{l}"))
                    pe.wait_ge(S("dn_y_taken"), 6 * g + l)
                    for m in range(4):
                        ins = nc.tensor.matmul(bank[4][:, m * 64:(m + 1) * 64], Yd[l % 2][:, m, :],
                                               parts(Ud[:, m:m + 1, :], l, 1)[:, 0], start=True, stop=True)
                    ins.then_inc(S("dn_delta"), 1)
                    dn_fill(dn_fill_end(g, f"delta{l}"))
                pe.wait_ge(S("dn_step"), 7 * g + 7)
                pe.wait_ge(S("dn_toks"), g + 1)
                for i in range(2):
                    nc.tensor.matmul(bank[2][:, i * P:(i + 1) * P], kbg[:, i, :], Ud[:, 2 * i + 1, :], start=True, stop=True)
                for i in range(2):
                    ins = nc.tensor.matmul(bank[2][:, (2 + i) * P:(3 + i) * P], Ud[:, 2 * i, :], vb[:, 2 * i, :], start=True, stop=True)
                ins.then_inc(S("dn_wv"), 1)
                dn_fill(dn_fill_end(g, "wv"))
                pe.wait_ge(S("dn_wv_taken"), g + 1)
                for i in range(2):
                    ins = nc.tensor.matmul(bank[3][:, i * P:(i + 1) * P], kdec[:, i, :], vn0[:, i, :], start=True, stop=True)
                ins.then_inc(S("dn_s"), 1)
                dn_fill(dn_fill_end(g, "s"))
                pe.wait_ge(S("dn_s_taken"), g + 1)
                for i in range(2):
                    nc.tensor.matmul(bank[4][:, i * P:(i + 1) * P], Ud[:, 2 * i + 1, :], vb[:, 2 * i + 1, :], start=True, stop=False)
                    ins = nc.tensor.matmul(bank[4][:, i * P:(i + 1) * P], w1T[:, i, :], S1[:, i, :], start=False, stop=True)
                ins.then_inc(S("dn_v1"), 1)
                dn_fill(dn_fill_end(g, "v1"))
                pe.wait_ge(S("dn_v1_taken"), g + 1)
                for i in range(2):
                    nc.tensor.matmul(bank[5][:, i * T1:i * T1 + P], vn0[:, i, :], attn[:, 2 * i, :], start=True, stop=True)
                    nc.tensor.matmul(bank[5][:, i * T1 + P:(i + 1) * T1], S1[:, i, :], qd[:, i, :], start=True, stop=False)
                    ins = nc.tensor.matmul(bank[5][:, i * T1 + P:(i + 1) * T1], vn1[:, i, :], attn[:, 2 * i + 1, :],
                                           start=False, stop=True)
                ins.then_inc(S("dn_o"), 1)
                dn_fill(dn_fill_end(g, "o"))
                pe.wait_ge(S("dn_o_sq"), g + 1)
                nc.tensor.matmul(bank[6][:, :], C("mean128"), sq2, start=True, stop=True).then_inc(S("dn_var"), 1)
                dn_fill(dn_fill_end(g, "var"))

            pe.wait_ge(S("dn_gated"), 4)
            for _m in range(8):
                project(lambda k: conv[:, 16 + k, :], DT, T1)
            pe.wait_ge(S("merged"), 1)
            project_and_sum(lambda k: gr[:, k, :], DT, T1)
            for m in range(2 * FT):
                project_split(u_hi, u_lo, DT, None if m else "u_lo_ready", DT)
            pe.wait_ge(S("prod_split"), FT)
            for m in range(DT + 2):
                if m < DT:
                    project_split(prod_hi, prod_lo, FT)
                if m >= 2:
                    sum_tile(m - 2, DT, T1)

            norm(DT, T2)
            pe.wait_ge(S("lerped"), 1)
            b = free_bank()
            wb = []
            for k in range(DT):
                wb.append(weights())
                for j in range(2):
                    ins = nc.tensor.matmul(b[64 * j:64 * j + 64, 0:T2], wb[k][:, 64 * j:64 * j + 64], xs_wa[:, j, k, :],
                                           start=k == 0, stop=k == DT - 1)
            ins.then_inc(S("proj_done"), 1)

            filled = [0]
            current = [None]

            def fill(upto):
                while filled[0] < upto:
                    q, k = divmod(filled[0], sum(RW_OUTS))
                    j = 0
                    while k >= RW_OUTS[j]:
                        k -= RW_OUTS[j]
                        j += 1
                    if k == 0:
                        if q == 0 and j in (R_K, R_R):
                            pe.wait_ge(S("lerped"), 2 if j == R_K else 3)
                        if q == 0 and j in (R_V, R_G):
                            pe.wait_ge(S("lerped_pool"), 1 if j == R_V else 2)
                        if j == R_KK:
                            pe.wait_ge(S("rw_kk2"), q + 1)
                        if j == R_BONUS:
                            pe.wait_ge(S("rw_feats"), q + 1)
                        current[0] = free_bank()
                    b = current[0]
                    if j in (R_W, R_A):
                        r = slice(64 * (j - R_W), 64 * (j - R_W) + 64)
                        ins = nc.tensor.matmul(b[:, 0:T2], wl[r, q * P:(q + 1) * P], lo[r, :], start=True, stop=True)
                    elif j in (R_KK, R_BONUS):
                        ins = nc.tensor.matmul(b[:, 0:T2], C("ones64"), kk2 if j == R_KK else tk, start=True, stop=True)
                    else:
                        x = xs[:, {R_K: 0, R_R: 1, R_V: 2, R_G: 3}[j], k, :]
                        ins = nc.tensor.matmul(b[:, 0:T2], weights(), x, start=k == 0, stop=k == DT - 1)
                    if k == RW_OUTS[j] - 1:
                        ins.then_inc(S("proj_done"), 1)
                    filled[0] += 1

            def grams(p, c):
                t0, n = RCH[c]
                t = slice(t0, t0 + n)
                banks = ((5, 6), (2, 3), (4, 7))[c]
                for i in range(2):
                    for j in range(2):
                        r = slice(64 * j, 64 * j + 64)
                        ins = nc.tensor.matmul(bank[banks[j]][0:n, i * 2 * n:(i + 1) * 2 * n], bk[r, i, t], ar[r, p % 2, :, t],
                                               start=True, stop=True)
                ins.then_inc(S("rw_grams"), 1)

            def to_tokens(p, c, b):
                t0, n = RCH[c]
                for j, src in enumerate((gin[:, p % 2, 4, :], bk[:, 1, :], bk[:, 0, :])):
                    ins = nc.tensor.transpose(bank[b][0:n, j * P:(j + 1) * P], src[:, t0:t0 + n], C("ident"))
                ins.then_inc(S("rw_toks"), 1)

            def gram_of(p, c, j, i):
                n = RCH[c][1]
                g = G0[0:n, p % 2, j, :] if c == 0 else GG[:, p % 2, 2 * (c - 1) + j, :]
                return g[:, i * n:(i + 1) * n]

            def chain_z(p, c):
                t0, n = RCH[c]
                t = slice(t0, t0 + n)
                if c >= 1:
                    pe.wait_ge(S("rw_state_taken"), 2 * p + c)
                    nc.tensor.matmul(bank[5][0:n, 0:P], ar[:, p % 2, 0, t], S0, start=True, stop=False)
                for j in range(2):
                    f = slice(64 * j, 64 * j + 64)
                    ins = nc.tensor.matmul(bank[5][0:n, f], gram_of(p, c, j, 2), tok[0:n, p % 2, c, 0, f],
                                           start=c == 0, stop=c == 0 or j == 1)
                ins.then_inc(S("rw_z"), 1)
                if c >= 1:
                    nc.tensor.matmul(bank[7][:, t], S0, ar[:, p % 2, 1, t], start=True, stop=False).then_inc(S("rw_s0_read"), 1)

            def chain_sa(p, c):
                n = RCH[c][1]
                pe.wait_ge(S("rw_z_taken"), 3 * p + c + 1)
                for j in range(2):
                    f = slice(64 * j, 64 * j + 64)
                    inv = U0[p % 2][0:n, j, :] if c == 0 else Ur[p % 2][:, 2 * (c - 1) + j, :]
                    ins = nc.tensor.matmul(bank[6][0:n, f], inv, Zs[0:n, f], start=True, stop=True)
                ins.then_inc(S("rw_sa"), 1)

            def chain_y(p, c):
                t0, n = RCH[c]
                t = slice(t0, t0 + n)
                pe.wait_ge(S("rw_sa_taken"), 3 * p + c + 1)
                if c < 2:
                    nc.tensor.matmul(bank[5][:, 0:P], tok[0:n, p % 2, c, 1, :], tok[0:n, p % 2, c, 0, :], start=True, stop=False)
                    nc.tensor.matmul(bank[5][:, 0:P], tok[0:n, p % 2, c, 2, :], nSA[0:n, :], start=False, stop=True)\
                        .then_inc(S("rw_state"), 1)
                for j in range(2):
                    f = slice(64 * j, 64 * j + 64)
                    nc.tensor.matmul(bank[7][f, t], nSA[0:n, f], gram_of(p, c, j, 1), start=c == 0, stop=False)
                    ins = nc.tensor.matmul(bank[7][f, t], tok[0:n, p % 2, c, 0, f], gram_of(p, c, j, 3), start=False, stop=True)
                ins.then_inc(S("rw_yc"), 1)

            def center(p):
                pe.wait_ge(S("rw_ys"), p + 1)
                nc.tensor.matmul(bank[5][:, 0:T2], C("center64"), ys, start=True, stop=True).then_inc(S("rw_centered"), 1)

            def variance(p):
                pe.wait_ge(S("rw_sq"), p + 1)
                nc.tensor.matmul(bank[6][:, 0:T2], C("mean64"), sqr, start=True, stop=True).then_inc(S("rw_var"), 1)

            pe.wait_ge(S("proj_taken"), pn[0])
            pe.wait_ge(S("wl_loaded"), 16)
            fill(RW_AHEAD)
            for p in range(PAIRS):
                fill(fill_end(p, "start1"))
                if p >= 2:
                    variance(p - 2)
                fill(fill_end(p, "start2"))
                fill(fill_end(p, "bonus"))
                pe.wait_ge(S("rw_feats"), p + 1)
                grams(p, 1)
                grams(p, 2)
                fill(fill_end(p, "grams"))
                if p >= 2:
                    pe.wait_ge(S("rw_normed"), p - 1)
                grams(p, 0)
                fill(fill_end(p, "gram0"))
                am, U, Y = AMr, Ur[p % 2], Yr
                pe.wait_ge(S("rw_grams_taken"), 3 * p + 3)
                to_tokens(p, 1, 5)
                to_tokens(p, 2, 6)
                fill(fill_end(p, "first"))
                pe.wait_ge(S("rw_toks_taken"), 3 * p + 1)
                to_tokens(p, 0, 5)
                for l in range(1, LEVELS):
                    short = l < 4
                    pe.wait_ge(S("rw_step"), 7 * p + l)
                    for m in range(4):
                        ins = nc.tensor.transpose(bank[3][:, m * P:(m + 1) * P], U[:, m, :], C("ident"))
                    if short:
                        for j in range(2):
                            ins = nc.tensor.transpose(bank[2][0:META, 320 + j * META:320 + (j + 1) * META], U0[p % 2][0:META, j, :],
                                                      C("ident", META, META))
                    ins.then_inc(S("rw_t"), 1)
                    fill(fill_end(p, f"t{l}"))
                    pe.wait_ge(S("rw_mask"), 7 * p + l + 1)
                    pe.wait_ge(S("rw_t_taken"), 6 * p + l)
                    for m in range(4):
                        ins = nc.tensor.matmul(bank[2][:, m * 64:(m + 1) * 64], am[l % 2][:, m, :], Tr[:, m, :], start=True, stop=True)
                    if short:
                        for j in range(2):
                            ins = nc.tensor.matmul(bank[2][0:META, 256 + j * META:256 + (j + 1) * META], AM0[l % 2][0:META, j, :],
                                                   T0[0:META, j, :], start=True, stop=True)
                    ins.then_inc(S("rw_y"), 1)
                    if l == 1:
                        pe.wait_ge(S("rw_toks_taken"), 3 * p + 3)
                    if p >= 1:
                        (chain_z, chain_y)[(l - 1) % 2](p - 1, (l - 1) // 2)
                    fill(fill_end(p, f"y{l}"))
                    pe.wait_ge(S("rw_y_taken"), 6 * p + l)
                    for m in range(4):
                        ins = nc.tensor.matmul(bank[4][:, m * 64:(m + 1) * 64], Y[l % 2][:, m, :],
                                               parts(U[:, m:m + 1, :], l, 1)[:, 0], start=True, stop=True)
                    if short:
                        for j in range(2):
                            ins = nc.tensor.matmul(bank[4][0:META, 256 + j * META:256 + (j + 1) * META], Y0[0:META, j, :],
                                                   U0[p % 2][0:META, j, :], start=True, stop=True)
                    ins.then_inc(S("rw_delta"), 1)
                    if p >= 1 and l % 2 == 1:
                        chain_sa(p - 1, (l - 1) // 2)
                    fill(fill_end(p, f"delta{l}"))
                if p >= 1:
                    center(p - 1)
            pe.wait_ge(S("rw_step"), 7 * PAIRS)
            variance(PAIRS - 2)
            pe.wait_ge(S("rw_pair_done"), PAIRS - 1)
            for c in range(3):
                chain_z(PAIRS - 1, c)
                chain_sa(PAIRS - 1, c)
                chain_y(PAIRS - 1, c)
            center(PAIRS - 1)
            variance(PAIRS - 1)
            pe.wait_ge(S("rw_pair_done"), PAIRS)
            project_and_sum(lambda k: yo[:, k, :], IT, T2)

            norm(DT, T2)
            u2 = lambda k: u[:, k, :]
            for m in range(2 + 1):
                project(u2, DT, T2, None if m else "u_tile", 2 * DT)
            norm(2, T2)
            for _m in range(4):
                project(u2, DT, T2)
            nc.tensor.matmul(bank[3][:, 0:T2], C("perm"), kr[:, 0, :], start=True, stop=True).then_inc(S("kr_swapped"), 1)
            pe.wait_ge(S("lat_ready"), 2)
            for g in range(4):
                project_tokens(lambda k: ckvn[:, k, :], 2, [(0, P), (P, P), (2 * P, META)])
                if g == 0:
                    norm(4, T2, 2)

            in_ready = {}

            def project_q(hd):
                if hd % 2 == 0:
                    project_split(cqn_hi, cqn_lo, 4, T=T2)
                    raw = pn[0]
                project_split(cqn_hi, cqn_lo, 4, T=T2)
                if hd % 2 == 0:
                    pe.wait_ge(S("proj_taken"), raw)
                    nc.tensor.matmul(bank[2][:, 0:T2], C("perm"), qr[:, (hd // 2) % 2, 0, :], start=True, stop=True)\
                        .then_inc(S("qr_swapped"), 1)

            def project_k(hd):
                project_split(ckvn_hi, ckvn_lo, 2, T=T2)
                in_ready[hd] = pn[0]

            def scores(hd):
                q, k = hin[:, hd % 2, 0, :], hin[:, hd % 2, 1, :]
                r = slice(64 * (hd % 2), 64 * (hd % 2) + 64)
                qrot, krot = qr[r, (hd // 2) % 2, 2, :], kr[r, 1, :]
                pe.wait_ge(S("proj_taken"), in_ready[hd])
                pe.wait_ge(S("qr_ready"), hd // 2 + 1)
                if hd >= 1:
                    pe.wait_ge(S("at_masked"), hd)
                for o, q0, nq, nk in ((bank[3][:, 0:128], 0, P, 128), (bank[3][:, 128:384], P, P, 256), (bank[4][0:META, 0:T2], 2 * P, META, T2)):
                    nc.tensor.matmul(o, q[:, q0:q0 + nq], k[:, 0:nk], start=True, stop=False)
                    ins = nc.tensor.matmul(o, qrot[:, q0:q0 + nq], krot[:, 0:nk], start=False, stop=True)
                ins.then_inc(S("at_scores"), 1)

            def transpose_probs(hd):
                pb = hd % 2
                pe.wait_ge(S("at_probs"), hd + 1)
                if hd >= 1:
                    pe.wait_ge(S("at_pT_taken"), hd)
                for o, src, n in ((bank[6][:, 0:128], pr[:, pb, 0:128], P), (bank[6][:, 128:256], pr[:, pb, 128:256], P),
                                  (bank[6][:, 256:272], pr2[0:META, pb, 0:128], META),
                                  (bank[6][:, 272:400], pr[:, pb, 256:384], P), (bank[6][:, 400:416], pr2[0:META, pb, 128:256], META),
                                  (bank[6][0:META, 416:432], pr2[0:META, pb, 256:272], META)):
                    ins = nc.tensor.transpose(o, src, C("ident", n, n))
                ins.then_inc(S("at_pT"), 1)

            def values(hd):
                pb = hd % 2
                pe.wait_ge(S("at_pT_taken"), hd + 1)
                if hd >= 1:
                    pe.wait_ge(S("at_o_taken"), hd)
                v = slice(hd * P, (hd + 1) * P)
                nc.tensor.matmul(bank[7][:, 0:T2], vt[:, 0, v], pT[:, pb, 0:T2], start=True, stop=False)
                nc.tensor.matmul(bank[7][:, P:T2], vt[:, 1, v], pT[:, pb, 272:416], start=False, stop=False)
                nc.tensor.matmul(bank[7][:, 2 * P:T2], vt[0:META, 2, v], pT[0:META, pb, 416:432], start=False, stop=True)\
                    .then_inc(S("at_o"), 1)

            pe.wait_ge(S("mla_lo"), 2 + DT + 4)
            project_q(0)
            project_k(0)
            project_split(u2_hi, u2_lo, DT, T=T2)
            pe.wait_ge(S("kr_ready"), 1)
            for hd in range(AH):
                scores(hd)
                if hd >= 1:
                    transpose_probs(hd - 1)
                if hd + 1 < AH:
                    project_q(hd + 1)
                if hd >= 1:
                    values(hd - 1)
                if hd + 1 < AH:
                    project_k(hd + 1)
                    project_split(u2_hi, u2_lo, DT, T=T2)
            transpose_probs(AH - 1)
            values(AH - 1)
            pe.wait_ge(S("at_o_taken"), AH)
            project_and_sum(lambda k: om[:, k, :], IT, T2)
            assert blk[0] == NBLOCKS

        @block.scalar
        def _(act):
            taken_n = [0]
            chain = [0]

            def link(ins):
                chain[0] += 1
                ins.then_inc(S("act_chain"), 1)
                act.wait_ge(S("act_chain"), chain[0])

            def take(out, func=ACT.Copy, rows_=slice(0, P), n=T1, **kw):
                i = taken_n[0]
                taken_n[0] += 1
                act.wait_ge(S("proj_done"), i + 1)
                nc.scalar.activation(out, bank[i % 2][rows_, 0:n], func, **kw).then_inc(S("proj_taken"), 1)

            norm_n = [0]

            def norm_square(src, slot, T):
                nc.scalar.activation(sq[:, slot, 0:T], src, ACT.Square).then_inc(S("norm_sq"), 1)

            def norm_root(T, width):
                norm_n[0] += 1
                act.wait_ge(S("norm_sum"), norm_n[0])
                nc.scalar.activation(sd[:, 0:T], bank[2][:, 0:T], ACT.Sqrt, bias=eps_col(0), scale=1.0 / width)\
                    .then_inc(S("norm_sd"), 1)

            def norm_of_h(base, T):
                for t in range(DT):
                    if base is not None:
                        act.wait_ge(S("h_tile"), base + t + 1)
                    norm_square(h[:, t, T2 - T:], t, T)
                norm_root(T, D)

            split = [0]

            def split_hi(upto):
                while split[0] < min(upto, len(unit_start)):
                    i = split[0]
                    split[0] += 1
                    whole, hi, _, c = unit(i)
                    act.wait_ge(loaded[c % SLOTS], 16 * (c // SLOTS + 1))
                    if i >= HALVES:
                        act.wait_ge(*unit_used(i - HALVES))
                    nc.scalar.activation(hi, whole, ACT.Copy).then_inc(S("w_hi_ready"), 1)

            def take_for_sum(outs, base):
                for b in range(DT + 1):
                    if b < DT:
                        if base:
                            split_hi(down_units(b))
                        take(outs[:, b, :])
                    if b >= 1:
                        act.wait_ge(S("h_tile"), base + b)
                        norm_square(h[:, b - 1, META:], b - 1, T1)
                norm_root(T1, D)

            def take_and_square(out, slot):
                i = taken_n[0]
                taken_n[0] += 1
                act.wait_ge(S("proj_done"), i + 1)
                norm_square(bank[i % 2][:, 0:T2], slot, T2)
                nc.scalar.activation(out, bank[i % 2][:, 0:T2], ACT.Copy).then_inc(S("proj_taken"), 1)

            act.dma_start(h[:, :, 0:META], metaT).then_inc(S("x_loaded"), 16)
            act.wait_ge(S("x_loaded"), 32)
            act.wait_ge(S("con_first"), 16)
            norm_of_h(None, T1)
            split_hi(1)
            for t in range(DT):
                act.wait_ge(S("u_tile"), t + 1)
                nc.scalar.activation(in_hi[:, t, :], u[:, t, 0:T1], ACT.Copy).then_inc(S("u_hi_ready"), 1)
            split_hi(HALVES)
            act.wait_ge(S("vec_loaded"), 16)
            act.wait_ge(S("con_loaded"), 16)
            for b in range(8):
                split_hi(b + HALVES)
                take(qkraw[:, b, :])
            split_hi(8 + HALVES)
            for g in range(2):
                for t in range(2):
                    take(vtok[:, t, g * 512:(g + 1) * 512], n=512)
            act.wait_ge(S("raw_zeroed"), 1)
            for b in range(24):
                split_hi(8 + b + HALVES)
                take(raw[:, b, 3:])
            for b in range(8):
                split_hi(min(32 + b + HALVES, first_units))
                take(rgate[:, b, :], ACT.Silu)
            act.wait_ge(S("dbda_done"), 1)
            nc.scalar.activation(rows[0:8, 0, :], bank[2][0:8, 0:T1], ACT.Sigmoid)
            nc.scalar.activation(rows[0:8, 1, :], bank[2][0:8, T1:2 * T1], ACT.Identity, bias=V("dt_bias", 0, 8))\
                .then_inc(S("row_y"), 1)
            act.wait_ge(S("row_abs"), 1)
            link(nc.scalar.activation(rows[0:8, 5, :], rows[0:8, 5, :], ACT.Exp))
            nc.scalar.activation(rows[0:8, 5, :], rows[0:8, 5, :], ACT.Ln, bias=1.0)
            nc.scalar.activation(sd[0:8, 0:1], V("a_log", 0, 8), ACT.Exp).then_inc(S("row_ln"), 1)
            for s in range(3):
                act.wait_ge(S("conv_done"), s + 1)
                nc.scalar.activation(conv[:, 8 * s:8 * s + 8, :], conv[:, 8 * s:8 * s + 8, :], ACT.Silu)\
                    .then_inc(S("conv_silu"), 1)
            for hd in range(H1):
                act.wait_ge(S("ret_out"), hd + 1)
                nc.scalar.activation(ro[:, hd, :], bank[5 + hd % 2][:, 0:T1], ACT.Copy).then_inc(S("ret_out_taken"), 1)
            for g in range(4):
                act.wait_ge(S("ret_centered"), g + 1)
                nc.scalar.activation(sq2, bank[7][:, :], ACT.Square).then_inc(S("ret_sq"), 1)
                act.wait_ge(S("ret_var"), g + 1)
                if g >= 1:
                    act.wait_ge(S("ret_normed"), g)
                nc.scalar.activation(rn2, bank[2][:, :], ACT.Sqrt, bias=eps_col(1)).then_inc(S("ret_sd"), 1)
                for b in (2 * g, 2 * g + 1):
                    take(dz[:, b, :])
            act.wait_ge(S("conv_silu"), 3)
            act.wait_ge(S("ret_normed"), 4)
            for n in range(8):
                nc.scalar.activation(sq2, conv[:, 2 * n:2 * n + 2, :].rearrange("p a b -> p (a b)"), ACT.Square)\
                    .then_inc(S("l2_sq"), 1)
                act.wait_ge(S("l2_sum"), n + 1)
                if n >= 2:
                    act.wait_ge(S("l2_done"), n - 1)
                nc.scalar.activation((rn2, rn2b)[n % 2], bank[3][:, :], ACT.Sqrt, bias=eps_col(0)).then_inc(S("l2_sd"), 1)
                take(gr[:, n, :])
            act.wait_ge(S("proj_taken"), taken_n[0])
            nc.scalar.activation(dz, dz, ACT.Silu).then_inc(S("dz_ready"), 1)
            act.wait_ge(S("rows_g"), 1)
            nc.scalar.activation(rows[0:8, 3, 0:CH], rows[0:8, 3, 0:CH], ACT.Exp)
            nc.scalar.activation(rows[0:8, 4, :], rows[0:8, 2, :], ACT.Exp).then_inc(S("rows_exp"), 1)
            act.wait_ge(S("cols_done"), 1)
            nc.scalar.activation(cols, bank[3][:, 0:48], ACT.Copy).then_inc(S("cols_taken"), 1)
            dn_took = [0]

            def dn_take(upto):
                while (dn_took[0] + 1) * DT <= upto:
                    b = dn_took[0]
                    take((gd, u)[b // 8][:, b % 8, 0:T1])
                    dn_took[0] += 1

            for g in range(4):
                act.wait_ge(S("dn_diff"), g + 1)
                nc.scalar.activation(Em, Em, ACT.Exp)
                for i in range(2):
                    ins = nc.scalar.activation(eg[:, i, :], bank[2][:, i * T1 + P:(i + 1) * T1], ACT.Exp)
                ins.then_inc(S("dn_exp"), 1)
                act.wait_ge(S("dn_grams"), g + 1)
                act.wait_ge(S("cols_taken"), 1)
                for i in range(2):
                    hd = 2 * g + i
                    for c in range(2):
                        m = 2 * i + c
                        nc.scalar.activation(vb[:, m, :], bank[6][:, m * P:(m + 1) * P], ACT.Copy, scale=cols[:, 8 * c + hd:8 * c + hd + 1])
                    nc.scalar.activation(kdec[:, i, :], bank[7][:, 2 * i * P:(2 * i + 1) * P], ACT.Copy, scale=cols[:, 32 + hd:33 + hd])
                    ins = nc.scalar.activation(kbg[:, i, :], bank[7][:, (2 * i + 1) * P:(2 * i + 2) * P], ACT.Copy,
                                               scale=cols[:, 40 + hd:41 + hd])
                ins.then_inc(S("dn_toks"), 1)
                dn_take(dn_fill_end(g, "first"))
                for l in range(1, LEVELS):
                    act.wait_ge(S("dn_t"), 6 * g + l)
                    nc.scalar.activation(packed(Td.rearrange("p a b -> p (a b)"), l), parts(bank[3][:, :].rearrange("p (a b) -> p a b", a=4), l, 0),
                                         ACT.Copy).then_inc(S("dn_t_taken"), 1)
                    act.wait_ge(S("dn_y"), 6 * g + l)
                    act.wait_ge(S("dn_y_zero"), 6 * g + l)
                    nc.scalar.activation(parts(Yd[l % 2], l, 0), packed(bank[2][:, 0:256], l), ACT.Copy).then_inc(S("dn_y_taken"), 1)
                    dn_take(dn_fill_end(g, f"delta{l}"))
                act.wait_ge(S("dn_wv"), g + 1)
                nc.scalar.activation(w1T, bank[2][:, 0:256], ACT.Copy)
                nc.scalar.activation(vn0, bank[2][:, 256:512], ACT.Copy).then_inc(S("dn_wv_taken"), 1)
                dn_take(dn_fill_end(g, "wv"))
                act.wait_ge(S("dn_s"), g + 1)
                nc.scalar.activation(S1, bank[3][:, 0:256], ACT.Copy).then_inc(S("dn_s_taken"), 1)
                dn_take(dn_fill_end(g, "s"))
                act.wait_ge(S("dn_v1"), g + 1)
                nc.scalar.activation(vn1, bank[4][:, 0:256], ACT.Copy).then_inc(S("dn_v1_taken"), 1)
                dn_take(dn_fill_end(g, "v1"))
                act.wait_ge(S("dn_o"), g + 1)
                nc.scalar.activation(sq2, bank[5][:, :], ACT.Square).then_inc(S("dn_o_sq"), 1)
                act.wait_ge(S("dn_var"), g + 1)
                nc.scalar.activation(rn2, bank[6][:, :], ACT.Sqrt, bias=eps_col(0)).then_inc(S("dn_sd"), 1)
                dn_take(dn_fill_end(g, "var"))
            nc.scalar.activation(gr, gr, ACT.Sigmoid)
            nc.scalar.activation(gd, gd, ACT.Sigmoid).then_inc(S("gates_ready"), 1)
            for b in range(8):
                take(sq[:, b, 0:T1])
            split_hi(first_units + HALVES)
            take_for_sum(conv, 0)
            for t in range(DT):
                act.wait_ge(S("u_tile"), DT + t + 1)
                nc.scalar.activation(u_hi[:, t, :], u[:, t, 0:T1], ACT.Copy).then_inc(S("u_hi_ready"), 1)
            act.wait_ge(S("up_zeroed"), 1)

            def up_silu(m):
                act.wait_ge(S("upc_ready"), m + 1)
                nc.scalar.activation(prod[:, m, :], upc[:, 2 * (m % 2), :], ACT.Silu).then_inc(S("up_silu"), 1)

            for m in range(FT):
                s = 2 * (m % 2)
                if m >= 2:
                    act.wait_ge(S("upc_ready"), m - 1)
                split_hi(first_units + 2 * m + 3)
                take(up[:, s, 2:])
                split_hi(first_units + 2 * m + 4)
                take(up[:, s + 1, 2:])
                if m >= 1:
                    up_silu(m - 1)
            up_silu(FT - 1)
            take_for_sum(down, DT)

            act.dma_start(wl, wlora).then_inc(S("wl_loaded"), 16)
            norm_of_h(2 * DT, T2)
            act.wait_ge(S("proj_done"), taken_n[0] + 1)
            i = taken_n[0]
            taken_n[0] += 1
            nc.scalar.activation(lo[0:64, :], bank[i % 2][0:64, 0:T2], ACT.Tanh)
            nc.scalar.activation(lo[64:128, :], bank[i % 2][64:128, 0:T2], ACT.Copy).then_inc(S("proj_taken"), 1)

            took = [0]

            def take_rwkv(q, j):
                if j == R_K:
                    if q >= 2:
                        act.wait_ge(S("rw_toks_taken"), 3 * q - 3)
                        act.wait_ge(S("rw_bonus_taken"), q - 1)
                    take(gin[:, q % 2, 2, :], n=T2)
                    act.wait_ge(S("proj_taken"), taken_n[0])
                    nc.scalar.activation(kk2, gin[:, q % 2, 2, :], ACT.Square, scale=V("rwkv_k_k_2", q)).then_inc(S("rw_kk2"), 1)
                elif j in (R_W, R_A):
                    i = j - R_W
                    take(gin[:, q % 2, i, :], ACT.Tanh, n=T2, bias=half_bias[:, i * PAIRS + q:i * PAIRS + q + 1], scale=0.5)
                elif j == R_KK:
                    if q >= 1:
                        act.wait_ge(S("rw_feats"), q)
                    take(sdk, ACT.Sqrt, n=T2)
                elif j in (R_R, R_V):
                    take(gin[:, q % 2, 3 if j == R_R else 4, :], n=T2)
                elif j == R_BONUS:
                    if q >= 3:
                        act.wait_ge(S("rw_pair_done"), q - 2)
                    take(bonv[:, q % 3, :], n=T2)
                else:
                    i = taken_n[0]
                    taken_n[0] += 1
                    act.wait_ge(S("proj_done"), i + 1)
                    nc.scalar.activation(gate[:, q % 3, :], bank[i % 2][:, 0:T2], ACT.Copy)
                    if q >= 1:
                        act.wait_ge(S("rw_gated"), q)
                    nc.scalar.activation(gtanh, bank[i % 2][:, 0:T2], ACT.Tanh, scale=0.5).then_inc(S("proj_taken"), 1)

            def take_until(n):
                while took[0] < outs_at(n):
                    take_rwkv(*divmod(took[0], 8))
                    took[0] += 1

            def exponentials(q):
                act.wait_ge(S("rw_cs"), q + 1)
                link(nc.scalar.activation(Wc, cs, ACT.Exp, scale=-DECAY_C))
                nc.scalar.activation(Wi, cs, ACT.Exp, scale=DECAY_C)
                nc.scalar.activation(fcol[:, q % 3], fcol[:, q % 3], ACT.Exp, scale=-DECAY_C)
                nc.scalar.activation(Wp, dd, ACT.Exp, scale=-DECAY_C).then_inc(S("rw_w"), 1)

            def chain_z(p, c):
                n = RCH[c][1]
                act.wait_ge(S("rw_z"), 3 * p + c + 1)
                nc.scalar.activation(Zs[0:n, :], bank[5][0:n, 0:P], ACT.Copy).then_inc(S("rw_z_taken"), 1)

            def chain_sa(p, c):
                n = RCH[c][1]
                act.wait_ge(S("rw_sa"), 3 * p + c + 1)
                if c >= 1 or p >= 1:
                    act.wait_ge(S("rw_yc"), 3 * p + c)
                nc.scalar.activation(nSA[0:n, :], bank[6][0:n, 0:P], ACT.Copy).then_inc(S("rw_sa_taken"), 1)

            def take_ys(p):
                act.wait_ge(S("rw_yc"), 3 * p + 3)
                if p >= 1:
                    act.wait_ge(S("rw_centered"), p)
                nc.scalar.activation(ys, bank[7][:, 0:T2], ACT.Copy).then_inc(S("rw_ys"), 1)

            def square(p):
                act.wait_ge(S("rw_centered"), p + 1)
                if p >= 1:
                    act.wait_ge(S("rw_var"), p)
                nc.scalar.activation(sqr, bank[5][:, 0:T2], ACT.Square).then_inc(S("rw_sq"), 1)

            def deviation(p):
                act.wait_ge(S("rw_var"), p + 1)
                if p >= 1:
                    act.wait_ge(S("rw_pair_done"), p)
                nc.scalar.activation(sdn, bank[6][:, 0:T2], ACT.Sqrt, bias=eps_col(2)).then_inc(S("rw_sd"), 1)

            act.wait_ge(S("half_bias_ready"), 1)
            take_until(10)
            exponentials(0)
            take_until(RW_AHEAD)
            for p in range(PAIRS):
                if p >= 2:
                    square(p - 2)
                take_until(fill_end(p, "start1"))
                if p >= 2:
                    deviation(p - 2)
                take_until(fill_end(p, "gram0"))
                for i, c in enumerate((1, 2, 0)):
                    n = RCH[c][1]
                    if c == 0:
                        take_until(fill_end(p, "first"))
                    act.wait_ge(S("rw_toks"), 3 * p + i + 1)
                    b = bank[(5, 6, 5)[i]]
                    nc.scalar.activation(tok[0:n, p % 2, c, 0:2, :], b[0:n, 0:256], ACT.Copy)
                    nc.scalar.activation(tok[0:n, p % 2, c, 2, :], b[0:n, 256:384], ACT.Copy, scale=-1.0)\
                        .then_inc(S("rw_toks_taken"), 1)
                for l in range(1, LEVELS):
                    act.wait_ge(S("rw_t"), 6 * p + l)
                    if l < 4:
                        nc.scalar.activation(T0[0:META].rearrange("p a b -> p (a b)"), bank[2][0:META, 320:352], ACT.Copy)
                    nc.scalar.activation(packed(Tr.rearrange("p a b -> p (a b)"), l), parts(bank[3][:, :].rearrange("p (a b) -> p a b", a=4), l, 0),
                                         ACT.Copy).then_inc(S("rw_t_taken"), 1)
                    take_until(fill_end(p, f"t{l}"))
                    act.wait_ge(S("rw_y"), 6 * p + l)
                    act.wait_ge(S("rw_y_zero"), 6 * p + l)
                    if l < 4:
                        nc.scalar.activation(Y0[0:META].rearrange("p a b -> p (a b)"), bank[2][0:META, 256:288], ACT.Copy)
                    nc.scalar.activation(parts(Yr[l % 2], l, 0), packed(bank[2][:, 0:256], l), ACT.Copy).then_inc(S("rw_y_taken"), 1)
                    if p >= 1 and l % 2 == 1:
                        chain_z(p - 1, (l - 1) // 2)
                    take_until(fill_end(p, f"y{l}"))
                    if l == 3 and p + 1 < PAIRS:
                        exponentials(p + 1)
                    if p >= 1 and l % 2 == 1:
                        chain_sa(p - 1, (l - 1) // 2)
                    take_until(fill_end(p, f"delta{l}"))
                if p >= 1:
                    take_ys(p - 1)
            square(PAIRS - 2)
            deviation(PAIRS - 2)
            for c in range(3):
                chain_z(PAIRS - 1, c)
                chain_sa(PAIRS - 1, c)
            take_ys(PAIRS - 1)
            square(PAIRS - 1)
            deviation(PAIRS - 1)
            act.wait_ge(S("rw_pair_done"), PAIRS)
            for b in range(DT):
                take_and_square(mo[:, b, :], b)
            norm_root(T2, D)

            norm_of_h(3 * DT, T2)
            for b in range(2):
                take_and_square(ckv[:, b, :], b)
            take(kr[:, 0, :], n=T2)
            norm_root(T2, 256)
            for b in range(4):
                take_and_square(cq[:, b, :], 2 + b)
            for g in range(4):
                for t, n in ((0, P), (1, P), (2, META)):
                    take(vt[0:n, t, g * 512:(g + 1) * 512], rows_=slice(0, n), n=512)
                if g == 0:
                    act.wait_ge(S("lat_ready"), 2)
                    norm_root(T2, 512)
                    split_hi(ffn_end + 1)
                    for t in range(2):
                        nc.scalar.activation(ckvn_hi[:, t, :], ckvn[:, t, :], ACT.Copy).then_inc(S("mla_hi"), 1)
                if g == 1:
                    for t in range(DT):
                        nc.scalar.activation(u2_hi[:, t, :], u[:, t, :], ACT.Copy).then_inc(S("mla_hi"), 1)
                if g == 2:
                    for t in range(4):
                        act.wait_ge(S("cq_ready"), t + 1)
                        nc.scalar.activation(cqn_hi[:, t, :], cqn[:, t, :], ACT.Copy).then_inc(S("mla_hi"), 1)
                    split_hi(ffn_end + HALVES)

            def split_ahead():
                split_hi(head_units(int(starts[taken_n[0] + 1])))

            def take_q(hd):
                if hd % 2 == 0:
                    split_ahead()
                    take(qr[:, (hd // 2) % 2, 0, :], n=T2)
                split_ahead()
                take(hin[:, hd % 2, 0, :], n=T2)

            def take_k_gate(hd):
                split_ahead()
                take(hin[:, hd % 2, 1, :], n=T2)
                split_ahead()
                if hd >= 2:
                    act.wait_ge(S("at_o_taken"), hd - 1)
                i = taken_n[0]
                taken_n[0] += 1
                act.wait_ge(S("proj_done"), i + 1)
                nc.scalar.activation(hin[:, hd % 2, 2, :], bank[i % 2][:, 0:T2], ACT.Copy)
                if hd >= 1:
                    act.wait_ge(S("at_gated"), hd)
                nc.scalar.activation(atanh, bank[i % 2][:, 0:T2], ACT.Tanh, scale=0.5).then_inc(S("proj_taken"), 1)

            def take_pT(hd):
                pb = hd % 2
                act.wait_ge(S("at_pT"), hd + 1)
                nc.scalar.activation(pT[:, pb, 0:416], bank[6][:, 0:416], ACT.Copy)
                nc.scalar.activation(pT[0:META, pb, 416:432], bank[6][0:META, 416:432], ACT.Copy).then_inc(S("at_pT_taken"), 1)

            take_q(0)
            take_k_gate(0)
            for hd in range(AH):
                pb = hd % 2
                if hd >= 1:
                    take_pT(hd - 1)
                if hd + 1 < AH:
                    take_q(hd + 1)
                act.wait_ge(S("at_max"), hd + 1)
                nc.scalar.activation(pr[:, pb, 0:128], pr[:, pb, 0:128], ACT.Exp, scale=SCALE_A, bias=nm[:, pb, 3:4], accum_out=nm[:, pb, 6:7])
                nc.scalar.activation(pr[:, pb, 128:384], pr[:, pb, 128:384], ACT.Exp, scale=SCALE_A, bias=nm[:, pb, 4:5], accum_out=nm[:, pb, 7:8])
                nc.scalar.activation(pr2[0:META, pb, :], pr2[0:META, pb, :], ACT.Exp, scale=SCALE_A, bias=nm[0:META, pb, 5:6],
                                     accum_out=nm[0:META, pb, 8:9]).then_inc(S("at_exp"), 1)
                if hd + 1 < AH:
                    take_k_gate(hd + 1)
            take_pT(AH - 1)
            for b in range(DT):
                take_and_square(mo2[:, b, :], b)
            norm_root(T2, D)

        @block.vector
        def _(dve):
            chain = [0]
            V_ = nc.vector

            def link(ins):
                chain[0] += 1
                ins.then_inc(S("dve_chain"), 1)
                dve.wait_ge(S("dve_chain"), chain[0])

            norm_n = [0]

            def norm(outs, srcs, gains, T, signal, **kw):
                norm_n[0] += 1
                dve.wait_ge(S("norm_sd"), norm_n[0])
                link(V_.reciprocal(rs[:, 0:T], sd[:, 0:T]))
                for o, s, g in zip(outs, srcs, gains):
                    ins = V_.scalar_tensor_tensor(out=o, in0=s, scalar=g, in1=rs[:, 0:T], op0=ALU.mult, op1=ALU.mult)
                    if signal is not None:
                        ins.then_inc(S(signal), 1)
                if signal is None:
                    link(ins)

            V_.memset(raw[:, :, 0:3], 0.0).then_inc(S("raw_zeroed"), 1)
            dve.wait_ge(S("vec_loaded"), 16)
            norm([u[:, t, 0:T1] for t in range(DT)], [h[:, t, META:] for t in range(DT)],
                 [V("g_mix", t) for t in range(DT)], T1, "u_tile")
            evens = [0]

            def split_even(upto):
                while 2 * evens[0] < min(upto, len(unit_start)):
                    split_lo(dve, V_, 2 * evens[0], "w_lo_even")
                    evens[0] += 1

            split_even(1)
            for t in range(DT):
                dve.wait_ge(S("u_tile"), t + 1)
                dve.wait_ge(S("u_hi_ready"), t + 1)
                V_.tensor_tensor(in_lo[:, t, :], u[:, t, 0:T1], in_hi[:, t, :].bitcast(F32), ALU.subtract).then_inc(S("u_lo_ready"), 1)
            dve.wait_ge(S("con_loaded"), 16)
            for s, first in enumerate((8, 0, 16)):
                ahead = 8 + 8 * (s + 1) + 2
                split_even(ahead)
                dve.wait_ge(S("proj_taken"), 12 + 8 * (s + 1))
                for n, tap in enumerate((3, 0, 1, 2)):
                    split_even(min(ahead + 2 * n + 2, first_units))
                    for b in range(8):
                        w = V("dn_conv_w", tap * 24 + first + b)
                        src, dst = raw[:, 8 * s + b, tap:tap + T1], conv[:, 8 * s + b, :]
                        if tap == 3:
                            ins = V_.tensor_scalar(dst, src, w, None, ALU.mult)
                        else:
                            ins = V_.scalar_tensor_tensor(out=dst, in0=src, scalar=w, in1=dst, op0=ALU.mult, op1=ALU.add)
                    if tap != 2:
                        link(ins)
                ins.then_inc(S("conv_done"), 1)
            dve.wait_ge(S("row_y"), 1)
            link(V_.tensor_scalar(rows[0:8, 5, :], rows[0:8, 1, :], -1.0, None, ALU.mult))
            link(V_.tensor_tensor(rows[0:8, 5, :], rows[0:8, 5, :], rows[0:8, 1, :], ALU.min))
            V_.tensor_scalar(rows[0:8, 1, :], rows[0:8, 1, :], 0.0, None, ALU.max).then_inc(S("row_abs"), 1)
            dve.wait_ge(S("swapped"), 1)
            cosb, sinb = C("cos", T1), C("sin", T1)
            link(V_.tensor_tensor(qk, qkraw, over(cosb, 8), ALU.mult))
            for g in range(4):
                ins = V_.tensor_tensor(qkraw[:, 2 * g:2 * g + 2, :], bank[3 + g][:, :].rearrange("p (a b) -> p a b", a=2),
                                       over(sinb, 2), ALU.mult)
            link(ins)
            V_.tensor_tensor(qk, qk, qkraw, ALU.add).then_inc(S("qk_ready"), 1)
            dve.wait_ge(S("row_ln"), 1)
            dve.wait_ge(S("row_abs"), 1)
            link(V_.tensor_tensor(rows[0:8, 1, :], rows[0:8, 1, :], rows[0:8, 5, :], ALU.add))
            link(V_.tensor_scalar(rows[0:8, 1, :], rows[0:8, 1, :], sd[0:8, 0:1], -1.0, ALU.mult, ALU.mult))
            link(V_.memset(rows[0:8, 5, :], 1.0))
            for c in range(2):
                t = slice(c * CH, (c + 1) * CH)
                ins = V_.tensor_tensor_scan(rows[0:8, 2, t], rows[0:8, 5, t], rows[0:8, 1, t], 0.0, ALU.mult, ALU.add)
            link(ins)
            V_.tensor_scalar(rows[0:8, 3, 0:CH], rows[0:8, 2, 0:CH], rows[0:8, 2, CH - 1:CH], -1.0, ALU.subtract, ALU.mult)\
                .then_inc(S("rows_g"), 1)
            dve.wait_ge(S("decay_loaded"), 16)
            for hd in range(H1):
                dve.wait_ge(S("ret_scores"), hd + 1)
                if hd >= 2:
                    dve.wait_ge(S("ret_out"), hd - 1)
                V_.tensor_tensor(sT[:, hd % 2, 0:256], bank[3 + hd % 2][:, 0:256], decay[:, hd, :], ALU.mult)
                V_.tensor_tensor(sT[:, hd % 2, 256:384], bank[3 + hd % 2][:, 256:384], decay[:, hd, 0:128], ALU.mult)\
                    .then_inc(S("ret_decayed"), 1)
            for g in range(4):
                dve.wait_ge(S("ret_sd"), g + 1)
                link(V_.reciprocal(rn2, rn2))
                for i in range(2):
                    hd = 2 * g + i
                    ins = V_.scalar_tensor_tensor(out=ro[:, hd, :], in0=bank[7][:, i * T1:(i + 1) * T1], scalar=V("ret_norm_g", hd),
                                                  in1=rn2[:, i * T1:(i + 1) * T1], op0=ALU.mult, op1=ALU.mult)
                ins.then_inc(S("ret_normed"), 1)
            dve.wait_ge(S("ret_normed"), 4)
            dve.wait_ge(S("proj_taken"), 44)
            V_.tensor_tensor(ro, ro, rgate, ALU.mult).then_inc(S("ret_gated"), 1)
            for s, sc in ((0, 1.0), (1, float(DN_SCALE))):
                for g in range(4):
                    n = 4 * s + g
                    dve.wait_ge(S("l2_sd"), n + 1)
                    rn = (rn2, rn2b)[n % 2]
                    link(V_.reciprocal(rn, rn))
                    cc = conv[:, 8 * s + 2 * g:8 * s + 2 * g + 2, :]
                    V_.scalar_tensor_tensor(out=cc, in0=cc, scalar=sc, in1=rn.rearrange("p (a b) -> p a b", a=2),
                                            op0=ALU.mult, op1=ALU.mult).then_inc(S("l2_done"), 1)
            dve.wait_ge(S("rows_exp"), 1)
            V_.scalar_tensor_tensor(out=rows[0:8, 4, :], in0=rows[0:8, 4, :], scalar=-1.0, in1=rows[0:8, 0, :],
                                    op0=ALU.mult, op1=ALU.mult).then_inc(S("rows_ready"), 1)
            dve.wait_ge(S("cols_taken"), 1)
            idd = over(C("ident"), 4)

            def dn_finish(g):
                dve.wait_ge(S("dn_sd"), g + 1)
                link(V_.reciprocal(rn2, rn2))
                for i in range(2):
                    hd = 2 * g + i
                    ins = V_.scalar_tensor_tensor(out=conv[:, 16 + hd, :], in0=bank[5][:, i * T1:(i + 1) * T1], scalar=V("dn_norm_g", 0),
                                                  in1=rn2[:, i * T1:(i + 1) * T1], op0=ALU.mult, op1=ALU.mult)
                ins.then_inc(S("dn_out"), 1)
                dve.wait_ge(S("dn_out"), g + 1)
                if g == 0:
                    dve.wait_ge(S("dz_ready"), 1)
                z = conv[:, 16 + 2 * g:18 + 2 * g, :]
                V_.tensor_tensor(z, z, dz[:, 2 * g:2 * g + 2, :], ALU.mult).then_inc(S("dn_gated"), 1)

            for g in range(4):
                dve.wait_ge(S("dn_bcast"), g + 1)
                if g >= 1:
                    dve.wait_ge(S("dn_o"), g)
                for i in range(2):
                    hd = 2 * g + i
                    for c in range(2):
                        ins = V_.tensor_scalar(Em[:, 2 * i + c, :], bank[2][:, i * T1 + c * P:i * T1 + (c + 1) * P],
                                               cols[:, 16 + 8 * c + hd:17 + 8 * c + hd], 0.0, ALU.subtract, ALU.min)
                ins.then_inc(S("dn_diff"), 1)
                if g >= 1:
                    dn_finish(g - 1)
                dve.wait_ge(S("dn_exp"), g + 1)
                link(V_.tensor_tensor(Ea, Em, over(C("strict"), 4), ALU.mult))
                V_.tensor_tensor(Ea, Ea, bank[3][:, :].rearrange("p (a b) -> p a b", a=4), ALU.mult)
                link(V_.tensor_tensor(Em, Em, over(C("causal"), 4), ALU.mult))
                dve.wait_ge(S("dn_keys"), g + 1)
                V_.tensor_tensor(ATd, bank[4][:, :].rearrange("p (a b) -> p a b", a=4), Ea, ALU.mult).then_inc(S("dn_A"), 1)
                dve.wait_ge(S("dn_grams"), g + 1)
                V_.tensor_tensor(attn, bank[5][:, :].rearrange("p (a b) -> p a b", a=4), Em, ALU.mult)
                V_.tensor_tensor(qd, conv[:, 8 + 2 * g:10 + 2 * g, CH:], eg, ALU.mult).then_inc(S("dn_e_ready"), 1)
                dve.wait_ge(S("dn_mask"), 7 * g + 1)
                V_.tensor_tensor(Ud, idd, AMd[:, 0], ALU.subtract).then_inc(S("dn_step"), 1)
                dve.wait_ge(S("dn_step"), 7 * g + 1)
                for l in range(1, LEVELS):
                    dve.wait_ge(S("dn_delta"), 6 * g + l)
                    V_.tensor_tensor(parts(Ud, l, 1), parts(Ud, l, 1), packed(bank[4][:, 0:256], l), ALU.subtract).then_inc(S("dn_step"), 1)
                    dve.wait_ge(S("dn_step"), 7 * g + 1 + l)
            dn_finish(3)
            dve.wait_ge(S("gates_ready"), 1)
            V_.tensor_tensor(gr, gr, u[:, :, 0:T1], ALU.mult)
            dve.wait_ge(S("proj_taken"), 68 + 16)
            link(V_.tensor_tensor(gd, gd, sq[:, :, 0:T1], ALU.mult))
            V_.tensor_tensor(gr, gr, gd, ALU.add).then_inc(S("merged"), 1)

            def add_to_h(outs, first, base):
                for b in range(DT):
                    if base:
                        split_even(down_units(b))
                    dve.wait_ge(S("proj_taken"), first + b + 1)
                    V_.tensor_tensor(h[:, b, META:], h[:, b, META:], outs[:, b, :], ALU.add).then_inc(S("h_tile"), 1)
                dve.wait_ge(S("h_tile"), base + DT)

            split_even(first_units + HALVES)
            add_to_h(conv, 68 + 16, 0)
            norm([u[:, t, 0:T1] for t in range(DT)], [h[:, t, META:] for t in range(DT)],
                 [V("g_ffn", t) for t in range(DT)], T1, "u_tile")
            for t in range(DT):
                dve.wait_ge(S("u_tile"), DT + t + 1)
                dve.wait_ge(S("u_hi_ready"), DT + t + 1)
                V_.tensor_tensor(u_lo[:, t, :], u[:, t, 0:T1], u_hi[:, t, :].bitcast(F32), ALU.subtract).then_inc(S("u_lo_ready"), 1)
            V_.memset(up[:, :, 0:2], 0.0).then_inc(S("up_zeroed"), 1)
            for m in range(FT + 1):
                if m < FT:
                    s = 2 * (m % 2)
                    split_even(first_units + 2 * m + 3)
                    dve.wait_ge(S("proj_taken"), 92 + 2 * m + 2)
                    if m >= 2:
                        dve.wait_ge(S("up_silu"), m - 1)
                        dve.wait_ge(S("ffn_prod"), m - 1)
                    for tap in (2, 0, 1):
                        for j in range(2):
                            w = V("ffn_conv_w", tap * 44 + j * FT + m)
                            src, dst = up[:, s + j, tap:tap + T1], upc[:, s + j, :]
                            if tap == 2:
                                ins = V_.tensor_scalar(dst, src, w, V("ffn_conv_b", j * FT + m), ALU.mult, ALU.add)
                            else:
                                ins = V_.scalar_tensor_tensor(out=dst, in0=src, scalar=w, in1=dst, op0=ALU.mult, op1=ALU.add)
                        if tap != 1:
                            link(ins)
                    ins.then_inc(S("upc_ready"), 1)
                if m >= 1:
                    dve.wait_ge(S("up_silu"), m)
                    dve.wait_ge(S("upc_ready"), m)
                    s = 2 * ((m - 1) % 2)
                    V_.tensor_tensor(prod[:, m - 1, :], prod[:, m - 1, :], upc[:, s + 1, :], ALU.mult).then_inc(S("ffn_prod"), 1)
            n0 = 92 + 2 * FT
            add_to_h(down, n0, DT)
            norm([h[:, t, META:] for t in range(DT)], [h[:, t, META:] for t in range(DT)],
                 [V("g_final", t) for t in range(DT)], T1, "h_tile")
            dve.wait_ge(S("h_tile"), 3 * DT)

            norm([u[:, t, :] for t in range(DT)], [h[:, t, :] for t in range(DT)],
                 [V("norm_pre_2", t) for t in range(DT)], T2, None)
            V_.tensor_scalar(dx[:, :, 0:1], u[:, :, 0:1], -1.0, None, ALU.mult)
            V_.tensor_tensor(dx[:, :, 1:], u[:, :, 0:T2 - 1], u[:, :, 1:], ALU.subtract).then_inc(S("dx_ready"), 1)
            dve.wait_ge(S("dx_ready"), 1)
            V_.tensor_scalar(half_bias, vec[:, VOFF["rwkv_w0_2"]:VOFF["rwkv_w0_2"] + 2 * PAIRS], 0.5, None, ALU.mult)\
                .then_inc(S("half_bias_ready"), 1)
            for row, dst in ((4, xs_wa[:, 0]), (5, xs_wa[:, 1]), (1, xs[:, 0]), (0, xs[:, 1])):
                for t in range(DT):
                    ins = V_.scalar_tensor_tensor(out=dst[:, t, :], in0=dx[:, t, :], scalar=V("rwkv_mu_2", row * 8 + t),
                                                  in1=u[:, t, :], op0=ALU.mult, op1=ALU.add)
                if row != 4:
                    ins.then_inc(S("lerped"), 1)
            dve.wait_ge(S("lerped"), 3)
            dve.wait_ge(S("lerped_pool"), 2)
            p0 = n0 + 8 + 1

            def scale_norm(p):
                dve.wait_ge(S("rw_sd"), p + 1)
                link(V_.reciprocal(sdn, sdn))
                V_.scalar_tensor_tensor(out=sdn, in0=bank[5][:, 0:T2], scalar=V("rwkv_ln_w_2", p), in1=sdn, op0=ALU.mult, op1=ALU.mult)\
                    .then_inc(S("rw_normed"), 1)

            def finish(p):
                dve.wait_ge(S("rw_normed"), p + 1)
                link(V_.scalar_tensor_tensor(out=sdn, in0=sdn, scalar=V("rwkv_ln_b_2", p), in1=bonv[:, p % 3, :], op0=ALU.add, op1=ALU.add))
                V_.scalar_tensor_tensor(out=yo[:, p, :], in0=sdn, scalar=0.5, in1=gate[:, p % 3, :], op0=ALU.mult, op1=ALU.mult).then_inc(S("rw_pair_done"), 1)

            def chain_state(p, c):
                dve.wait_ge(S("rw_state"), 2 * p + c + 1)
                if c == 1:
                    link(V_.tensor_tensor(S0, S0, bank[5][:, 0:P], ALU.add))
                elif p >= 1:
                    dve.wait_ge(S("rw_s0_read"), 2 * p)
                V_.scalar_tensor_tensor(out=S0, in0=S0 if c else bank[5][:, 0:P], scalar=fcol[:, p % 3, c:c + 1], in1=C("ones64"),
                                        op0=ALU.mult, op1=ALU.mult).then_inc(S("rw_state_taken"), 1)

            def feats_decay(q):
                sg = gin[:, q % 2, 0, :]
                dve.wait_ge(S("proj_taken"), p0 + 8 * q + R_A + 1)
                link(V_.tensor_scalar(gin[:, q % 2, 0:2, :], gin[:, q % 2, 0:2, :], 0.5, 0.5, ALU.mult, ALU.add))
                link(V_.tensor_tensor_scan(cs, C("reset", T2), sg, 0.0, ALU.mult, ALU.add))
                link(V_.tensor_copy(mids, cs[:, META + 63:META + 63 + CH + 1:CH]))
                long_cs = cs[:, META:].rearrange("p (c t) -> p c t", c=2)
                link(V_.tensor_tensor(long_cs, long_cs, mids.unsqueeze(2).to_broadcast([P, 2, CH]), ALU.subtract))
                V_.tensor_tensor(fcol[:, q % 3], cs[:, META - 1:META + CH:CH], mids, ALU.add)
                V_.tensor_tensor(dd, cs, sg, ALU.subtract).then_inc(S("rw_cs"), 1)

            def feats_key(q):
                a, k = gin[:, q % 2, 1, :], gin[:, q % 2, 2, :]
                link(V_.tensor_scalar(kp, a, 1.0, V("rwkv_k_a_2", q), ALU.subtract, ALU.mult))
                link(V_.scalar_tensor_tensor(out=kp, in0=kp, scalar=1.0, in1=k, op0=ALU.add, op1=ALU.mult))

            def feats_decayed_key(q):
                if q >= 1:
                    dve.wait_ge(S("rw_toks"), 3 * q)
                dve.wait_ge(S("rw_w"), q + 1)
                V_.tensor_tensor(bk[:, 1, :], kp, Wi, ALU.mult)

            def feats_norm(q):
                dve.wait_ge(S("proj_taken"), p0 + 8 * q + R_KK + 1)
                link(V_.tensor_scalar(kkn, sdk, 1e-12, None, ALU.max))
                link(V_.reciprocal(kkn, kkn))

            def feats_products(q):
                a, k = gin[:, q % 2, 1, :], gin[:, q % 2, 2, :]
                link(V_.scalar_tensor_tensor(out=kkn, in0=k, scalar=V("rwkv_k_k_2", q), in1=kkn, op0=ALU.mult, op1=ALU.mult))
                link(V_.tensor_tensor(bk[:, 0, :], kkn, a, ALU.mult))
                V_.tensor_tensor(bk[:, 0, :], bk[:, 0, :], Wi, ALU.mult)
                if q >= 2:
                    dve.wait_ge(S("rw_s0_read"), 2 * (q - 1))
                V_.tensor_tensor(ar[:, q % 2, 0, :], kkn, Wp, ALU.mult)

            def feats_last(q):
                feats_products(q)
                r = gin[:, q % 2, 3, :]
                dve.wait_ge(S("proj_taken"), p0 + 8 * q + R_R + 1)
                V_.scalar_tensor_tensor(out=tk, in0=r, scalar=V("rwkv_r_k_2", q), in1=kp, op0=ALU.mult, op1=ALU.mult)
                V_.tensor_tensor(ar[:, q % 2, 1, :], r, Wc, ALU.mult).then_inc(S("rw_feats"), 1)

            for part in (feats_decay, feats_key, feats_decayed_key, feats_norm, feats_last):
                part(0)
            for p in range(PAIRS):
                if p >= 2:
                    dve.wait_ge(S("rw_yc"), 3 * (p - 1))
                    scale_norm(p - 2)
                for i, c in enumerate((1, 2, 0)):
                    n = RCH[c][1]
                    dve.wait_ge(S("rw_grams"), 3 * p + i + 1)
                    for j in range(2):
                        if c == 0:
                            ins = V_.tensor_tensor(G0[0:n, p % 2, j, :], bank[5 + j][0:n, 0:4 * n], C("mask_rw0", 4 * n, n), ALU.mult)
                        else:
                            b = ((2, 3), (4, 7))[c - 1][j]
                            ins = V_.tensor_tensor(GG[:, p % 2, 2 * (c - 1) + j, :], bank[b][:, :], C("mask_rw", 4 * P), ALU.mult)
                    ins.then_inc(S("rw_grams_taken"), 1)
                if p >= 2:
                    finish(p - 2)
                dve.wait_ge(S("proj_taken"), p0 + 8 * p + R_BONUS + 1)
                V_.tensor_tensor(bonv[:, p % 3, :], bonv[:, p % 3, :], gin[:, p % 2, 4, :], ALU.mult).then_inc(S("rw_bonus_taken"), 1)
                U = Ur[p % 2]
                dve.wait_ge(S("rw_mask"), 7 * p + 1)
                V_.tensor_tensor(U0[p % 2][0:META], over(C("ident", META, META), 2), AM0[0][0:META], ALU.subtract)
                V_.tensor_tensor(U, over(C("ident"), 4), AMr[0], ALU.subtract).then_inc(S("rw_step"), 1)
                dve.wait_ge(S("rw_step"), 7 * p + 1)
                for l in range(1, LEVELS):
                    dve.wait_ge(S("rw_delta"), 6 * p + l)
                    if l < 4:
                        M = U0[p % 2][0:META]
                        V_.tensor_tensor(M, M, bank[4][0:META, 256:256 + 2 * META].rearrange("p (a b) -> p a b", a=2), ALU.subtract)
                    V_.tensor_tensor(parts(U, l, 1), parts(U, l, 1), packed(bank[4][:, 0:256], l), ALU.subtract).then_inc(S("rw_step"), 1)
                    if p >= 1 and l in (2, 4):
                        chain_state(p - 1, l // 2 - 1)
                    if l == 1:
                        dve.wait_ge(S("proj_taken"), p0 + 8 * p + R_G + 1)
                        V_.scalar_tensor_tensor(out=gate[:, p % 3, :], in0=gtanh, scalar=1.0, in1=gate[:, p % 3, :],
                                                op0=ALU.add, op1=ALU.mult).then_inc(S("rw_gated"), 1)
                    elif p + 1 < PAIRS:
                        (feats_decay, feats_key, feats_decayed_key, feats_norm, feats_last)[l - 2](p + 1)
                    dve.wait_ge(S("rw_step"), 7 * p + 1 + l)
            scale_norm(PAIRS - 2)
            finish(PAIRS - 2)
            for c in range(2):
                chain_state(PAIRS - 1, c)
            scale_norm(PAIRS - 1)
            finish(PAIRS - 1)
            n1 = p0 + 8 * PAIRS

            def post(layer):
                mixed = (mo, mo2)[layer]
                norm_n[0] += 1
                dve.wait_ge(S("norm_sd"), norm_n[0])
                link(V_.reciprocal(rs[:, :], sd[:, :]))
                for t in range(DT):
                    if t == 0:
                        dve.wait_ge(S("proj_taken"), (n1, n_all)[layer])
                    link(V_.scalar_tensor_tensor(out=mixed[:, t, :], in0=mixed[:, t, :], scalar=V("norm_post_2", 8 * layer + t),
                                                 in1=rs[:, :], op0=ALU.mult, op1=ALU.mult))
                    V_.tensor_tensor(h[:, t, :], h[:, t, :], mixed[:, t, :], ALU.add).then_inc(S("h_tile"), 1)

            n_all = len(gemm_sizes())
            n1 += 8
            post(0)
            dve.wait_ge(S("h_tile"), 4 * DT)
            norm([u[:, t, :] for t in range(DT)], [h[:, t, :] for t in range(DT)],
                 [V("norm_pre_2", 8 + t) for t in range(DT)], T2, "u_tile")
            norm([ckvn[:, t, :] for t in range(2)], [ckv[:, t, :] for t in range(2)],
                 [V("mla_kv_norm_2", t) for t in range(2)], T2, "lat_ready")
            cosb, sinb = C("cos", T2), C("sin", T2)
            dve.wait_ge(S("kr_swapped"), 1)
            link(V_.tensor_tensor(kr[:, 1, :], kr[:, 0, :], cosb, ALU.mult))
            link(V_.tensor_tensor(kr[:, 0, :], bank[3][:, 0:T2], sinb, ALU.mult))
            V_.tensor_tensor(kr[:, 1, :], kr[:, 1, :], kr[:, 0, :], ALU.add).then_inc(S("kr_ready"), 1)
            norm([cqn[:, t, :] for t in range(4)], [cq[:, t, :] for t in range(4)],
                 [V("mla_q_norm_2", t) for t in range(4)], T2, "cq_ready")
            split_even(ffn_end + 1)
            n = 0
            for full, hi, lo_, tiles in ((ckvn, ckvn_hi, ckvn_lo, 2), (u, u2_hi, u2_lo, DT), (cqn, cqn_hi, cqn_lo, 4)):
                if full is cqn:
                    dve.wait_ge(S("cq_ready"), 4)
                for t in range(tiles):
                    n += 1
                    dve.wait_ge(S("mla_hi"), n)
                    V_.tensor_tensor(lo_[:, t, :], full[:, t, :], hi[:, t, :].bitcast(F32), ALU.subtract).then_inc(S("mla_lo"), 1)
            split_even(ffn_end + HALVES)

            def rotate_q(hd):
                q = qr[:, (hd // 2) % 2]
                dve.wait_ge(S("qr_swapped"), hd // 2 + 1)
                link(V_.tensor_tensor(q[:, 1, :], q[:, 0, :], cosb, ALU.mult))
                link(V_.tensor_tensor(q[:, 0, :], bank[2][:, 0:T2], sinb, ALU.mult))
                V_.tensor_tensor(q[:, 2, :], q[:, 1, :], q[:, 0, :], ALU.add).then_inc(S("qr_ready"), 1)

            def gated(hd):
                g = hin[:, hd % 2, 2, :]
                dve.wait_ge(S("proj_taken"), gate_taken[hd])
                V_.scalar_tensor_tensor(out=g, in0=atanh, scalar=1.0, in1=g, op0=ALU.add, op1=ALU.mult).then_inc(S("at_gated"), 1)

            def output(hd):
                dve.wait_ge(S("at_o"), hd + 1)
                dve.wait_ge(S("at_gated"), hd + 1)
                V_.scalar_tensor_tensor(out=om[:, hd, :], in0=bank[7][:, 0:T2], scalar=0.5, in1=hin[:, hd % 2, 2, :],
                                        op0=ALU.mult, op1=ALU.mult).then_inc(S("at_o_taken"), 1)

            first_head = n1 + 7 + 12
            gate_taken = [first_head + 3 * (hd + 1) + hd // 2 + 1 for hd in range(AH)]
            split_even(head_units(int(starts[first_head + 2])))
            rotate_q(0)
            for hd in range(AH):
                pb = hd % 2
                split_even(head_units(int(starts[gate_taken[hd]])))
                dve.wait_ge(S("at_scores"), hd + 1)
                if hd >= 2:
                    dve.wait_ge(S("at_pT"), hd - 1)
                V_.tensor_tensor(pr[:, pb, :], bank[3][:, 0:384], C("amask", 384), ALU.add)
                V_.tensor_tensor(pr2[0:META, pb, :], bank[4][0:META, 0:T2], C("amask2", T2, META), ALU.add).then_inc(S("at_masked"), 1)
                dve.wait_ge(S("at_masked"), hd + 1)
                V_.reduce_max(nm[:, pb, 0:1], pr[:, pb, 0:128], axis=AX_X)
                V_.reduce_max(nm[:, pb, 1:2], pr[:, pb, 128:384], axis=AX_X)
                link(V_.reduce_max(nm[0:META, pb, 2:3], pr2[0:META, pb, :], axis=AX_X))
                V_.tensor_scalar(nm[:, pb, 3:5], nm[:, pb, 0:2], -SCALE_A, None, ALU.mult)
                V_.tensor_scalar(nm[0:META, pb, 5:6], nm[0:META, pb, 2:3], -SCALE_A, None, ALU.mult).then_inc(S("at_max"), 1)
                if hd + 1 < AH and (hd + 1) % 2 == 0:
                    rotate_q(hd + 1)
                if hd >= 1:
                    output(hd - 1)
                gated(hd)
                dve.wait_ge(S("at_exp"), hd + 1)
                V_.reciprocal(nm[:, pb, 9:11], nm[:, pb, 6:8])
                link(V_.reciprocal(nm[0:META, pb, 11:12], nm[0:META, pb, 8:9]))
                V_.tensor_scalar(pr[:, pb, 0:128], pr[:, pb, 0:128], nm[:, pb, 9:10], None, ALU.mult)
                V_.tensor_scalar(pr[:, pb, 128:384], pr[:, pb, 128:384], nm[:, pb, 10:11], None, ALU.mult)
                V_.tensor_scalar(pr2[0:META, pb, :], pr2[0:META, pb, :], nm[0:META, pb, 11:12], None, ALU.mult).then_inc(S("at_probs"), 1)
            output(AH - 1)
            post(1)

        @block.gpsimd
        def _(pool):
            for i in range(1, first_units, 2):
                split_lo(pool, nc.gpsimd, i, "w_lo_odd")
            for g in range(4):
                pool.wait_ge(S("dn_A"), g + 1)
                for l in range(LEVELS):
                    if l >= 2:
                        pool.wait_ge(S("dn_y"), 6 * g + l - 2) if l >= 3 else pool.wait_ge(S("dn_step"), 7 * g + 1)
                    nc.gpsimd.tensor_tensor(AMd[:, l % 2], ATd, over(levels[:, l, :], 4), ALU.mult).then_inc(S("dn_mask"), 1)
                    if l >= 1:
                        if l >= 3:
                            pool.wait_ge(S("dn_delta"), 6 * g + l - 2)
                        nc.gpsimd.memset(parts(Yd[l % 2], l, 1), 0.0).then_inc(S("dn_y_zero"), 1)
            for m in range(-1, FT + 1):
                if m < FT:
                    split_lo(pool, nc.gpsimd, first_units + 2 * m + 3, "w_lo_odd")
                if m >= 1:
                    pool.wait_ge(S("ffn_prod"), m)
                    nc.gpsimd.tensor_copy(prod_hi[:, m - 1, :], prod[:, m - 1, :]).then_inc(S("prod_hi_ready"), 1)
                    pool.wait_ge(S("prod_hi_ready"), m)
                    nc.gpsimd.tensor_tensor(prod_lo[:, m - 1, :], prod[:, m - 1, :], prod_hi[:, m - 1, :].bitcast(F32), ALU.subtract)\
                        .then_inc(S("prod_split"), 1)
            for i in range(first_units + 2 * FT + 3, ffn_end, 2):
                split_lo(pool, nc.gpsimd, i, "w_lo_odd")
            pool.wait_ge(S("dx_ready"), 1)
            for row, dst in ((2, xs[:, 2]), (3, xs[:, 3])):
                for t in range(DT):
                    ins = nc.gpsimd.tensor_scalar(dst[:, t, :], dx[:, t, :], V("rwkv_mu_2", row * 8 + t), None, ALU.mult)
                ins.then_inc(S("scaled_pool"), 1)
                pool.wait_ge(S("scaled_pool"), row - 1)
                nc.gpsimd.tensor_tensor(dst, dst, u[:, :, :], ALU.add).then_inc(S("lerped_pool"), 1)
            pool.wait_ge(S("lerped_pool"), 2)
            for p in range(PAIRS):
                pool.wait_ge(S("rw_grams_taken"), 3 * p + 2)
                if p >= 1:
                    pool.wait_ge(S("rw_y"), 6 * p)
                for l in range(LEVELS):
                    if l == 2:
                        pool.wait_ge(S("rw_step"), 7 * p + 1)
                    if l >= 3:
                        pool.wait_ge(S("rw_y"), 6 * p + l - 2)
                    if l == 0:
                        nc.gpsimd.tensor_tensor(AMr[0], GG[:, p % 2, :, 0:P], over(levels[:, 0, :], 4), ALU.mult)
                        pool.wait_ge(S("rw_grams_taken"), 3 * p + 3)
                    if l < 4:
                        ins = nc.gpsimd.tensor_tensor(AM0[l % 2][0:META], G0[0:META, p % 2, :, 0:META],
                                                over(levels[0:META, l, 0:META], 2), ALU.mult)
                    if l >= 1:
                        ins = nc.gpsimd.tensor_tensor(AMr[l % 2], GG[:, p % 2, :, 0:P], over(levels[:, l, :], 4), ALU.mult)
                    ins.then_inc(S("rw_mask"), 1)
                    if l >= 1:
                        if l >= 3:
                            pool.wait_ge(S("rw_delta"), 6 * p + l - 2)
                        nc.gpsimd.memset(parts(Yr[l % 2], l, 1), 0.0).then_inc(S("rw_y_zero"), 1)
            for i in range(ffn_end + 1, len(unit_start), 2):
                split_lo(pool, nc.gpsimd, i, "w_lo_odd")


DN_SCALE = 128 ** -0.5


def gemm_sizes():
    n = [DT] * 8 + [0, 4 * DT] * 2 + [DT] * 56 + [DT] * 24 + [DT] * (2 * FT) + [FT] * 8
    n += [DT]
    for p in range(PAIRS):
        n += [DT, 0, 0, DT, 0, DT, 0, DT]
    n += [IT] * 8 + [DT] * 7 + [0, 0, 8] * 4
    for hd in range(AH):
        n += ([4] if hd % 2 == 0 else []) + [4, 2, DT]
    return n + [IT] * 8


def kernel(**inputs):
    import concourse.bacc as _bacc
    from concourse.bass_utils import run_bass_kernel_spmd as _run

    a = {k: np.asarray(v) for k, v in inputs.items()}
    two = {k: (v[0] if v.ndim == 3 else v) for k, v in a.items()}
    stream = np.zeros((NCHUNKS, P, CB, P), np.float32)
    for b, (w, r0, pieces) in enumerate(weight_order()):
        at = 0
        for c0, n in pieces:
            stream[b // CB, :, b % CB, at:at + n] = two[w][r0:r0 + P, c0:c0 + n]
            at += n
    vecs = np.zeros((P, NVEC), np.float32)
    for name, n in VECTORS:
        if name == "a_log":
            vecs[:H1, VOFF[name]] = a["dn_a_log"].reshape(-1)
        elif name == "dt_bias":
            vecs[:H1, VOFF[name]] = a["dn_dt_bias"].reshape(-1)
        else:
            vecs[:, VOFF[name]:VOFF[name] + n] = a[name].reshape(n, P).T
    consts = np.concatenate([v.astype(np.float32) for v in CONST.values()], axis=1)
    arrays = {
        "xT": a["x"].reshape(T1, DT, P).transpose(2, 1, 0),
        "metaT": a["meta_tokens_2"].reshape(META, DT, P).transpose(2, 1, 0),
        "wstream": stream.reshape(NCHUNKS, P, CB * P),
        "vecs": vecs,
        "consts": consts,
        "decays": decay_table(),
        "wdbda": two["w_in"][:, O_DB:O_DB + 16].reshape(DT, P, 16).transpose(1, 0, 2).reshape(P, DT * 16),
        "wlora": np.concatenate([a["rwkv_w2_2"][0], a["rwkv_a2_2"][0]], axis=0),
    }
    arrays = {k: np.ascontiguousarray(v) for k, v in arrays.items()}
    nc = _bacc.Bacc("TRN2", target_bir_lowering=False, num_devices=1, dynamic_dma_scratch_size=1024)
    args = [nc.dram_tensor(k, v.shape, F32, kind="ExternalInput").ap() for k, v in arrays.items()]
    out = nc.dram_tensor("outT", (P, DT, T1), F32, kind="ExternalOutput").ap()
    build(nc, *args, out)
    r = _run(nc, [arrays], core_ids=[0])
    got = np.asarray(r.results[0]["outT"])
    return np.ascontiguousarray(got.transpose(2, 1, 0).reshape(1, T1, D))
```
